# Optimizing a Trainium2 kernel written in Bass

```python
import jax, jax.numpy as jnp
from jax import lax
import numpy as np

D_MODEL = 1024
BATCH = 1
SEQ = 2048
DEPTH = 1

HEAD_DIM = 64
SWA_Q_HEADS = 8
SWA_KV_HEADS = 2
SWA_GROUP = SWA_Q_HEADS // SWA_KV_HEADS
SWA_WIDTH = SWA_Q_HEADS * HEAD_DIM
SWA_KV_WIDTH = SWA_KV_HEADS * HEAD_DIM
FOX_HEADS = 8
FOX_WIDTH = FOX_HEADS * HEAD_DIM
WINDOW = 128
BLOCK = 128
ROPE_THETA = 10000.0
NORM_EPS = 1e-6
FORGET_BIAS_INIT = 2.0

IN_SPLITS = (SWA_WIDTH, SWA_KV_WIDTH, SWA_KV_WIDTH, SWA_WIDTH,
             FOX_WIDTH, FOX_WIDTH, FOX_WIDTH, FOX_HEADS, FOX_WIDTH,
             D_MODEL, D_MODEL)
IN_WIDTH = sum(IN_SPLITS)

kernel_name = "hybrid_swa_sink_fox_gated_block"

def rms_norm(x, g):
    xf = x.astype(jnp.float32)
    y = xf * lax.rsqrt(jnp.mean(xf * xf, axis=-1, keepdims=True) + NORM_EPS)
    return (y * g.astype(jnp.float32)).astype(x.dtype)

def rope_tables(positions):
    inv_freq = ROPE_THETA ** (-jnp.arange(0, HEAD_DIM, 2, dtype=jnp.float32) / HEAD_DIM)
    ang = positions.astype(jnp.float32)[..., None] * inv_freq
    ang = jnp.concatenate([ang, ang], axis=-1)[:, :, None, :]
    return jnp.cos(ang), jnp.sin(ang)

def apply_rope(t, cos, sin):
    half = HEAD_DIM // 2
    tf = t.astype(jnp.float32)
    rot = jnp.concatenate([-tf[..., half:], tf[..., :half]], axis=-1)
    return (tf * cos + rot * sin).astype(t.dtype)

def split_cols(p, sizes):
    offs = np.cumsum(sizes)[:-1].tolist()
    return jnp.split(p, offs, axis=-1)

def sliding_window_gqa_sinks(q, k, v, sinks):
    b, s = q.shape[:2]
    nb = s // BLOCK
    q = q.reshape(b, nb, BLOCK, SWA_KV_HEADS, SWA_GROUP, HEAD_DIM)
    k = k.reshape(b, nb, BLOCK, SWA_KV_HEADS, HEAD_DIM)
    v = v.reshape(b, nb, BLOCK, SWA_KV_HEADS, HEAD_DIM)
    pad_k = jnp.zeros_like(k[:, :1])
    pad_v = jnp.zeros_like(v[:, :1])
    k_band = jnp.concatenate([jnp.concatenate([pad_k, k[:, :-1]], axis=1), k], axis=2)
    v_band = jnp.concatenate([jnp.concatenate([pad_v, v[:, :-1]], axis=1), v], axis=2)
    logits = jnp.einsum('bnqkgd,bnskd->bnkgqs', q, k_band).astype(jnp.float32) * (HEAD_DIM ** -0.5)
    blk = jnp.arange(nb)[:, None, None]
    qpos = blk * BLOCK + jnp.arange(BLOCK)[None, :, None]
    kpos = (blk - 1) * BLOCK + jnp.arange(2 * BLOCK)[None, None, :]
    rel = qpos - kpos
    mask = (rel >= 0) & (rel < WINDOW) & (kpos >= 0)
    logits = jnp.where(mask[None, :, None, None], logits, -jnp.inf)
    sink = sinks.astype(jnp.float32).reshape(SWA_KV_HEADS, SWA_GROUP)[None, None, :, :, None, None]
    m = jnp.maximum(jnp.max(logits, axis=-1, keepdims=True), sink)
    p = jnp.exp(logits - m)
    denom = jnp.sum(p, axis=-1, keepdims=True) + jnp.exp(sink - m)
    out = jnp.einsum('bnkgqs,bnskd->bnqkgd', (p / denom).astype(v.dtype), v_band)
    return out.reshape(b, s, SWA_WIDTH)

def forgetting_attention(q, k, v, cum):
    b, s = q.shape[:2]
    nb = s // BLOCK
    q_blocks = q.reshape(b, nb, BLOCK, FOX_HEADS, HEAD_DIM).transpose(1, 0, 2, 3, 4)
    cq_blocks = cum.reshape(b, nb, BLOCK, FOX_HEADS).transpose(1, 0, 3, 2)
    ck = cum.transpose(0, 2, 1)[:, :, None, :]
    kpos = jnp.arange(s)
    scale = HEAD_DIM ** -0.5

    def one_block(args):
        qb, cqb, n = args
        logits = jnp.einsum('bqhd,bshd->bhqs', qb, k).astype(jnp.float32) * scale
        logits = logits + cqb[..., None] - ck
        qpos = n * BLOCK + jnp.arange(BLOCK)
        mask = kpos[None, :] <= qpos[:, None]
        logits = jnp.where(mask, logits, -jnp.inf)
        p = jax.nn.softmax(logits, axis=-1)
        return jnp.einsum('bhqs,bshd->bqhd', p.astype(v.dtype), v)

    out = lax.map(one_block, (q_blocks, cq_blocks, jnp.arange(nb)))
    return out.transpose(1, 0, 2, 3, 4).reshape(b, s, FOX_WIDTH)

def setup_inputs(seed: int = 0) -> dict:
    key = jax.random.key(seed)
    ks = jax.random.split(key, 14)
    f32 = jnp.float32
    x = jax.random.normal(ks[0], (BATCH, SEQ, D_MODEL), f32)
    c = jax.random.normal(ks[1], (BATCH, D_MODEL), f32)
    positions = jnp.broadcast_to(jnp.arange(SEQ, dtype=jnp.int32), (BATCH, SEQ))
    w_ada = jax.random.normal(ks[2], (DEPTH, D_MODEL, 3 * D_MODEL), f32) * (0.5 * D_MODEL ** -0.5)
    b_ada = jax.random.normal(ks[3], (DEPTH, 3 * D_MODEL), f32) * 0.02
    g_norm = 1.0 + 0.05 * jax.random.normal(ks[4], (DEPTH, D_MODEL), f32)
    w_in = jax.random.normal(ks[5], (DEPTH, D_MODEL, IN_WIDTH), f32) * D_MODEL ** -0.5
    b_f = FORGET_BIAS_INIT + 0.1 * jax.random.normal(ks[6], (DEPTH, FOX_HEADS), f32)
    sinks = jax.random.normal(ks[7], (DEPTH, SWA_Q_HEADS), f32) * 0.5
    w_o_swa = jax.random.normal(ks[8], (DEPTH, SWA_WIDTH, D_MODEL), f32) * SWA_WIDTH ** -0.5
    w_o_fox = jax.random.normal(ks[9], (DEPTH, FOX_WIDTH, D_MODEL), f32) * FOX_WIDTH ** -0.5
    w_out = jax.random.normal(ks[10], (DEPTH, D_MODEL, D_MODEL), f32) * D_MODEL ** -0.5
    g_final = 1.0 + 0.05 * jax.random.normal(ks[11], (D_MODEL,), f32)
    return {"x": x, "c": c, "positions": positions, "w_ada": w_ada, "b_ada": b_ada,
            "g_norm": g_norm, "w_in": w_in, "b_f": b_f, "sinks": sinks,
            "w_o_swa": w_o_swa, "w_o_fox": w_o_fox, "w_out": w_out, "g_final": g_final}

def reference(x, c, positions, w_ada, b_ada, g_norm, w_in, b_f, sinks, w_o_swa, w_o_fox, w_out, g_final):
    b, s, _ = x.shape
    cos, sin = rope_tables(positions)
    for l in range(DEPTH):
        ada = c @ w_ada[l] + b_ada[l]
        shift, scale, gate = jnp.split(ada, 3, axis=-1)
        h = rms_norm(x, g_norm[l]) * (1.0 + scale[:, None, :]) + shift[:, None, :]
        proj = h @ w_in[l]
        qa, ka, va, za, qb, kb, vb, fb, zb, ga, gb = split_cols(proj, IN_SPLITS)
        qa = apply_rope(qa.reshape(b, s, SWA_Q_HEADS, HEAD_DIM), cos, sin)
        ka = apply_rope(ka.reshape(b, s, SWA_KV_HEADS, HEAD_DIM), cos, sin)
        va = va.reshape(b, s, SWA_KV_HEADS, HEAD_DIM)
        att_a = sliding_window_gqa_sinks(qa, ka, va, sinks[l])
        y_a = (att_a * jax.nn.silu(za)) @ w_o_swa[l]
        log_f = jax.nn.log_sigmoid(fb.astype(jnp.float32) + b_f[l].astype(jnp.float32))
        cum = jnp.cumsum(log_f, axis=1)
        att_b = forgetting_attention(qb.reshape(b, s, FOX_HEADS, HEAD_DIM),
                                     kb.reshape(b, s, FOX_HEADS, HEAD_DIM),
                                     vb.reshape(b, s, FOX_HEADS, HEAD_DIM), cum)
        y_b = (att_b * jax.nn.silu(zb)) @ w_o_fox[l]
        merged = jax.nn.sigmoid(ga) * y_a + jax.nn.sigmoid(gb) * y_b
        x = x + gate[:, None, :] * (merged @ w_out[l])
    return rms_norm(x, g_final)


_drawn_inputs = setup_inputs


def setup_inputs(seed=0):
    import zlib

    import numpy as np

    out = dict(_drawn_inputs(seed))
    spreads = {}
    factors = {'b_ada': 4.358, 'g_norm': 3.394, 'b_f': 38.79, 'sinks': 200.0}
    for name, (base, spread) in spreads.items():
        noise = np.random.default_rng([zlib.crc32(name.encode()), seed]).standard_normal(out[name].shape)
        drawn = base * np.exp(spread * noise) if base else spread * noise
        out[name] = __import__('jax').numpy.asarray(drawn.astype(out[name].dtype))
    for name, factor in factors.items():
        out[name] = (out[name] * factor).astype(out[name].dtype)
    return out
```

```python
from contextlib import ExitStack

import concourse.bass as bass
from concourse import mybir

ALU = mybir.AluOpType
ACT = mybir.ActivationFunctionType
AX = mybir.AxisListType
F32 = mybir.dt.float32
F32R = mybir.dt.float32r
BF16 = mybir.dt.bfloat16
I32 = mybir.dt.int32

P = 128
T = 2048
D = 1024
KT = D // P
HD = 64
NH = 8
W = NH * HD
KV = 2
GROUP = NH // KV
NB = T // P
CH = 512
NC = T // CH
SCALE = HD ** -0.5
EPS = 1e-6
MASKED = -1e30

QA0 = 0
KA0 = QA0 + W
VA0 = KA0 + KV * HD
ZA0 = VA0 + KV * HD
QB0 = ZA0 + W
KB0 = QB0 + W
VB0 = KB0 + W
FB0 = VB0 + W
ZB0 = FB0 + NH
GA0 = ZB0 + W

VW = W + KV * HD
VF = VW + NH
VN = VF // 2

TWO_PI = 6.283185307179586
COARSE = 4096.0


def parts_of(value, bits, count):
    import math
    out = []
    for _ in range(count):
        e = math.floor(math.log2(value)) + 1 - bits if value > 0 else 0
        part = math.floor(value / 2.0 ** e) * 2.0 ** e
        out.append(part)
        value -= part
    return out


def f32(ap):
    return ap.bitcast(F32)


class Memory:

    def __init__(self, nc, ctx, stage, kept=None):
        self.nc, self.ctx, self.stage = nc, ctx, stage
        self.kept = kept

    def sb(self, name, shape, dt=F32):
        return self.ctx.enter_context(self.nc.sbuf_tensor(f"{self.stage}_{name}", shape, dt))

    def ps(self, name, shape, dt=F32):
        return self.ctx.enter_context(self.nc.psum_tensor(f"{self.stage}_{name}", shape, dt))

    def sem(self, name):
        if self.kept is not None:
            if name not in self.kept:
                self.kept[name] = self.nc.alloc_semaphore(name)
            return self.kept[name]
        return self.ctx.enter_context(self.nc.semaphore(f"{self.stage}_{name}"))


def chain(eng, sem):
    count = [0]

    def step(instruction):
        count[0] += 1
        instruction.then_inc(sem, 1)
        eng.wait_ge(sem, count[0])
    return step


def prepare_and_values(nc, I, S, hT_hi, hT_lo):
    with ExitStack() as ctx:
        m = Memory(nc, ctx, "prep")
        cond = m.sb("cond", [P, KT])
        bias_cols = m.sb("bias_cols", [P, 2 * KT])
        g_col = m.sb("g_col", [P, KT])
        gain = m.sb("gain", [P, KT])
        shift = m.sb("shift", [P, KT])
        ada_cols = m.sb("ada_cols", [P, 2 * KT])
        ident = m.sb("ident", [P, P])
        rstd = m.sb("rstd", [P, NB])
        vv = m.sb("vv", [P, NB])
        tmp = m.sb("tmp", [P, NB])
        forget = m.sb("forget", [P, NB, NH])

        with ExitStack() as early:
            a = Memory(nc, early, "ada")
            x_sb = a.sb("x", [P, NB, D])
            with ExitStack() as inner:
                b = Memory(nc, inner, "cond")
                WB = 3
                w_ada = b.sb("w_ada", [P, WB, D])
                square = b.ps("square", [P, D])
                sums = b.sb("sums", [P, NB])
                ada_ps = b.ps("ada_ps", [P, 2 * KT])
                small = b.sem("small_loaded")
                w_loaded = [b.sem(f"w_ada_loaded{i}") for i in range(WB)]
                x_loaded = [b.sem(f"x_loaded{i}") for i in range(4)]
                w_used = b.sem("w_ada_used")
                summed = b.sem("squares_summed")
                dve = b.sem("dve_steps")
                rooted = b.sem("rooted")
                pool = b.sem("identity_steps")
                inverted = b.sem("inverted")
                with nc.Block() as block:
                    @block.sync
                    def _(sp):
                        sp.dma_start(cond[:], I["c"].rearrange("o (k p) -> p (o k)", p=P), allow_slow_non_contiguous=True).then_inc(small, 16)
                        sp.dma_start(bias_cols[:], I["b_ada"][0, 0:2 * D].rearrange("(k p) -> p k", p=P), allow_slow_non_contiguous=True).then_inc(small, 16)
                        sp.dma_start(g_col[:], I["g_norm"][0, :].rearrange("(k p) -> p k", p=P), allow_slow_non_contiguous=True).then_inc(small, 16)
                        for u in range(2 * KT):
                            k, half = divmod(u, 2)
                            if u >= WB:
                                sp.wait_ge(w_used, u - WB + 1)
                            sp.dma_start(w_ada[:, u % WB, :], I["w_ada"][0, k * P:(k + 1) * P, half * D:(half + 1) * D]).then_inc(w_loaded[u % WB], 16)

                    @block.gpsimd
                    def _(gp):
                        gp.memset(ident[:], 0.0).then_inc(pool, 1)
                        gp.wait_ge(pool, 1)
                        gp.affine_select(out=ident[:], in_=ident[:], compare_op=ALU.not_equal, fill=1.0,
                                         base=0, pattern=[[-1, P]], channel_multiplier=1).then_inc(pool, 1)

                    @block.tensor
                    def _(pe):
                        pe.wait_ge(small, 48)
                        for u in range(2 * KT):
                            k, half = divmod(u, 2)
                            pe.wait_ge(w_loaded[u % WB], 16 * (u // WB + 1))
                            for j in range(KT):
                                col = half * KT + j
                                last = nc.tensor.matmul(ada_ps[:, col:col + 1], w_ada[:, u % WB, j * P:(j + 1) * P], cond[:, k:k + 1],
                                                        start=(u == 0 and j == 0), stop=(k == KT - 1), skip_group_check=True)
                            last.then_inc(w_used, 1)

                    @block.scalar
                    def _(act):
                        for q in range(4):
                            act.dma_start(x_sb[:, 4 * q:4 * q + 4, :],
                                          I["x"][0, q * CH:(q + 1) * CH, :].rearrange("(n p) d -> p n d", p=P)).then_inc(x_loaded[q], 16)
                        for n in range(NB):
                            act.wait_ge(x_loaded[n // 4], 16)
                            if n:
                                act.wait_ge(summed, n)
                            nc.scalar.activation(square[:], x_sb[:, n, :], ACT.Square, accum_out=sums[:, n:n + 1]).then_inc(summed, 1)
                        act.wait_ge(inverted, 1)
                        nc.scalar.activation(rstd[:], tmp[:], ACT.Sqrt).then_inc(rooted, 1)

                    @block.vector
                    def _(dv):
                        step = chain(dv, dve)
                        dv.wait_ge(summed, NB)
                        step(nc.vector.tensor_scalar(vv[:], sums[:], 1.0 / D, EPS, ALU.mult, ALU.add))
                        nc.vector.reciprocal(tmp[:], vv[:]).then_inc(inverted, 1)
                        dv.wait_ge(rooted, 1)
                        step(nc.vector.tensor_tensor(tmp[:], rstd[:], rstd[:], ALU.mult))
                        step(nc.vector.tensor_tensor(tmp[:], tmp[:], vv[:], ALU.mult))
                        step(nc.vector.tensor_scalar(tmp[:], tmp[:], -0.5, 1.5, ALU.mult, ALU.add))
                        step(nc.vector.tensor_tensor(rstd[:], rstd[:], tmp[:], ALU.mult))
                        dv.wait_ge(w_used, 2 * KT)
                        dv.wait_ge(small, 48)
                        step(nc.vector.tensor_tensor(ada_cols[:], ada_ps[:], bias_cols[:], ALU.add))
                        step(nc.vector.tensor_copy(shift[:], ada_cols[:, 0:KT]))
                        step(nc.vector.scalar_tensor_tensor(gain[:], ada_cols[:, KT:2 * KT], 1.0, g_col[:], ALU.add, ALU.mult))

            with ExitStack() as inner:
                b = Memory(nc, inner, "norm")
                xn = b.sb("xn", [P, D])
                h_raw = b.sb("h_raw", [P, KT, P])
                turned = b.ps("turned", [P, 2, 2, 4, P])
                xn_ready = b.sem("xn_ready")
                half_turned = b.sem("half_turned")
                raw_half = b.sem("raw_half_ready")
                hi_ready = b.sem("hi_ready")
                lo_ready = b.sem("lo_ready")
                with nc.Block() as block:
                    @block.vector
                    def _(dv):
                        with dv.Fori(0, NB) as n:
                            dv.wait_ge(half_turned, n * 2)
                            nc.vector.tensor_scalar(xn[:], x_sb[:, bass.ds(n, 1), :].rearrange("p a d -> p (a d)"),
                                                    rstd[:, bass.ds(n, 1)], None, ALU.mult).then_inc(xn_ready, 1)
                            dv.wait_ge(lo_ready, n)
                            for half in range(2):
                                dv.wait_ge(half_turned, n * 2 + half + 1)
                                for j in range(4):
                                    k = 4 * half + j
                                    last = nc.vector.tensor_scalar(h_raw[:, k, :], turned[:, half, 0, j, :], gain[:, k:k + 1], shift[:, k:k + 1],
                                                                   ALU.mult, ALU.add)
                                last.then_inc(raw_half, 1)

                    @block.tensor
                    def _(pe):
                        with pe.Fori(0, NB) as n:
                            pe.wait_ge(xn_ready, n + 1)
                            for half in range(2):
                                pe.wait_ge(raw_half, n * 2)
                                for j in range(4):
                                    k = 4 * half + j
                                    last = nc.tensor.transpose(turned[:, half, 0, j, :], xn[:, k * P:(k + 1) * P], ident[:])
                                last.then_inc(half_turned, 1)

                    @block.scalar
                    def _(act):
                        with act.Fori(0, NB) as n:
                            act.wait_ge(raw_half, n * 2 + 2)
                            nc.scalar.activation(hT_hi[:, :, bass.ds(n * P, P)], h_raw[:], ACT.Copy).then_inc(hi_ready, 1)

                    @block.gpsimd
                    def _(gp):
                        with gp.Fori(0, NB) as n:
                            gp.wait_ge(hi_ready, n + 1)
                            gp.tensor_tensor(hT_lo[:, :, bass.ds(n * P, P)], h_raw[:], f32(hT_hi[:, :, bass.ds(n * P, P)]),
                                             ALU.subtract).then_inc(lo_ready, 1)

        with ExitStack() as inner:
            b = Memory(nc, inner, "val")
            w_raw = b.sb("w_raw", [P, 2, VF])
            w_hi = b.sb("w_hi", [P, KT, VF], F32R)
            w_lo = b.sb("w_lo", [P, KT, VF], F32R)
            v_hi = b.sb("v_hi", [P, 2, VF], F32R)
            v_lo = b.sb("v_lo", [P, 2, VF], F32R)
            bf_row = b.sb("bf_row", [P, NH])
            upper = b.sb("upper", [P, P])
            ones = b.sb("ones", [P, P])
            e_neg = b.sb("e_neg", [P, NB, NH])
            one_e = b.sb("one_e", [P, NB, NH])
            ln_e = b.sb("ln_e", [P, NB, NH])
            flat = b.sb("flat", [P, NB, NH])
            cum = b.sb("cum", [P, NH, NB])
            c_hi = b.sb("c_hi", [P, P], F32R)
            c_lo = b.sb("c_lo", [P, P], F32R)
            zeros = b.sb("zeros", [P, P])
            out_ps = b.ps("out_ps", [P, 4, CH])
            sum_ps = b.ps("sum_ps", [P, NB, NH])
            tot_ps = b.ps("tot_ps", [P, 512])
            row_ps = b.ps("row_ps", [P, 512])
            loaded = [b.sem(f"w_loaded{i}") for i in range(2)]
            split_hi = b.sem("w_hi_ready")
            split = b.sem("w_split")
            small = b.sem("small_loaded")
            done = b.sem("products_done")
            hi_ready = b.sem("v_hi_ready")
            lo_ready = b.sem("v_lo_ready")
            stored = [b.sem(f"v_stored{i}") for i in range(2)]
            consts = b.sem("constants")
            dve = b.sem("dve_steps")
            logit_ready = b.sem("logit_ready")
            e_ready = b.sem("e_ready")
            one_ready = b.sem("one_ready")
            ln_ready = b.sem("ln_ready")
            logf_ready = b.sem("logf_ready")
            sums_ready = b.sem("sums_ready")
            cum_ready = b.sem("cum_ready")
            rows_ready = b.sem("rows_ready")
            rows_split = b.sem("rows_split")
            rows_stored = b.sem("rows_stored")
            with nc.Block() as block:
                @block.sync
                def _(sp):
                    sp.dma_start(bf_row[:], I["b_f"].to_broadcast([P, NH])).then_inc(small, 16)
                    for k in range(KT):
                        if k >= 2:
                            sp.wait_ge(split, k - 1)
                        rows = I["w_in"][0, k * P:(k + 1) * P, :]
                        sp.dma_start(w_raw[:, k % 2, 0:W], rows[:, VB0:VB0 + W]).then_inc(loaded[k % 2], 16)
                        sp.dma_start(w_raw[:, k % 2, W:VW], rows[:, VA0:VA0 + KV * HD]).then_inc(loaded[k % 2], 16)
                        sp.dma_start(w_raw[:, k % 2, VW:VF], rows[:, FB0:FB0 + NH]).then_inc(loaded[k % 2], 16)
                    for n in range(NB):
                        sp.wait_ge(lo_ready, 2 * n + 2)
                        for part, src in enumerate((v_hi, v_lo)):
                            sp.dma_start(S["v"][part, n * P:(n + 1) * P, :], f32(src[:, n % 2, 0:VW])).then_inc(stored[n % 2], 16)
                    sp.wait_ge(consts, 4)
                    for part in range(2):
                        sp.dma_start(S["negc"][part, 0:NH, :].rearrange("h (n p) -> (h n) p", p=P), zeros[:]).then_inc(rows_stored, 16)
                    sp.wait_ge(rows_split, 2)
                    for part, src in enumerate((c_hi, c_lo)):
                        sp.dma_start(S["negc"][part, NH:2 * NH, :].rearrange("h (n p) -> (h n) p", p=P), f32(src[:])).then_inc(rows_stored, 16)
                    sp.wait_ge(stored[0], 16 * NB)
                    sp.wait_ge(stored[1], 16 * NB)
                    sp.wait_ge(rows_stored, 64)

                @block.gpsimd
                def _(gp):
                    gp.memset(upper[:], 1.0).then_inc(consts, 1)
                    gp.memset(ones[:], 1.0).then_inc(consts, 1)
                    gp.memset(zeros[:], 0.0).then_inc(consts, 1)
                    gp.wait_ge(consts, 3)
                    gp.affine_select(out=upper[:], in_=upper[:], compare_op=ALU.is_ge, fill=0.0,
                                     base=0, pattern=[[1, P]], channel_multiplier=-1).then_inc(consts, 1)
                    for k in range(KT):
                        gp.wait_ge(loaded[k % 2], 48 * (k // 2 + 1))
                        gp.tensor_copy(w_hi[:, k, :], w_raw[:, k % 2, :]).then_inc(split_hi, 1)
                        gp.wait_ge(split_hi, k + 1)
                        gp.tensor_tensor(w_lo[:, k, :], w_raw[:, k % 2, :], f32(w_hi[:, k, :]), ALU.subtract).then_inc(split, 1)

                @block.tensor
                def _(pe):
                    for n in range(NB):
                        tok = slice(n * P, (n + 1) * P)
                        for half in range(2):
                            unit = 2 * n + half
                            cols = slice(half * VN, (half + 1) * VN)
                            out = out_ps[:, unit % 4, 0:VN]
                            if unit >= 4:
                                pe.wait_ge(lo_ready, unit - 3)
                            for k in range(KT):
                                if unit == 0:
                                    pe.wait_ge(split, k + 1)
                                nc.tensor.matmul(out, hT_hi[:, k, tok], w_hi[:, k, cols], start=(k == 0), stop=False)
                                nc.tensor.matmul(out, hT_hi[:, k, tok], w_lo[:, k, cols], start=False, stop=False)
                                last = nc.tensor.matmul(out, hT_lo[:, k, tok], w_hi[:, k, cols], start=False, stop=(k == KT - 1))
                            last.then_inc(done, 1)
                    pe.wait_ge(logf_ready, 1)
                    pe.wait_ge(consts, 4)
                    nc.tensor.matmul(sum_ps[:], upper[:], flat[:], start=True, stop=True)
                    nc.tensor.matmul(tot_ps[:, 0:NB * NH], ones[:], flat[:].rearrange("p n h -> p (n h)"), start=True, stop=True).then_inc(sums_ready, 1)
                    pe.wait_ge(cum_ready, 1)
                    nc.tensor.transpose(row_ps[:, 0:P], cum[:].rearrange("p h n -> p (h n)"), ident[:]).then_inc(rows_ready, 1)

                @block.scalar
                def _(act):
                    for n in range(NB):
                        if n >= 2:
                            act.wait_ge(stored[n % 2], 32 * (n // 2))
                        for half in range(2):
                            unit = 2 * n + half
                            act.wait_ge(done, unit + 1)
                            nc.scalar.activation(v_hi[:, n % 2, half * VN:(half + 1) * VN], out_ps[:, unit % 4, 0:VN], ACT.Copy).then_inc(hi_ready, 1)
                    act.wait_ge(logit_ready, 1)
                    nc.scalar.activation(e_neg[:], flat[:], ACT.Exp, scale=-1.0).then_inc(e_ready, 1)
                    act.wait_ge(one_ready, 1)
                    nc.scalar.activation(ln_e[:], one_e[:], ACT.Ln).then_inc(ln_ready, 1)
                    act.wait_ge(rows_ready, 1)
                    nc.scalar.activation(c_hi[:], row_ps[:, 0:P], ACT.Copy, scale=-1.0).then_inc(rows_split, 1)

                @block.vector
                def _(dv):
                    step = chain(dv, dve)
                    for n in range(NB):
                        if n >= 2:
                            dv.wait_ge(stored[n % 2], 32 * (n // 2))
                        for half in range(2):
                            unit = 2 * n + half
                            dv.wait_ge(hi_ready, unit + 1)
                            cols = slice(half * VN, (half + 1) * VN)
                            if half:
                                step(nc.vector.tensor_copy(forget[:, n, :], out_ps[:, unit % 4, VN - NH:VN]))
                            nc.vector.tensor_tensor(v_lo[:, n % 2, cols], out_ps[:, unit % 4, 0:VN], f32(v_hi[:, n % 2, cols]),
                                                    ALU.subtract).then_inc(lo_ready, 1)
                    dv.wait_ge(small, 16)
                    step(nc.vector.tensor_tensor(forget[:], forget[:], bf_row[:].unsqueeze(1).to_broadcast([P, NB, NH]), ALU.add))
                    step(nc.vector.tensor_scalar(flat[:], forget[:], -1.0, None, ALU.mult))
                    nc.vector.tensor_tensor(flat[:], flat[:], forget[:], ALU.max).then_inc(logit_ready, 1)
                    dv.wait_ge(e_ready, 1)
                    nc.vector.tensor_scalar(one_e[:], e_neg[:], 1.0, None, ALU.add).then_inc(one_ready, 1)
                    dv.wait_ge(ln_ready, 1)
                    step(nc.vector.tensor_scalar(one_e[:], one_e[:], -1.0, None, ALU.add))
                    step(nc.vector.tensor_scalar(flat[:], one_e[:], 0.0, None, ALU.is_equal))
                    step(nc.vector.tensor_tensor(ln_e[:], ln_e[:], flat[:], ALU.add))
                    step(nc.vector.tensor_tensor(one_e[:], one_e[:], flat[:], ALU.add))
                    step(nc.vector.reciprocal(one_e[:], one_e[:]))
                    step(nc.vector.tensor_tensor(ln_e[:], ln_e[:], one_e[:], ALU.mult))
                    step(nc.vector.tensor_tensor(ln_e[:], ln_e[:], e_neg[:], ALU.mult))
                    nc.vector.scalar_tensor_tensor(flat[:], forget[:], 0.0, ln_e[:], ALU.min, ALU.subtract).then_inc(logf_ready, 1)
                    dv.wait_ge(sums_ready, 1)
                    step(nc.vector.memset(e_neg[:, 0, :], 0.0))
                    for n in range(1, NB):
                        step(nc.vector.tensor_tensor(e_neg[:, n, :], e_neg[:, n - 1, :], tot_ps[:, (n - 1) * NH:n * NH], ALU.add))
                    nc.vector.tensor_tensor(cum[:].rearrange("p h n -> p n h"), sum_ps[:], e_neg[:], ALU.add).then_inc(cum_ready, 1)
                    dv.wait_ge(rows_split, 1)
                    nc.vector.scalar_tensor_tensor(c_lo[:], row_ps[:, 0:P], -1.0, f32(c_hi[:]), ALU.mult, ALU.subtract).then_inc(rows_split, 1)


ROPE, RAW, SILU, SIGMOID = "rope", "raw", "silu", "sigmoid"


def project(nc, I, S, hT_hi, hT_lo):
    segments = [
        (ROPE, KA0, 1, 1.0, ("k", 0)),
        (ROPE, QA0, 4, SCALE, ("q", 0)),
        (RAW, QB0, 4, SCALE, ("q", NH)),
        (RAW, KB0, 4, 1.0, ("k", KV)),
        (SILU, ZA0, 4, 1.0, ("z", 0)),
        (SILU, ZB0, 4, 1.0, ("z", W)),
        (SIGMOID, GA0, 16, 1.0, ("g", 0)),
    ]

    def each_tile(eng, emit):
        first = 0
        for kind, col, tiles, factor, (name, row) in segments:
            if tiles == 1:
                emit(kind, 0, 0, col, factor, name, 0, row)
            else:
                with eng.Fori(0, tiles // 2) as i:
                    for k in range(2):
                        emit(kind, 2 * i + (first + k), (first + k) % 2, col + 2 * P * i + k * P, factor, name, 2 * i + k, row)
            first += tiles

    with ExitStack() as ctx:
        b = Memory(nc, ctx, "proj")
        cosT = b.sb("cos", [P, T])
        sinT = b.sb("sin", [P, T])

        with ExitStack() as inner:
            a = Memory(nc, inner, "tab")
            half_t = T // 2
            pos_i = a.sb("pos_i", [P, half_t], I32)
            turns_i = a.sb("turns_i", [P, half_t], I32)
            turns = a.sb("turns", [P, half_t])
            inv = a.sb("inv", [P, 1])
            loaded = a.sem("loaded")
            dve = a.sem("dve_steps")
            angle = a.sem("angle_ready")
            sined = a.sem("sines_done")
            coarse = parts_of(TWO_PI * COARSE, 7, 8)
            fine = parts_of(TWO_PI, 10, 5)
            with nc.Block() as block:
                @block.sync
                def _(sp):
                    sp.dma_start(inv[:], I["inv_freq"]).then_inc(loaded, 16)
                    for s in range(2):
                        if s:
                            sp.wait_ge(angle, 1)
                        sp.dma_start(pos_i[:], I["positions"][:, s * half_t:(s + 1) * half_t].to_broadcast([P, half_t])).then_inc(loaded, 16)

                @block.vector
                def _(dv):
                    step = chain(dv, dve)
                    for s in range(2):
                        ang = sinT[:, s * half_t:(s + 1) * half_t]
                        oth = cosT[:, s * half_t:(s + 1) * half_t]
                        dv.wait_ge(loaded, 32 + 16 * s)
                        step(nc.vector.tensor_copy(ang, pos_i[:]))
                        step(nc.vector.tensor_scalar(ang, ang, inv[:, 0:1], None, ALU.mult))
                        for period, pieces in ((TWO_PI * COARSE, coarse), (TWO_PI, fine)):
                            step(nc.vector.tensor_scalar(turns[:], ang, 1.0 / period, None, ALU.mult))
                            step(nc.vector.tensor_copy(turns_i[:], turns[:]))
                            step(nc.vector.tensor_copy(turns[:], turns_i[:]))
                            for piece in pieces:
                                step(nc.vector.scalar_tensor_tensor(ang, turns[:], -piece, ang, ALU.mult, ALU.add))
                        for op, bound, turn in ((ALU.is_gt, TWO_PI / 2, -TWO_PI), (ALU.is_lt, -TWO_PI / 2, TWO_PI)):
                            step(nc.vector.tensor_scalar(turns[:], ang, bound, turn, op, ALU.mult))
                            step(nc.vector.tensor_tensor(ang, ang, turns[:], ALU.add))
                        step(nc.vector.tensor_scalar(ang, ang, 3.1415925, -3.1415925, ALU.min, ALU.max))
                        step(nc.vector.tensor_scalar(oth, ang, -1.0, None, ALU.mult))
                        step(nc.vector.tensor_tensor(oth, oth, ang, ALU.max))
                        step(nc.vector.tensor_scalar(oth, oth, -1.0, TWO_PI / 4, ALU.mult, ALU.add))
                        nc.vector.tensor_scalar(ang[64:P, :], ang[64:P, :], -1.0, None, ALU.mult).then_inc(angle, 1)

                @block.scalar
                def _(act):
                    for s in range(2):
                        act.wait_ge(angle, s + 1)
                        for tab in (sinT, cosT):
                            part = tab[:, s * half_t:(s + 1) * half_t]
                            nc.scalar.activation(part, part, ACT.Sin).then_inc(sined, 1)

        w_raw = b.sb("w_raw", [P, 2, KT, P])
        w_hi = b.sb("w_hi", [P, 2, KT, P], F32R)
        w_lo = b.sb("w_lo", [P, 2, KT, P], F32R)
        o_hi = b.sb("o_hi", [P, 2, CH], F32R)
        o_lo = b.sb("o_lo", [P, 2, CH], F32R)
        o_act = b.sb("o_act", [P, 2, CH])
        direct = b.sb("direct", [P, CH])
        crossed = b.sb("crossed", [P, CH])
        out_ps = b.ps("out_ps", [P, 2, NC, CH])
        passed = b.sem("passed")
        w_loaded = [b.sem(f"w_loaded{i}") for i in range(2)]
        w_hi_ready = b.sem("w_hi_ready")
        w_ready = b.sem("w_ready")
        chunk_done = b.sem("chunk_done")
        bank_free = b.sem("bank_free")
        rotated = b.sem("rotated")
        hi_ready = b.sem("hi_ready")
        lo_ready = b.sem("lo_ready")
        act_ready = b.sem("act_ready")
        stored = [b.sem(f"stored{i}") for i in range(2)]

        ROPES = 5
        SPLITS = 13
        DMAS = {ROPE: 4, RAW: 2, SILU: 1, SIGMOID: 1}

        def stored_before(kind, n, c):
            since = {ROPE: 0, RAW: ROPES, SILU: SPLITS, SIGMOID: SPLITS}[kind]
            base = {ROPE: 0, RAW: 2 * 4 * ROPES}.get(kind, 2 * 4 * ROPES + 2 * 2 * (SPLITS - ROPES))
            return (n - since) * (2 * 16 * DMAS[kind]) + 16 * (base + DMAS[kind] * (c // 2))

        with nc.Block() as block:
            @block.sync
            def _(sp):
                def emit(kind, n, par, col, factor, name, tile, row):
                    if not (isinstance(n, int) and n == 0):
                        sp.wait_ge(w_ready, n - 1)
                    sp.dma_start(w_raw[:, par, :, :],
                                 I["w_in"][0, :, bass.ds(col, P)].rearrange("(k p) c -> p k c", p=P)).then_inc(w_loaded[par], 16)
                each_tile(sp, emit)

            @block.gpsimd
            def _(gp):
                def emit(kind, n, par, col, factor, name, tile, row):
                    gp.wait_ge(w_loaded[par], (n - par) * 8 + 16)
                    if not (isinstance(n, int) and n == 0):
                        gp.wait_ge(chunk_done, (n - 1) * NC)
                        gp.sem_inc(passed, 1)
                    if kind == ROPE:
                        src = w_raw[:, par, :, :].rearrange("p k (h s c) -> p s k h c", h=2, s=2)
                        hi = w_hi[:, par, :, :].rearrange("p k (s h c) -> p s k h c", h=2, s=2)
                        lo = w_lo[:, par, :, :].rearrange("p k (s h c) -> p s k h c", h=2, s=2)
                        trios = [(src[:, s], hi[:, s], lo[:, s]) for s in range(2)]
                    else:
                        trios = [(w_raw[:, par, :, :], w_hi[:, par, :, :], w_lo[:, par, :, :])]
                    for s, h, _ in trios:
                        last = gp.tensor_copy(h, s)
                    last.then_inc(w_hi_ready, 1)
                    gp.wait_ge(w_hi_ready, n + 1)
                    for s, h, l in trios:
                        last = gp.tensor_tensor(l, s, f32(h), ALU.subtract)
                    last.then_inc(w_ready, 1)
                each_tile(gp, emit)

            @block.tensor
            def _(pe):
                def emit(kind, n, par, col, factor, name, tile, row):
                    pe.wait_ge(w_ready, n + 1)
                    if kind not in (ROPE, RAW):
                        pe.wait_ge(bank_free, (SPLITS + 2) * NC)
                    for c in range(NC):
                        if kind in (ROPE, RAW):
                            pe.wait_ge(bank_free, n * NC + (c + 1))
                        else:
                            pe.wait_ge(act_ready, (n - SPLITS) * NC + (c + 1))
                        tok = slice(c * CH, (c + 1) * CH)
                        out = out_ps[:, par, c, :]
                        for k in range(KT):
                            nc.tensor.matmul(out, w_hi[:, par, k, :], hT_hi[:, k, tok], start=(k == 0), stop=False)
                            nc.tensor.matmul(out, w_hi[:, par, k, :], hT_lo[:, k, tok], start=False, stop=False)
                            last = nc.tensor.matmul(out, w_lo[:, par, k, :], hT_hi[:, k, tok], start=False, stop=(k == KT - 1))
                        last.then_inc(chunk_done, 1)
                each_tile(pe, emit)

            @block.scalar
            def _(act):
                def emit(kind, n, par, col, factor, name, tile, row):
                    for c in range(NC):
                        q = n * NC + (c + 1)
                        out = out_ps[:, par, c, :]
                        tok = slice(c * CH, (c + 1) * CH)
                        act.wait_ge(stored[c % 2], stored_before(kind, n, c))
                        if kind in (ROPE, RAW):
                            act.wait_ge(rotated if kind == ROPE else chunk_done, q)
                            src = direct[:] if kind == ROPE else out
                            nc.scalar.activation(o_hi[:, c % 2, :], src, ACT.Copy, scale=factor).then_inc(hi_ready, 1)
                            act.wait_ge(lo_ready, q)
                            for part, stage in enumerate((o_hi, o_lo)):
                                if kind == RAW:
                                    dst = S[name][part, bass.ds(tile * 2 + row, 2), :, tok].rearrange("h d t -> (h d) t")
                                    act.dma_start(dst, f32(stage[:, c % 2, :])).then_inc(stored[c % 2], 16)
                                else:
                                    for s in range(2):
                                        dst = S[name][part, bass.ds(tile * 2 + row, 2), s * 32:(s + 1) * 32, tok]
                                        act.dma_start(dst, f32(stage[64 * s:64 * s + 64, c % 2, :])).then_inc(stored[c % 2], 16)
                        else:
                            act.wait_ge(chunk_done, q)
                            f = ACT.Silu if kind == SILU else ACT.Sigmoid
                            nc.scalar.activation(o_act[:, c % 2, :], out, f).then_inc(act_ready, 1)
                            act.wait_ge(act_ready, (n - SPLITS + 2) * NC + (c + 1))
                            act.dma_start(S[name][bass.ds(tile * P + row, P), tok], o_act[:, c % 2, :]).then_inc(stored[c % 2], 16)
                act.sem_inc(act_ready, 2 * NC)
                each_tile(act, emit)
                for par in range(2):
                    act.wait_ge(stored[par], 16 * 2 * (4 * ROPES + 2 * (SPLITS - ROPES) + 24))

            @block.vector
            def _(dv):
                dv.sem_inc(bank_free, 2 * NC)

                def emit(kind, n, par, col, factor, name, tile, row):
                    if kind not in (ROPE, RAW):
                        return
                    for c in range(NC):
                        q = n * NC + (c + 1)
                        out = out_ps[:, par, c, :]
                        tok = slice(c * CH, (c + 1) * CH)
                        src = out
                        if kind == ROPE:
                            dv.wait_ge(chunk_done, q)
                            nc.vector.tensor_tensor(direct[:], out, cosT[:, tok], ALU.mult)
                            nc.vector.tensor_tensor(crossed[0:64, :], out[64:P, :], sinT[64:P, tok], ALU.mult)
                            nc.vector.tensor_tensor(crossed[64:P, :], out[0:64, :], sinT[0:64, tok], ALU.mult).then_inc(bank_free, 1)
                            dv.wait_ge(bank_free, q + 2 * NC)
                            nc.vector.tensor_tensor(direct[:], direct[:], crossed[:], ALU.add).then_inc(rotated, 1)
                            src = direct[:]
                        dv.wait_ge(stored[c % 2], stored_before(kind, n, c))
                        dv.wait_ge(hi_ready, q)
                        lo = nc.vector.scalar_tensor_tensor(o_lo[:, c % 2, :], src, factor, f32(o_hi[:, c % 2, :]), ALU.mult, ALU.subtract)
                        lo.then_inc(lo_ready, 1)
                        dv.wait_ge(lo_ready, q)
                        if kind == RAW:
                            dv.sem_inc(bank_free, 1)
                first = 0
                for kind, col, tiles, factor, (name, row) in segments:
                    if kind in (ROPE, RAW):
                        if tiles == 1:
                            emit(kind, 0, 0, col, factor, name, 0, row)
                        else:
                            with dv.Fori(0, tiles // 2) as i:
                                for k in range(2):
                                    emit(kind, 2 * i + (first + k), (first + k) % 2, 0, factor, name, 2 * i + k, row)
                    first += tiles


SLIDING, FORGETTING = "swa", "fox"
UNROLLED = 4
SC = 4


def max_units(kind):
    units = []
    for i in range(NB):
        if kind == SLIDING:
            if i:
                units.append((i, (i - 1) * P, 2 * P, 0, 2 * P, 2 * P))
            else:
                units.append((0, 0, 2 * P, 0, P, P))
        else:
            for kc in range(i // 4 + 1):
                used = min(CH, (i + 1) * P - kc * CH)
                units.append((i, kc * CH, max(used, 2 * P), kc, used, P if kc == i // 4 else 0))
    return units


def score_units(kind, c):
    units = []
    if kind == SLIDING:
        if c:
            units.append((4 * c - 1, 0, 2 * P, slice(2 * P, 4 * P)))
        for r in range(3):
            units.append((4 * c + r, r * P, 2 * P, slice(P, 3 * P)))
        units.append((4 * c + 3, 2 * P, 2 * P, slice(0, 2 * P)))
    else:
        for j in range(4 * c):
            units.append((j, 0, CH, None))
        for r in range(3):
            units.append((4 * c + r, r * P, CH - r * P, slice(P, 2 * P)))
        units.append((4 * c + 3, 2 * P, 2 * P, slice(0, 2 * P)))
    return units


def clear(nc, kept):
    with nc.Block() as block:
        @block.gpsimd
        def _(gp):
            for sem in kept.values():
                gp.sem_clear(sem)


def attend(nc, I, S, kind, gate_row, kept):
    swa = kind == SLIDING
    first_head = 0 if swa else NH
    sets = UNROLLED if swa else 2
    kv_sets = 1 if swa else 2
    MUS = max_units(kind)
    MU = len(MUS)
    SU = sum(len(score_units(kind, c)) for c in range(NC))
    FROM = 256
    MAX_AFTER = 1 if swa else 2

    with ExitStack() as ctx:
        b = Memory(nc, ctx, kind, kept)
        qA = b.sb("q_hi_lo", [P, sets, T], F32R)
        qB = b.sb("q_hi_rows", [P, sets, T], F32R)
        kA = b.sb("k_hi_hi", [P, kv_sets, T], F32R)
        kB = b.sb("k_lo_rows", [P, kv_sets, T], F32R)
        v = b.sb("v", [P, kv_sets, NB, 4 * HD], F32R)
        z = b.sb("z", [HD, 2, T])
        p_raw = b.sb("p_raw", [P, SC, CH])
        p_hi = b.sb("p_hi", [P, SC, CH], F32R)
        p_lo = b.sb("p_lo", [P, SC, CH], F32R)
        recip = b.sb("recip", [HD, CH])
        head = b.sb("head", [HD, 2, CH])
        gated = b.sb("gated", [HD, 2, CH])
        pm = b.sb("part_max", [P, NB, NC])
        neg_m = b.sb("neg_m", [P, NB])
        m_hi = b.sb("m_hi", [NB, P], F32R)
        m_lo = b.sb("m_lo", [NB, P], F32R)
        ident = b.sb("ident", [P, P])
        ident_b = b.sb("ident_b", [P, P], BF16)
        mask_t = b.sb("mask_t", [P, 4 * P], BF16)
        mask_r = b.sb("mask_r", [P, 2 * P], BF16)
        s_ps = b.ps("s_ps", [P, 2, CH])
        max_ps = b.ps("max_ps", [P, 2, CH])
        att_ps = b.ps("att_ps", [P, 2, CH])
        row_ps = b.ps("row_ps", [P, CH])
        if swa:
            sink = b.sb("sink", [P, NH])
            e_raw = b.sb("e_raw", [NB, P])
            e_hi = b.sb("e_hi", [NB, P], F32R)
            e_lo = b.sb("e_lo", [NB, P], F32R)
            e_rows = b.sb("e_rows", [2, sets, T], F32R)
            e_one = b.sb("e_one", [2, P], F32R)
        else:
            cond = b.sb("cond", [P, KT])
            cond_bc = b.sb("cond_bc", [P, KT, P])
            w_gate = b.sb("w_gate", [P, KT, D])
            b_gate = b.sb("b_gate", [P, D])

        passed = b.sem("passed")
        small = b.sem("small_loaded")
        consts = b.sem("constants")
        filled = b.sem("rows_filled")
        q_loaded = [b.sem(f"q_loaded{i}") for i in range(sets)]
        kv_loaded = [b.sem(f"kv_loaded{i}") for i in range(kv_sets)]
        z_loaded = [b.sem(f"z_loaded{i}") for i in range(2)]
        head_done = b.sem("head_done")
        max_done = b.sem("max_scores_done")
        maxed = b.sem("max_taken")
        m_ready = b.sem("neg_max_ready")
        turned = b.sem("max_turned")
        m_split = b.sem("max_split")
        m_steps = b.sem("max_steps")
        e_ready = b.sem("sink_exp_ready")
        m_stored = b.sem("max_stored")
        m_rows = b.sem("max_rows_loaded")
        s_done = b.sem("scores_done")
        p_raw_ready = b.sem("p_raw_ready")
        p_hi_ready = b.sem("p_hi_ready")
        p_lo_ready = b.sem("p_lo_ready")
        pv_done = b.sem("pv_done")
        att_done = b.sem("att_done")
        recip_ready = b.sem("recip_ready")
        head_ready = b.sem("head_ready")
        gated_ready = b.sem("gated_ready")
        stored = [ctx.enter_context(nc.semaphore(f"{kind}_stored{i}")) for i in range(2)]
        gate_done = b.sem("gate_done")
        gate_loaded = b.sem("gate_loaded")
        SPLIT_STEPS = 4 if swa else 2

        made_all = []
        with nc.Block() as block:
            @block.sync
            def _(sp):
                if swa:
                    sp.dma_start(sink[:], I["sinks"].to_broadcast([P, NH])).then_inc(small, 16)
                else:
                    sp.dma_start(cond[:], I["c"].rearrange("o (k p) -> p (o k)", p=P), allow_slow_non_contiguous=True).then_inc(small, 16)

                def load_kv(j, u):
                    h = 4 * j + u
                    ks = 0 if swa else u % 2
                    kh = j if swa else h + KV
                    vcol = W + HD * j if swa else HD * h
                    sem = kv_loaded[ks]
                    for part in (0, 1):
                        sp.dma_start(f32(kA[part * HD:(part + 1) * HD, ks, :]), S["k"][0, bass.ds(kh, 1), :, :].rearrange("h d t -> (h d) t")).then_inc(sem, 16)
                        sp.dma_start(f32(v[:, ks, :, part * 2 * HD:part * 2 * HD + HD]),
                                     S["v"][part, :, bass.ds(vcol, HD)].rearrange("(n p) d -> p n d", p=P)).then_inc(sem, 16)
                    sp.dma_start(f32(kB[0:HD, ks, :]), S["k"][1, bass.ds(kh, 1), :, :].rearrange("h d t -> (h d) t")).then_inc(sem, 16)
                    sp.wait_ge(filled, 1)
                    sp.dma_start(f32(kB[HD:HD + 2, ks, :]), S["negc"][:, bass.ds(h + first_head, 1), :].rearrange("s h t -> s (h t)")).then_inc(sem, 16)

                def load_q(j, u):
                    h = 4 * j + u
                    sp.wait_ge(filled, 2)
                    for part, (dst, rows) in enumerate(((qA, 0), (qA, HD), (qB, 0))):
                        src = S["q"][part % 2, bass.ds(h + first_head, 1), :, :].rearrange("h d t -> (h d) t")
                        sp.dma_start(f32(dst[rows:rows + HD, u % sets, :]), src).then_inc(q_loaded[u % sets], 16)

                def max_rows(j, u):
                    h = 4 * j + u
                    sp.wait_ge(m_split, (h + 1) * SPLIT_STEPS)
                    for part, src in enumerate((m_hi, m_lo)):
                        sp.dma_start(S["m"][part, bass.ds(h, 1), :].rearrange("h (n p) -> (h n) p", p=P), f32(src[:])).then_inc(m_stored, 16)
                    if swa:
                        for part, src in enumerate((e_hi, e_lo)):
                            sp.dma_start(S["m"][part, bass.ds(h + NH, 1), :].rearrange("h (n p) -> (h n) p", p=P), f32(src[:])).then_inc(m_stored, 16)
                    rows = 4 if swa else 2
                    sp.wait_ge(m_stored, (h + 1) * 16 * rows)
                    sp.dma_start(f32(qB[HD + 2:HD + 4, u % sets, :]), S["m"][:, bass.ds(h, 1), :].rearrange("s h t -> s (h t)")).then_inc(m_rows, 16)
                    if swa:
                        sp.dma_start(f32(e_rows[:, u % sets, :]), S["m"][:, bass.ds(h + NH, 1), :].rearrange("s h t -> s (h t)")).then_inc(m_rows, 16)

                with sp.Fori(0, NH // UNROLLED) as j:
                    for u in range(UNROLLED):
                        h = 4 * j + u
                        sp.wait_ge(head_done, h + 1)
                        sp.sem_inc(passed, 1)
                        if swa and u == 0:
                            sp.wait_ge(head_done, h + sets)
                        if not swa or u == 0:
                            load_kv(j, u)
                        load_q(j, u)
                        sp.wait_ge(gated_ready, h * NC + NC)
                        sp.dma_start(z[:, u % 2, :], S["z"][bass.ds(HD * h + (0 if swa else W), HD), :]).then_inc(z_loaded[u % 2], 16)
                        max_rows(j, u)
                if not swa:
                    sp.dma_start(b_gate[:], I["b_ada"][:, 2 * D:3 * D].to_broadcast([P, D])).then_inc(small, 16)

            @block.gpsimd
            def _(gp):
                made = [0]

                def const(instruction):
                    made[0] += 1
                    instruction.then_inc(consts, 1)
                    gp.wait_ge(consts, made[0])

                const(gp.memset(f32(v[:, :, :, HD:2 * HD]), 1.0))
                const(gp.memset(f32(v[:, :, :, 3 * HD:4 * HD]), 0.0))
                const(gp.memset(ident[:], 0.0))
                const(gp.memset(mask_t[:, 0:P], MASKED))
                const(gp.memset(mask_t[:, P:3 * P], 0.0))
                const(gp.memset(mask_t[:, 3 * P:4 * P], MASKED))
                const(gp.memset(mask_r[:], 0.0))
                if swa:
                    const(gp.memset(f32(e_one[:, 0:HD]), 0.0))
                    const(gp.memset(f32(e_one[:, HD:P]), 1.0))
                const(gp.affine_select(out=ident[:], in_=ident[:], compare_op=ALU.not_equal, fill=1.0,
                                       base=0, pattern=[[-1, P]], channel_multiplier=1))
                const(gp.affine_select(out=mask_t[:, P:2 * P], in_=mask_t[:, P:2 * P], compare_op=ALU.is_ge, fill=MASKED,
                                       base=0, pattern=[[1, P]], channel_multiplier=-1))
                const(gp.affine_select(out=mask_t[:, 2 * P:3 * P], in_=mask_t[:, 2 * P:3 * P], compare_op=ALU.is_gt, fill=MASKED,
                                       base=0, pattern=[[-1, P]], channel_multiplier=1))
                const(gp.affine_select(out=mask_r[:, 0:P], in_=mask_r[:, 0:P], compare_op=ALU.is_gt, fill=MASKED,
                                       base=0, pattern=[[1, P]], channel_multiplier=-1))
                const(gp.affine_select(out=mask_r[:, P:2 * P], in_=mask_r[:, P:2 * P], compare_op=ALU.is_ge, fill=MASKED,
                                       base=0, pattern=[[-1, P]], channel_multiplier=1))
                const(gp.tensor_copy(ident_b[:], ident[:]))
                made_all.append(made[0])
                if not swa:
                    gp.dma_start(w_gate[:], I["w_ada"][0, :, 2 * D:3 * D].rearrange("(k p) n -> p k n", p=P)).then_inc(gate_loaded, 16)
                gp.sem_inc(gated_ready, 2 * NC)
                with gp.Fori(0, NH // UNROLLED) as j:
                    for u in range(UNROLLED):
                        h = 4 * j + u
                        gp.wait_ge(z_loaded[u % 2], (2 * j + u // 2 + 1) * 16)
                        for c in range(NC):
                            tok = slice(c * CH, (c + 1) * CH)
                            gp.wait_ge(head_ready, h * NC + c + 3)
                            gp.wait_ge(stored[c % 2], (h * 2 + c // 2) * 16)
                            gp.tensor_tensor(gated[:, c % 2, :], head[:, c % 2, :], z[:, u % 2, tok], ALU.mult).then_inc(gated_ready, 1)
                            gp.wait_ge(gated_ready, h * NC + c + 1 + 2 * NC)
                            gp.dma_start(S["za"][bass.ds(HD * h + (0 if swa else W), HD), tok], gated[:, c % 2, :]).then_inc(stored[c % 2], 16)
                for i in range(2):
                    gp.wait_ge(stored[i], 2 * NH * 16)

            @block.tensor
            def _(pe):
                pe.sem_inc(head_done, sets)
                pe.sem_inc(max_done, FROM)
                pe.sem_inc(pv_done, SC)

                def maxima(j, u):
                    h = 4 * j + u
                    qs, ks = u % sets, (0 if swa else u % 2)
                    pe.wait_ge(q_loaded[qs], q_count(j, u))
                    pe.wait_ge(kv_loaded[ks], kv_count(j, u))
                    for n, (i, k0, width, _, used, mask) in enumerate(MUS):
                        blk, keys = slice(i * P, (i + 1) * P), slice(k0, k0 + width)
                        out = max_ps[:, n % 2, 0:width]
                        pe.wait_ge(maxed, h * MU + (n + 1 + FROM))
                        nc.tensor.matmul(out, qA[:, qs, blk], kA[:, ks, keys], start=True, stop=False)
                        last = nc.tensor.matmul(out, qB[0:HD + 2, qs, blk], kB[0:HD + 2, ks, keys], start=False, stop=not mask)
                        if mask:
                            last = nc.tensor.matmul(max_ps[:, n % 2, used - mask:used], ident_b[:], mask_r[:, 2 * P - mask:2 * P],
                                                    start=False, stop=True)
                        last.then_inc(max_done, 1)

                def turn(j, u):
                    h = 4 * j + u
                    pe.wait_ge(m_ready, h + 1)
                    nc.tensor.transpose(row_ps[0:NB, 0:P], neg_m[:], ident[:]).then_inc(turned, 1)

                def chunks(j, u, cs, behind=None):
                    h = 4 * j + u
                    qs, ks = u % sets, (0 if swa else u % 2)
                    for c in cs:
                        units = score_units(kind, c)
                        base = sum(len(score_units(kind, x)) for x in range(c))
                        for n in range(len(units) + 2):
                            if n < len(units):
                                blk, off, width, mask = units[n]
                                keys = slice(blk * P, (blk + 1) * P)
                                qry = slice(c * CH + off, c * CH + off + width)
                                bank = (u * SU + base + n) % 2
                                out = s_ps[:, bank, off:off + width]
                                pe.wait_ge(p_hi_ready, h * SU + (base + n + 1))
                                nc.tensor.matmul(out, kA[:, ks, keys], qA[:, qs, qry], start=True, stop=False)
                                last = nc.tensor.matmul(out, kB[0:HD + 4, ks, keys], qB[0:HD + 4, qs, qry], start=False, stop=mask is None)
                                if mask is not None:
                                    mw = mask.stop - mask.start
                                    last = nc.tensor.matmul(s_ps[:, bank, off:off + mw], ident_b[:], mask_t[:, mask], start=False, stop=True)
                                last.then_inc(s_done, 1)
                            if n >= 2:
                                blk, off, width, _ = units[n - 2]
                                slot = (u * SU + base + n - 2) % SC
                                out = att_ps[:, c % 2, off:off + width]
                                if n == 2:
                                    pe.wait_ge(head_ready, h * NC + (c + 1))
                                pe.wait_ge(p_lo_ready, h * SU + (base + n - 1))
                                final = n - 2 == len(units) - 1
                                kw = dict(skip_group_check=True)
                                nc.tensor.matmul(out, v[:, ks, blk, 0:2 * HD], p_hi[:, slot, off:off + width], start=(n == 2), stop=False, **kw)
                                nc.tensor.matmul(out, v[:, ks, blk, 0:2 * HD], p_lo[:, slot, off:off + width], start=False, stop=False, **kw)
                                last = nc.tensor.matmul(out, v[:, ks, blk, 2 * HD:4 * HD], p_hi[:, slot, off:off + width], start=False,
                                                        stop=final and not swa, **kw)
                                last.then_inc(pv_done, 1)
                        if swa:
                            last = nc.tensor.matmul(att_ps[:, c % 2, :], e_one[:], e_rows[:, qs, c * CH:(c + 1) * CH], start=False, stop=True, **kw)
                            last.then_inc(att_done, 1)
                        if c == cs[0] and behind is not None:
                            behind()

                def q_count(j, u):
                    return (j * (UNROLLED // sets) + u // sets + 1) * 48

                def kv_count(j, u):
                    return (j + 1) * 96 if swa else (2 * j + u // 2 + 1) * 96

                pe.wait_ge(consts, made_all[0])
                with pe.Fori(0, NH // UNROLLED) as j:
                    maxima(j, 0)
                    turn(j, 0)
                    for u in range(UNROLLED):
                        h = 4 * j + u
                        pe.wait_ge(m_rows, (h + 1) * (32 if swa else 16))
                        chunks(j, u, range(0, MAX_AFTER + 1))
                        if u + 1 < UNROLLED:
                            maxima(j, u + 1)
                        chunks(j, u, range(MAX_AFTER + 1, NC), behind=(lambda: turn(j, u + 1)) if u + 1 < UNROLLED else None)
                        pe.wait_ge(pv_done, (h + 1) * SU + SC)
                        if swa:
                            pe.wait_ge(att_done, (h + 1) * NC)
                        pe.sem_inc(head_done, 1)
                if not swa:
                    pe.wait_ge(gate_loaded, 16)
                    pe.wait_ge(gate_done, 1)
                    for half in range(2):
                        for k in range(KT):
                            last = nc.tensor.matmul(max_ps[:, half, :], cond_bc[:, k, :], w_gate[:, k, half * CH:(half + 1) * CH],
                                                    start=(k == 0), stop=(k == KT - 1))
                        last.then_inc(gate_done, 1)

            @block.scalar
            def _(act):
                act.sem_inc(p_hi_ready, 2)

                def sinks(j, u):
                    h = 4 * j + u
                    act.wait_ge(turned, h + 1)
                    act.wait_ge(small, 16)
                    act.wait_ge(m_split, h * SPLIT_STEPS)
                    nc.scalar.activation(e_raw[:], row_ps[0:NB, 0:P], ACT.Exp, bias=sink[0:NB, bass.ds(h, 1)]).then_inc(e_ready, 1)

                def chunks(j, u, cs, behind=None):
                    h = 4 * j + u
                    for c in cs:
                        base = sum(len(score_units(kind, x)) for x in range(c))
                        for n, (blk, off, width, mask) in enumerate(score_units(kind, c)):
                            at = base + n
                            slot, bank = (u * SU + at) % SC, (u * SU + at) % 2
                            src = s_ps[:, bank, off:off + width]
                            act.wait_ge(s_done, h * SU + (at + 1))
                            act.wait_ge(pv_done, h * SU + (at + 1))
                            nc.scalar.activation(p_raw[:, slot, off:off + width], src, ACT.Exp).then_inc(p_raw_ready, 1)
                            nc.scalar.activation(p_hi[:, slot, off:off + width], src, ACT.Exp).then_inc(p_hi_ready, 1)
                        if c == cs[0] and behind is not None:
                            behind()

                with act.Fori(0, NH // UNROLLED) as j:
                    if swa:
                        sinks(j, 0)
                    for u in range(UNROLLED):
                        chunks(j, u, range(0, MAX_AFTER + 1))
                        chunks(j, u, range(MAX_AFTER + 1, NC), behind=(lambda: sinks(j, u + 1)) if swa and u + 1 < UNROLLED else None)

            @block.vector
            def _(dv):
                dv.sem_inc(maxed, 2 + FROM)
                dv.sem_inc(head_ready, 2)
                nc.vector.memset(f32(kB[HD:HD + 32, :, :]), 1.0).then_inc(filled, 1)
                nc.vector.memset(f32(qB[HD:HD + 32, :, :]), 1.0).then_inc(filled, 1)
                nc.vector.memset(pm[:], MASKED).then_inc(m_steps, 1)
                dv.wait_ge(m_steps, 1)
                if not swa:
                    dv.wait_ge(small, 16)
                    nc.vector.tensor_copy(cond_bc[:], cond[:].unsqueeze(2).to_broadcast([P, KT, P])).then_inc(gate_done, 1)

                def maxima(j, u):
                    h = 4 * j + u
                    dv.wait_ge(turned, h)
                    for n, (i, k0, width, kc, used, mask) in enumerate(MUS):
                        dv.wait_ge(max_done, h * MU + (n + 1 + FROM))
                        nc.vector.reduce_max(pm[:, i, kc:kc + 1], max_ps[:, n % 2, 0:used], AX.X).then_inc(maxed, 1)
                    dv.wait_ge(maxed, (h + 1) * MU + (2 + FROM))
                    if swa:
                        dv.wait_ge(small, 16)
                        nc.vector.tensor_scalar(neg_m[:], pm[:, :, 0], sink[:, bass.ds(h, 1)], -1.0, ALU.max, ALU.mult).then_inc(m_ready, 1)
                    else:
                        nc.vector.reduce_max(neg_m[:], pm[:], AX.X, negate=True).then_inc(m_ready, 1)

                def split(j, u):
                    h = 4 * j + u
                    row = row_ps[0:NB, 0:P]
                    if swa:
                        dv.wait_ge(e_ready, h + 1)
                    dv.wait_ge(turned, h + 1)
                    dv.wait_ge(m_stored, h * 16 * (4 if swa else 2))
                    nc.vector.tensor_copy(m_hi[:], row).then_inc(m_split, 1)
                    dv.wait_ge(m_split, h * SPLIT_STEPS + 1)
                    nc.vector.tensor_tensor(m_lo[:], row, f32(m_hi[:]), ALU.subtract).then_inc(m_split, 1)
                    if swa:
                        nc.vector.tensor_copy(e_hi[:], e_raw[:]).then_inc(m_split, 1)
                        dv.wait_ge(m_split, h * SPLIT_STEPS + 3)
                        nc.vector.tensor_tensor(e_lo[:], e_raw[:], f32(e_hi[:]), ALU.subtract).then_inc(m_split, 1)

                def chunks(j, u, cs, behind=None):
                    h = 4 * j + u
                    for c in cs:
                        base = sum(len(score_units(kind, x)) for x in range(c))
                        for n, (blk, off, width, mask) in enumerate(score_units(kind, c)):
                            at = base + n
                            slot = (u * SU + at) % SC
                            dv.wait_ge(p_hi_ready, h * SU + (at + 3))
                            nc.vector.tensor_tensor(p_lo[:, slot, off:off + width], p_raw[:, slot, off:off + width],
                                                    f32(p_hi[:, slot, off:off + width]), ALU.subtract).then_inc(p_lo_ready, 1)
                        if c == cs[0] and behind is not None:
                            behind()
                        if swa:
                            dv.wait_ge(att_done, h * NC + (c + 1))
                        else:
                            dv.wait_ge(pv_done, h * SU + (base + len(score_units(kind, c)) + SC))
                        nc.vector.reciprocal(recip[:], att_ps[HD:P, c % 2, :]).then_inc(recip_ready, 1)
                        dv.wait_ge(recip_ready, h * NC + (c + 1))
                        dv.wait_ge(gated_ready, h * NC + (c + 2 * NC - 1))
                        nc.vector.tensor_tensor(head[:, c % 2, :], att_ps[0:HD, c % 2, :], recip[:], ALU.mult).then_inc(head_ready, 1)
                        dv.wait_ge(head_ready, h * NC + (c + 3))

                with dv.Fori(0, NH // UNROLLED) as j:
                    maxima(j, 0)
                    split(j, 0)
                    for u in range(UNROLLED):
                        chunks(j, u, range(0, MAX_AFTER + 1))
                        if u + 1 < UNROLLED:
                            maxima(j, u + 1)
                        chunks(j, u, range(MAX_AFTER + 1, NC), behind=(lambda: split(j, u + 1)) if u + 1 < UNROLLED else None)
                if not swa:
                    for half in range(2):
                        dv.wait_ge(gate_done, 2 + half)
                        dv.wait_ge(small, 32)
                        cols = slice(half * CH, (half + 1) * CH)
                        nc.vector.tensor_tensor(gate_row[:, cols], max_ps[:, half, :], b_gate[:, cols], ALU.add)


def merge(nc, I, S):
    with ExitStack() as ctx:
        b = Memory(nc, ctx, "merge")
        a_raw = b.sb("a_raw", [P, KT, CH])
        a_hi = b.sb("a_hi", [P, KT, T], F32R)
        a_lo = b.sb("a_lo", [P, KT, T], F32R)
        w_raw = b.sb("w_raw", [P, 2, KT, P])
        w_hi = b.sb("w_hi", [P, 2, KT, P], F32R)
        w_lo = b.sb("w_lo", [P, 2, KT, P], F32R)
        gates = b.sb("gates", [P, 2, 2, CH])
        part = b.sb("part", [P, 2, CH])
        merged = b.sb("merged", [P, 2, CH])
        out_ps = b.ps("out_ps", [P, NC, 2, CH])
        passed = b.sem("passed")
        a_loaded = b.sem("a_loaded")
        a_hi_ready = b.sem("a_hi_ready")
        a_ready = b.sem("a_ready")
        w_loaded = [b.sem(f"w_loaded{i}") for i in range(2)]
        w_hi_ready = b.sem("w_hi_ready")
        w_ready = b.sem("w_ready")
        g_loaded = [b.sem(f"g_loaded{i}") for i in range(2)]
        chunk_done = b.sem("chunk_done")
        gated = b.sem("gated")
        merged_ready = b.sem("merged_ready")
        stored = [b.sem(f"stored{i}") for i in range(2)]
        TILES = D // P
        with nc.Block() as block:
            @block.sync
            def _(sp):
                def emit(n, par):
                    sp.wait_ge(w_ready, n + 1)
                    for half, w in enumerate(("w_o_swa", "w_o_fox")):
                        sp.dma_start(w_raw[:, par, 4 * half:4 * half + 4, :],
                                     I[w][0, :, bass.ds(n * P, P)].rearrange("(k p) c -> p k c", p=P)).then_inc(w_loaded[par], 16)
                    for c in range(NC):
                        sp.wait_ge(gated, n * NC + (c + 1))
                        for half in range(2):
                            sp.dma_start(gates[:, c % 2, half, :], S["g"][bass.ds(n * P + half * D, P), c * CH:(c + 1) * CH]).then_inc(g_loaded[c % 2], 16)
                for c in range(NC):
                    if c:
                        sp.wait_ge(a_ready, c)
                    sp.dma_start(a_raw[:], S["za"][:, c * CH:(c + 1) * CH].rearrange("(k p) t -> p k t", p=P)).then_inc(a_loaded, 16)
                with sp.Fori(0, TILES // 2) as i:
                    for par in range(2):
                        emit(2 * i + par, par)

            @block.gpsimd
            def _(gp):
                gp.sem_inc(w_ready, 2)
                with gp.Fori(0, TILES // 2) as i:
                    for par in range(2):
                        n = 2 * i + par
                        gp.wait_ge(w_loaded[par], (i + 1) * 32)
                        gp.wait_ge(chunk_done, n * NC)
                        gp.sem_inc(passed, 1)
                        gp.tensor_copy(w_hi[:, par], w_raw[:, par]).then_inc(w_hi_ready, 1)
                        gp.wait_ge(w_hi_ready, n + 1)
                        gp.tensor_tensor(w_lo[:, par], w_raw[:, par], f32(w_hi[:, par]), ALU.subtract).then_inc(w_ready, 1)

            @block.tensor
            def _(pe):
                pe.sem_inc(chunk_done, NC)
                with pe.Fori(0, TILES // 2) as i:
                    for par in range(2):
                        n = 2 * i + par
                        pe.wait_ge(w_ready, n + 3)
                        for c in range(NC):
                            tok = slice(c * CH, (c + 1) * CH)
                            pe.wait_ge(a_ready, c + 1)
                            pe.wait_ge(merged_ready, n * NC + (c + 1))
                            for k in range(KT):
                                out = out_ps[:, c, k // 4, :]
                                nc.tensor.matmul(out, w_hi[:, par, k, :], a_hi[:, k, tok], start=(k % 4 == 0), stop=False)
                                nc.tensor.matmul(out, w_hi[:, par, k, :], a_lo[:, k, tok], start=False, stop=False)
                                last = nc.tensor.matmul(out, w_lo[:, par, k, :], a_hi[:, k, tok], start=False, stop=(k % 4 == 3))
                            last.then_inc(chunk_done, 1)

            @block.scalar
            def _(act):
                for c in range(NC):
                    act.wait_ge(a_loaded, 16 * (c + 1))
                    nc.scalar.activation(a_hi[:, :, c * CH:(c + 1) * CH], a_raw[:], ACT.Copy).then_inc(a_hi_ready, 1)
                with act.Fori(0, TILES // 2) as i:
                    for par in range(2):
                        n = 2 * i + par
                        for c in range(NC):
                            act.wait_ge(merged_ready, n * NC + (c + 1 + NC))
                            act.dma_start(S["mg"][bass.ds(n * P, P), c * CH:(c + 1) * CH], merged[:, c % 2, :]).then_inc(stored[c % 2], 16)
                for c in range(2):
                    act.wait_ge(stored[c], TILES * NC // 2 * 16)

            @block.vector
            def _(dv):
                dv.sem_inc(gated, 2)
                dv.sem_inc(merged_ready, NC)
                for c in range(NC):
                    dv.wait_ge(a_hi_ready, c + 1)
                    nc.vector.tensor_tensor(a_lo[:, :, c * CH:(c + 1) * CH], a_raw[:], f32(a_hi[:, :, c * CH:(c + 1) * CH]),
                                            ALU.subtract).then_inc(a_ready, 1)
                with dv.Fori(0, TILES // 2) as i:
                    for par in range(2):
                        n = 2 * i + par
                        for c in range(NC):
                            dv.wait_ge(chunk_done, n * NC + (c + 1 + NC))
                            dv.wait_ge(g_loaded[c % 2], (n * 2 + (c // 2 + 1)) * 32)
                            for half in range(2):
                                last = nc.vector.tensor_tensor(part[:, half, :], out_ps[:, c, half, :], gates[:, c % 2, half, :], ALU.mult)
                            last.then_inc(gated, 1)
                            dv.wait_ge(gated, n * NC + (c + 3))
                            dv.wait_ge(stored[c % 2], (n * 2 + c // 2) * 16)
                            nc.vector.tensor_tensor(merged[:, c % 2, :], part[:, 0, :], part[:, 1, :], ALU.add).then_inc(merged_ready, 1)
                            dv.wait_ge(merged_ready, n * NC + (c + 1 + NC))


def finish(nc, I, S, gate_row, out):
    with ExitStack() as ctx:
        b = Memory(nc, ctx, "fin")
        w_raw = b.sb("w_raw", [P, 2, D])
        w_hi = b.sb("w_hi", [P, KT, D], F32R)
        w_lo = b.sb("w_lo", [P, KT, D], F32R)
        m_raw = b.sb("m_raw", [P, 2, KT, P])
        m_hi = b.sb("m_hi", [P, 2, KT, P], F32R)
        m_lo = b.sb("m_lo", [P, 2, KT, P], F32R)
        x_t = b.sb("x_t", [P, 2, D])
        res = b.sb("res", [P, 2, D])
        square = b.sb("square", [P, D])
        out_t = b.sb("out_t", [P, 2, D])
        g_row = b.sb("g_row", [P, D])
        ss = b.sb("ss", [P, 2])
        var = b.sb("var", [P, 2])
        inv = b.sb("inv", [P, 2])
        root = b.sb("root", [P, 2])
        fix = b.sb("fix", [P, 1])
        rstd = b.sb("rstd", [P, 1])
        out_ps = b.ps("out_ps", [P, 2, 2, CH])
        w_loaded = [b.sem(f"w_loaded{i}") for i in range(2)]
        w_hi_ready = b.sem("w_hi_ready")
        w_ready = b.sem("w_ready")
        small = b.sem("small_loaded")
        m_loaded = [b.sem(f"m_loaded{i}") for i in range(2)]
        x_loaded = [b.sem(f"x_loaded{i}") for i in range(2)]
        m_hi_ready = b.sem("m_hi_ready")
        m_ready = b.sem("m_ready")
        done = b.sem("products_done")
        scaled = b.sem("scaled")
        res_ready = b.sem("res_ready")
        summed = b.sem("summed")
        inverted = b.sem("inverted")
        rooted = b.sem("rooted")
        steps = b.sem("newton_steps")
        out_ready = b.sem("out_ready")
        stored = [b.sem(f"stored{i}") for i in range(2)]
        NEWTON = 5
        with nc.Block() as block:
            @block.sync
            def _(sp):
                sp.dma_start(g_row[:], I["g_final"].rearrange("(a n) -> a n", a=1).to_broadcast([P, D])).then_inc(small, 16)
                for k in range(KT):
                    if k >= 2:
                        sp.wait_ge(w_ready, k - 1)
                    sp.dma_start(w_raw[:, k % 2, :], I["w_out"][0, k * P:(k + 1) * P, :]).then_inc(w_loaded[k % 2], 16)
                with sp.Fori(0, NB // 2) as i:
                    for par in range(2):
                        n = 2 * i + par
                        sp.wait_ge(m_ready, n + 1)
                        sp.dma_start(m_raw[:, par], S["mg"][:, bass.ds(n * P, P)].rearrange("(k p) t -> p k t", p=P)).then_inc(m_loaded[par], 16)
                        sp.wait_ge(res_ready, n + 1)
                        sp.dma_start(x_t[:, par, :], I["x"][0, bass.ds(n * P, P), :]).then_inc(x_loaded[par], 16)

            @block.gpsimd
            def _(gp):
                for k in range(KT):
                    gp.wait_ge(w_loaded[k % 2], 16 * (k // 2 + 1))
                    gp.tensor_copy(w_hi[:, k, :], w_raw[:, k % 2, :]).then_inc(w_hi_ready, 1)
                    gp.wait_ge(w_hi_ready, k + 1)
                    gp.tensor_tensor(w_lo[:, k, :], w_raw[:, k % 2, :], f32(w_hi[:, k, :]), ALU.subtract).then_inc(w_ready, 1)

            @block.tensor
            def _(pe):
                pe.sem_inc(done, 2)
                pe.wait_ge(w_ready, KT)
                with pe.Fori(0, NB // 2) as i:
                    for par in range(2):
                        n = 2 * i + par
                        pe.wait_ge(m_ready, n + 3)
                        pe.wait_ge(scaled, n + 1)
                        for half in range(2):
                            cols = slice(half * CH, (half + 1) * CH)
                            o = out_ps[:, par, half, :]
                            for k in range(KT):
                                nc.tensor.matmul(o, m_hi[:, par, k, :], w_hi[:, k, cols], start=(k == 0), stop=False)
                                nc.tensor.matmul(o, m_hi[:, par, k, :], w_lo[:, k, cols], start=False, stop=False)
                                last = nc.tensor.matmul(o, m_lo[:, par, k, :], w_hi[:, k, cols], start=False, stop=(k == KT - 1))
                        last.then_inc(done, 1)

            @block.scalar
            def _(act):
                def split(n, par):
                    act.wait_ge(m_loaded[par], (n - par) * 8 + 16)
                    act.wait_ge(done, n + 1)
                    nc.scalar.activation(m_hi[:, par], m_raw[:, par], ACT.Copy).then_inc(m_hi_ready, 1)

                def norm(n, par):
                    act.wait_ge(res_ready, n + 3)
                    nc.scalar.activation(square[:], res[:, par, :], ACT.Square, accum_out=ss[:, par:par + 1]).then_inc(summed, 1)
                    act.wait_ge(inverted, n + 1)
                    nc.scalar.activation(root[:, par:par + 1], inv[:, par:par + 1], ACT.Sqrt).then_inc(rooted, 1)
                    act.wait_ge(out_ready, n + 1)
                    act.dma_start(out[0, bass.ds(n * P, P), :], out_t[:, par, :]).then_inc(stored[par], 16)

                split(0, 0)
                with act.Fori(0, NB // 2 - 1) as i:
                    for par in range(2):
                        split(2 * i + (par + 1), 1 - par)
                        norm(2 * i + par, par)
                split(NB - 1, 1)
                norm(NB - 2, 0)
                norm(NB - 1, 1)
                for par in range(2):
                    act.wait_ge(stored[par], NB // 2 * 16)

            @block.vector
            def _(dv):
                dv.sem_inc(m_ready, 2)
                dv.sem_inc(res_ready, 2)
                dv.sem_inc(scaled, 2)

                def split(n, par):
                    dv.wait_ge(m_hi_ready, n + 1)
                    nc.vector.tensor_tensor(m_lo[:, par], m_raw[:, par], f32(m_hi[:, par]), ALU.subtract).then_inc(m_ready, 1)

                def norm(n, par):
                    r = res[:, par, :]
                    dv.wait_ge(done, n + 3)
                    dv.wait_ge(out_ready, n)
                    nc.vector.tensor_tensor(r, out_ps[:, par, :, :].rearrange("p a b -> p (a b)"), gate_row[:], ALU.mult).then_inc(scaled, 1)
                    dv.wait_ge(scaled, n + 3)
                    dv.wait_ge(x_loaded[par], (n - par) * 8 + 16)
                    nc.vector.tensor_tensor(r, r, x_t[:, par, :], ALU.add).then_inc(res_ready, 1)
                    dv.wait_ge(summed, n + 1)
                    v, y = var[:, par:par + 1], root[:, par:par + 1]
                    nc.vector.tensor_scalar(v, ss[:, par:par + 1], 1.0 / D, EPS, ALU.mult, ALU.add).then_inc(steps, 1)
                    dv.wait_ge(steps, n * NEWTON + 1)
                    nc.vector.reciprocal(inv[:, par:par + 1], v).then_inc(inverted, 1)
                    dv.wait_ge(rooted, n + 1)
                    nc.vector.tensor_tensor(fix[:], y, y, ALU.mult).then_inc(steps, 1)
                    dv.wait_ge(steps, n * NEWTON + 2)
                    nc.vector.tensor_tensor(fix[:], fix[:], v, ALU.mult).then_inc(steps, 1)
                    dv.wait_ge(steps, n * NEWTON + 3)
                    nc.vector.tensor_scalar(fix[:], fix[:], -0.5, 1.5, ALU.mult, ALU.add).then_inc(steps, 1)
                    dv.wait_ge(steps, n * NEWTON + 4)
                    nc.vector.tensor_tensor(rstd[:], y, fix[:], ALU.mult).then_inc(steps, 1)
                    dv.wait_ge(steps, n * NEWTON + 5)
                    dv.wait_ge(stored[par], (n - par) * 8)
                    nc.vector.scalar_tensor_tensor(out_t[:, par, :], r, rstd[:, 0:1], g_row[:], ALU.mult, ALU.mult).then_inc(out_ready, 1)
                    dv.wait_ge(out_ready, n + 1)

                dv.wait_ge(small, 16)
                split(0, 0)
                with dv.Fori(0, NB // 2 - 1) as i:
                    for par in range(2):
                        split(2 * i + (par + 1), 1 - par)
                        norm(2 * i + par, par)
                split(NB - 1, 1)
                norm(NB - 2, 0)
                norm(NB - 1, 1)


_INS = ["x", "c", "positions", "w_ada", "b_ada", "g_norm", "w_in", "b_f", "sinks", "w_o_swa", "w_o_fox", "w_out", "g_final"]


def build(nc, I, out, upto=9):
    S = {
        "q": nc.dram_tensor("q_parts", (2, 2 * NH, HD, T), F32).ap(),
        "k": nc.dram_tensor("k_parts", (2, KV + NH, HD, T), F32).ap(),
        "v": nc.dram_tensor("v_parts", (2, T, VW), F32).ap(),
        "negc": nc.dram_tensor("negc_parts", (2, 2 * NH, T), F32).ap(),
        "m": nc.dram_tensor("m_parts", (2, 2 * NH, T), F32).ap(),
        "z": nc.dram_tensor("z_silu", (2 * W, T), F32).ap(),
        "g": nc.dram_tensor("sigmoid_gates", (2 * D, T), F32).ap(),
        "za": nc.dram_tensor("gated_heads", (2 * W, T), F32).ap(),
        "mg": nc.dram_tensor("merged", (D, T), F32).ap(),
    }
    with ExitStack() as ctx:
        keep = Memory(nc, ctx, "h")
        hT_hi = keep.sb("hT_hi", [P, KT, T], F32R)
        hT_lo = keep.sb("hT_lo", [P, KT, T], F32R)
        prepare_and_values(nc, I, S, hT_hi, hT_lo)
        if upto >= 2:
            project(nc, I, S, hT_hi, hT_lo)
    if upto >= 3:
        with ExitStack() as ctx:
            gate_row = Memory(nc, ctx, "gate").sb("row", [P, D])
            kept = {}
            attend(nc, I, S, SLIDING, gate_row, kept)
            clear(nc, kept)
            attend(nc, I, S, FORGETTING, gate_row, kept)
            if upto >= 4:
                merge(nc, I, S)
                finish(nc, I, S, gate_row, out)


def kernel(**inputs):
    import numpy as _np
    import concourse.bacc as _bacc
    from concourse import mybir as _mybir
    from concourse.bass_utils import run_bass_kernel_spmd as _run

    nc = _bacc.Bacc("TRN2", target_bir_lowering=False, num_devices=1)
    arrays = {name: _np.ascontiguousarray(inputs[name]) for name in _INS}
    freq = _np.float64(10000.0) ** (-_np.arange(0, HD, 2, dtype=_np.float64) / HD)
    arrays["inv_freq"] = _np.tile(freq.astype(_np.float32), 4).reshape(P, 1)
    I = {n: nc.dram_tensor(f"in_{n}", a.shape, _mybir.dt.from_np(a.dtype), kind="ExternalInput").ap() for n, a in arrays.items()}
    out = nc.dram_tensor("out_0", (1, T, D), _mybir.dt.float32, kind="ExternalOutput").ap()
    build(nc, I, out)
    r = _run(nc, [{f"in_{n}": a for n, a in arrays.items()}], core_ids=[0])
    return r.results[0]["out_0"]
```

```python
from contextlib import ExitStack

import concourse.bass as bass
from concourse import mybir

ALU = mybir.AluOpType
ACT = mybir.ActivationFunctionType
AX = mybir.AxisListType
F32 = mybir.dt.float32
F32R = mybir.dt.float32r
BF16 = mybir.dt.bfloat16
I32 = mybir.dt.int32

P = 128
T = 2048
D = 1024
KT = D // P
HD = 64
NH = 8
W = NH * HD
KV = 2
GROUP = NH // KV
NB = T // P
CH = 512
NC = T // CH
SCALE = HD ** -0.5
EPS = 1e-6
MASKED = -1e30

QA0 = 0
KA0 = QA0 + W
VA0 = KA0 + KV * HD
ZA0 = VA0 + KV * HD
QB0 = ZA0 + W
KB0 = QB0 + W
VB0 = KB0 + W
FB0 = VB0 + W
ZB0 = FB0 + NH
GA0 = ZB0 + W

VW = W + KV * HD
VF = VW + NH
VN = VF // 2

TWO_PI = 6.283185307179586
COARSE = 4096.0


def parts_of(value, bits, count):
    import math
    out = []
    for _ in range(count):
        e = math.floor(math.log2(value)) + 1 - bits if value > 0 else 0
        part = math.floor(value / 2.0 ** e) * 2.0 ** e
        out.append(part)
        value -= part
    return out


def f32(ap):
    return ap.bitcast(F32)


class Memory:

    def __init__(self, nc, ctx, stage):
        self.nc, self.ctx, self.stage = nc, ctx, stage

    def sb(self, name, shape, dt=F32):
        return self.ctx.enter_context(self.nc.sbuf_tensor(f"{self.stage}_{name}", shape, dt))

    def ps(self, name, shape, dt=F32):
        return self.ctx.enter_context(self.nc.psum_tensor(f"{self.stage}_{name}", shape, dt))

    def sem(self, name):
        return self.ctx.enter_context(self.nc.semaphore(f"{self.stage}_{name}"))


def chain(eng, sem):
    count = [0]

    def step(instruction):
        count[0] += 1
        instruction.then_inc(sem, 1)
        eng.wait_ge(sem, count[0])
    return step


def prepare_and_values(nc, I, S, hT_hi, hT_lo):
    with ExitStack() as ctx:
        m = Memory(nc, ctx, "prep")
        cond = m.sb("cond", [P, KT])
        bias_cols = m.sb("bias_cols", [P, 2 * KT])
        g_col = m.sb("g_col", [P, KT])
        gain = m.sb("gain", [P, KT])
        shift = m.sb("shift", [P, KT])
        ada_cols = m.sb("ada_cols", [P, 2 * KT])
        ident = m.sb("ident", [P, P])
        rstd = m.sb("rstd", [P, NB])
        vv = m.sb("vv", [P, NB])
        tmp = m.sb("tmp", [P, NB])
        forget = m.sb("forget", [P, NB, NH])

        with ExitStack() as early:
            a = Memory(nc, early, "ada")
            x_sb = a.sb("x", [P, NB, D])
            with ExitStack() as inner:
                b = Memory(nc, inner, "cond")
                WB = 3
                w_ada = b.sb("w_ada", [P, WB, D])
                square = b.ps("square", [P, D])
                sums = b.sb("sums", [P, NB])
                ada_ps = b.ps("ada_ps", [P, 2 * KT])
                small = b.sem("small_loaded")
                w_loaded = [b.sem(f"w_ada_loaded{i}") for i in range(WB)]
                x_loaded = [b.sem(f"x_loaded{i}") for i in range(4)]
                w_used = b.sem("w_ada_used")
                summed = b.sem("squares_summed")
                dve = b.sem("dve_steps")
                rooted = b.sem("rooted")
                pool = b.sem("identity_steps")
                inverted = b.sem("inverted")
                with nc.Block() as block:
                    @block.sync
                    def _(sp):
                        sp.dma_start(cond[:], I["c"].rearrange("o (k p) -> p (o k)", p=P), allow_slow_non_contiguous=True).then_inc(small, 16)
                        sp.dma_start(bias_cols[:], I["b_ada"][0, 0:2 * D].rearrange("(k p) -> p k", p=P), allow_slow_non_contiguous=True).then_inc(small, 16)
                        sp.dma_start(g_col[:], I["g_norm"][0, :].rearrange("(k p) -> p k", p=P), allow_slow_non_contiguous=True).then_inc(small, 16)
                        for u in range(2 * KT):
                            k, half = divmod(u, 2)
                            if u >= WB:
                                sp.wait_ge(w_used, u - WB + 1)
                            sp.dma_start(w_ada[:, u % WB, :], I["w_ada"][0, k * P:(k + 1) * P, half * D:(half + 1) * D]).then_inc(w_loaded[u % WB], 16)

                    @block.gpsimd
                    def _(gp):
                        gp.memset(ident[:], 0.0).then_inc(pool, 1)
                        gp.wait_ge(pool, 1)
                        gp.affine_select(out=ident[:], in_=ident[:], compare_op=ALU.not_equal, fill=1.0,
                                         base=0, pattern=[[-1, P]], channel_multiplier=1).then_inc(pool, 1)

                    @block.tensor
                    def _(pe):
                        pe.wait_ge(small, 48)
                        for u in range(2 * KT):
                            k, half = divmod(u, 2)
                            pe.wait_ge(w_loaded[u % WB], 16 * (u // WB + 1))
                            for j in range(KT):
                                col = half * KT + j
                                last = nc.tensor.matmul(ada_ps[:, col:col + 1], w_ada[:, u % WB, j * P:(j + 1) * P], cond[:, k:k + 1],
                                                        start=(u == 0 and j == 0), stop=(k == KT - 1), skip_group_check=True)
                            last.then_inc(w_used, 1)

                    @block.scalar
                    def _(act):
                        for q in range(4):
                            act.dma_start(x_sb[:, 4 * q:4 * q + 4, :],
                                          I["x"][0, q * CH:(q + 1) * CH, :].rearrange("(n p) d -> p n d", p=P)).then_inc(x_loaded[q], 16)
                        for n in range(NB):
                            act.wait_ge(x_loaded[n // 4], 16)
                            if n:
                                act.wait_ge(summed, n)
                            nc.scalar.activation(square[:], x_sb[:, n, :], ACT.Square, accum_out=sums[:, n:n + 1]).then_inc(summed, 1)
                        act.wait_ge(inverted, 1)
                        nc.scalar.activation(rstd[:], tmp[:], ACT.Sqrt).then_inc(rooted, 1)

                    @block.vector
                    def _(dv):
                        step = chain(dv, dve)
                        dv.wait_ge(summed, NB)
                        step(nc.vector.tensor_scalar(vv[:], sums[:], 1.0 / D, EPS, ALU.mult, ALU.add))
                        nc.vector.reciprocal(tmp[:], vv[:]).then_inc(inverted, 1)
                        dv.wait_ge(rooted, 1)
                        step(nc.vector.tensor_tensor(tmp[:], rstd[:], rstd[:], ALU.mult))
                        step(nc.vector.tensor_tensor(tmp[:], tmp[:], vv[:], ALU.mult))
                        step(nc.vector.tensor_scalar(tmp[:], tmp[:], -0.5, 1.5, ALU.mult, ALU.add))
                        step(nc.vector.tensor_tensor(rstd[:], rstd[:], tmp[:], ALU.mult))
                        dv.wait_ge(w_used, 2 * KT)
                        dv.wait_ge(small, 48)
                        step(nc.vector.tensor_tensor(ada_cols[:], ada_ps[:], bias_cols[:], ALU.add))
                        step(nc.vector.tensor_copy(shift[:], ada_cols[:, 0:KT]))
                        step(nc.vector.scalar_tensor_tensor(gain[:], ada_cols[:, KT:2 * KT], 1.0, g_col[:], ALU.add, ALU.mult))

            with ExitStack() as inner:
                b = Memory(nc, inner, "norm")
                xn = b.sb("xn", [P, D])
                h_raw = b.sb("h_raw", [P, KT, P])
                turned = b.ps("turned", [P, 2, 2, 4, P])
                xn_ready = b.sem("xn_ready")
                half_turned = b.sem("half_turned")
                raw_half = b.sem("raw_half_ready")
                hi_ready = b.sem("hi_ready")
                lo_ready = b.sem("lo_ready")
                with nc.Block() as block:
                    @block.vector
                    def _(dv):
                        with dv.Fori(0, NB) as n:
                            dv.wait_ge(half_turned, n * 2)
                            nc.vector.tensor_scalar(xn[:], x_sb[:, bass.ds(n, 1), :].rearrange("p a d -> p (a d)"),
                                                    rstd[:, bass.ds(n, 1)], None, ALU.mult).then_inc(xn_ready, 1)
                            dv.wait_ge(lo_ready, n)
                            for half in range(2):
                                dv.wait_ge(half_turned, n * 2 + half + 1)
                                for j in range(4):
                                    k = 4 * half + j
                                    last = nc.vector.tensor_scalar(h_raw[:, k, :], turned[:, half, 0, j, :], gain[:, k:k + 1], shift[:, k:k + 1],
                                                                   ALU.mult, ALU.add)
                                last.then_inc(raw_half, 1)

                    @block.tensor
                    def _(pe):
                        with pe.Fori(0, NB) as n:
                            pe.wait_ge(xn_ready, n + 1)
                            for half in range(2):
                                pe.wait_ge(raw_half, n * 2)
                                for j in range(4):
                                    k = 4 * half + j
                                    last = nc.tensor.transpose(turned[:, half, 0, j, :], xn[:, k * P:(k + 1) * P], ident[:])
                                last.then_inc(half_turned, 1)

                    @block.scalar
                    def _(act):
                        with act.Fori(0, NB) as n:
                            act.wait_ge(raw_half, n * 2 + 2)
                            nc.scalar.activation(hT_hi[:, :, bass.ds(n * P, P)], h_raw[:], ACT.Copy).then_inc(hi_ready, 1)

                    @block.gpsimd
                    def _(gp):
                        with gp.Fori(0, NB) as n:
                            gp.wait_ge(hi_ready, n + 1)
                            gp.tensor_tensor(hT_lo[:, :, bass.ds(n * P, P)], h_raw[:], f32(hT_hi[:, :, bass.ds(n * P, P)]),
                                             ALU.subtract).then_inc(lo_ready, 1)

        with ExitStack() as inner:
            b = Memory(nc, inner, "val")
            w_raw = b.sb("w_raw", [P, 2, VF])
            w_hi = b.sb("w_hi", [P, KT, VF], F32R)
            w_lo = b.sb("w_lo", [P, KT, VF], F32R)
            v_hi = b.sb("v_hi", [P, 2, VF], F32R)
            v_lo = b.sb("v_lo", [P, 2, VF], F32R)
            bf_row = b.sb("bf_row", [P, NH])
            upper = b.sb("upper", [P, P])
            ones = b.sb("ones", [P, P])
            e_neg = b.sb("e_neg", [P, NB, NH])
            one_e = b.sb("one_e", [P, NB, NH])
            ln_e = b.sb("ln_e", [P, NB, NH])
            flat = b.sb("flat", [P, NB, NH])
            cum = b.sb("cum", [P, NH, NB])
            c_hi = b.sb("c_hi", [P, P], F32R)
            c_lo = b.sb("c_lo", [P, P], F32R)
            zeros = b.sb("zeros", [P, P])
            out_ps = b.ps("out_ps", [P, 4, CH])
            sum_ps = b.ps("sum_ps", [P, NB, NH])
            tot_ps = b.ps("tot_ps", [P, 512])
            row_ps = b.ps("row_ps", [P, 512])
            loaded = [b.sem(f"w_loaded{i}") for i in range(2)]
            split_hi = b.sem("w_hi_ready")
            split = b.sem("w_split")
            small = b.sem("small_loaded")
            done = b.sem("products_done")
            hi_ready = b.sem("v_hi_ready")
            lo_ready = b.sem("v_lo_ready")
            stored = [b.sem(f"v_stored{i}") for i in range(2)]
            consts = b.sem("constants")
            dve = b.sem("dve_steps")
            logit_ready = b.sem("logit_ready")
            e_ready = b.sem("e_ready")
            one_ready = b.sem("one_ready")
            ln_ready = b.sem("ln_ready")
            logf_ready = b.sem("logf_ready")
            sums_ready = b.sem("sums_ready")
            cum_ready = b.sem("cum_ready")
            rows_ready = b.sem("rows_ready")
            rows_split = b.sem("rows_split")
            rows_stored = b.sem("rows_stored")
            with nc.Block() as block:
                @block.sync
                def _(sp):
                    sp.dma_start(bf_row[:], I["b_f"].to_broadcast([P, NH])).then_inc(small, 16)
                    for k in range(KT):
                        if k >= 2:
                            sp.wait_ge(split, k - 1)
                        rows = I["w_in"][0, k * P:(k + 1) * P, :]
                        sp.dma_start(w_raw[:, k % 2, 0:W], rows[:, VB0:VB0 + W]).then_inc(loaded[k % 2], 16)
                        sp.dma_start(w_raw[:, k % 2, W:VW], rows[:, VA0:VA0 + KV * HD]).then_inc(loaded[k % 2], 16)
                        sp.dma_start(w_raw[:, k % 2, VW:VF], rows[:, FB0:FB0 + NH]).then_inc(loaded[k % 2], 16)
                    for n in range(NB):
                        sp.wait_ge(lo_ready, 2 * n + 2)
                        for part, src in enumerate((v_hi, v_lo)):
                            sp.dma_start(S["v"][part, n * P:(n + 1) * P, :], f32(src[:, n % 2, 0:VW])).then_inc(stored[n % 2], 16)
                    sp.wait_ge(consts, 4)
                    for part in range(2):
                        sp.dma_start(S["negc"][part, 0:NH, :].rearrange("h (n p) -> (h n) p", p=P), zeros[:]).then_inc(rows_stored, 16)
                    sp.wait_ge(rows_split, 2)
                    for part, src in enumerate((c_hi, c_lo)):
                        sp.dma_start(S["negc"][part, NH:2 * NH, :].rearrange("h (n p) -> (h n) p", p=P), f32(src[:])).then_inc(rows_stored, 16)
                    sp.wait_ge(stored[0], 16 * NB)
                    sp.wait_ge(stored[1], 16 * NB)
                    sp.wait_ge(rows_stored, 64)

                @block.gpsimd
                def _(gp):
                    gp.memset(upper[:], 1.0).then_inc(consts, 1)
                    gp.memset(ones[:], 1.0).then_inc(consts, 1)
                    gp.memset(zeros[:], 0.0).then_inc(consts, 1)
                    gp.wait_ge(consts, 3)
                    gp.affine_select(out=upper[:], in_=upper[:], compare_op=ALU.is_ge, fill=0.0,
                                     base=0, pattern=[[1, P]], channel_multiplier=-1).then_inc(consts, 1)
                    for k in range(KT):
                        gp.wait_ge(loaded[k % 2], 48 * (k // 2 + 1))
                        gp.tensor_copy(w_hi[:, k, :], w_raw[:, k % 2, :]).then_inc(split_hi, 1)
                        gp.wait_ge(split_hi, k + 1)
                        gp.tensor_tensor(w_lo[:, k, :], w_raw[:, k % 2, :], f32(w_hi[:, k, :]), ALU.subtract).then_inc(split, 1)

                @block.tensor
                def _(pe):
                    for n in range(NB):
                        tok = slice(n * P, (n + 1) * P)
                        for half in range(2):
                            unit = 2 * n + half
                            cols = slice(half * VN, (half + 1) * VN)
                            out = out_ps[:, unit % 4, 0:VN]
                            if unit >= 4:
                                pe.wait_ge(lo_ready, unit - 3)
                            for k in range(KT):
                                if unit == 0:
                                    pe.wait_ge(split, k + 1)
                                nc.tensor.matmul(out, hT_hi[:, k, tok], w_hi[:, k, cols], start=(k == 0), stop=False)
                                nc.tensor.matmul(out, hT_hi[:, k, tok], w_lo[:, k, cols], start=False, stop=False)
                                last = nc.tensor.matmul(out, hT_lo[:, k, tok], w_hi[:, k, cols], start=False, stop=(k == KT - 1))
                            last.then_inc(done, 1)
                    pe.wait_ge(logf_ready, 1)
                    pe.wait_ge(consts, 4)
                    nc.tensor.matmul(sum_ps[:], upper[:], flat[:], start=True, stop=True)
                    nc.tensor.matmul(tot_ps[:, 0:NB * NH], ones[:], flat[:].rearrange("p n h -> p (n h)"), start=True, stop=True).then_inc(sums_ready, 1)
                    pe.wait_ge(cum_ready, 1)
                    nc.tensor.transpose(row_ps[:, 0:P], cum[:].rearrange("p h n -> p (h n)"), ident[:]).then_inc(rows_ready, 1)

                @block.scalar
                def _(act):
                    for n in range(NB):
                        if n >= 2:
                            act.wait_ge(stored[n % 2], 32 * (n // 2))
                        for half in range(2):
                            unit = 2 * n + half
                            act.wait_ge(done, unit + 1)
                            nc.scalar.activation(v_hi[:, n % 2, half * VN:(half + 1) * VN], out_ps[:, unit % 4, 0:VN], ACT.Copy).then_inc(hi_ready, 1)
                    act.wait_ge(logit_ready, 1)
                    nc.scalar.activation(e_neg[:], flat[:], ACT.Exp, scale=-1.0).then_inc(e_ready, 1)
                    act.wait_ge(one_ready, 1)
                    nc.scalar.activation(ln_e[:], one_e[:], ACT.Ln).then_inc(ln_ready, 1)
                    act.wait_ge(rows_ready, 1)
                    nc.scalar.activation(c_hi[:], row_ps[:, 0:P], ACT.Copy, scale=-1.0).then_inc(rows_split, 1)

                @block.vector
                def _(dv):
                    step = chain(dv, dve)
                    for n in range(NB):
                        if n >= 2:
                            dv.wait_ge(stored[n % 2], 32 * (n // 2))
                        for half in range(2):
                            unit = 2 * n + half
                            dv.wait_ge(hi_ready, unit + 1)
                            cols = slice(half * VN, (half + 1) * VN)
                            if half:
                                step(nc.vector.tensor_copy(forget[:, n, :], out_ps[:, unit % 4, VN - NH:VN]))
                            nc.vector.tensor_tensor(v_lo[:, n % 2, cols], out_ps[:, unit % 4, 0:VN], f32(v_hi[:, n % 2, cols]),
                                                    ALU.subtract).then_inc(lo_ready, 1)
                    dv.wait_ge(small, 16)
                    step(nc.vector.tensor_tensor(forget[:], forget[:], bf_row[:].unsqueeze(1).to_broadcast([P, NB, NH]), ALU.add))
                    step(nc.vector.tensor_scalar(flat[:], forget[:], -1.0, None, ALU.mult))
                    nc.vector.tensor_tensor(flat[:], flat[:], forget[:], ALU.max).then_inc(logit_ready, 1)
                    dv.wait_ge(e_ready, 1)
                    nc.vector.tensor_scalar(one_e[:], e_neg[:], 1.0, None, ALU.add).then_inc(one_ready, 1)
                    dv.wait_ge(ln_ready, 1)
                    step(nc.vector.tensor_scalar(one_e[:], one_e[:], -1.0, None, ALU.add))
                    step(nc.vector.tensor_scalar(flat[:], one_e[:], 0.0, None, ALU.is_equal))
                    step(nc.vector.tensor_tensor(ln_e[:], ln_e[:], flat[:], ALU.add))
                    step(nc.vector.tensor_tensor(one_e[:], one_e[:], flat[:], ALU.add))
                    step(nc.vector.reciprocal(one_e[:], one_e[:]))
                    step(nc.vector.tensor_tensor(ln_e[:], ln_e[:], one_e[:], ALU.mult))
                    step(nc.vector.tensor_tensor(ln_e[:], ln_e[:], e_neg[:], ALU.mult))
                    nc.vector.scalar_tensor_tensor(flat[:], forget[:], 0.0, ln_e[:], ALU.min, ALU.subtract).then_inc(logf_ready, 1)
                    dv.wait_ge(sums_ready, 1)
                    step(nc.vector.memset(e_neg[:, 0, :], 0.0))
                    for n in range(1, NB):
                        step(nc.vector.tensor_tensor(e_neg[:, n, :], e_neg[:, n - 1, :], tot_ps[:, (n - 1) * NH:n * NH], ALU.add))
                    nc.vector.tensor_tensor(cum[:].rearrange("p h n -> p n h"), sum_ps[:], e_neg[:], ALU.add).then_inc(cum_ready, 1)
                    dv.wait_ge(rows_split, 1)
                    nc.vector.scalar_tensor_tensor(c_lo[:], row_ps[:, 0:P], -1.0, f32(c_hi[:]), ALU.mult, ALU.subtract).then_inc(rows_split, 1)


ROPE, RAW, SILU, SIGMOID = "rope", "raw", "silu", "sigmoid"


def project(nc, I, S, hT_hi, hT_lo):
    segments = [
        (ROPE, KA0, 1, 1.0, ("k", 0)),
        (ROPE, QA0, 4, SCALE, ("q", 0)),
        (RAW, QB0, 4, SCALE, ("q", NH)),
        (RAW, KB0, 4, 1.0, ("k", KV)),
        (SILU, ZA0, 4, 1.0, ("z", 0)),
        (SILU, ZB0, 4, 1.0, ("z", W)),
        (SIGMOID, GA0, 16, 1.0, ("g", 0)),
    ]

    def each_tile(eng, emit):
        first = 0
        for kind, col, tiles, factor, (name, row) in segments:
            if tiles == 1:
                emit(kind, 0, 0, col, factor, name, 0, row)
            else:
                with eng.Fori(0, tiles // 2) as i:
                    for k in range(2):
                        emit(kind, 2 * i + (first + k), (first + k) % 2, col + 2 * P * i + k * P, factor, name, 2 * i + k, row)
            first += tiles

    with ExitStack() as ctx:
        b = Memory(nc, ctx, "proj")
        cosT = b.sb("cos", [P, T])
        sinT = b.sb("sin", [P, T])

        with ExitStack() as inner:
            a = Memory(nc, inner, "tab")
            half_t = T // 2
            pos_i = a.sb("pos_i", [P, half_t], I32)
            turns_i = a.sb("turns_i", [P, half_t], I32)
            turns = a.sb("turns", [P, half_t])
            inv = a.sb("inv", [P, 1])
            loaded = a.sem("loaded")
            dve = a.sem("dve_steps")
            angle = a.sem("angle_ready")
            sined = a.sem("sines_done")
            coarse = parts_of(TWO_PI * COARSE, 7, 8)
            fine = parts_of(TWO_PI, 10, 5)
            with nc.Block() as block:
                @block.sync
                def _(sp):
                    sp.dma_start(inv[:], I["inv_freq"]).then_inc(loaded, 16)
                    for s in range(2):
                        if s:
                            sp.wait_ge(angle, 1)
                        sp.dma_start(pos_i[:], I["positions"][:, s * half_t:(s + 1) * half_t].to_broadcast([P, half_t])).then_inc(loaded, 16)

                @block.vector
                def _(dv):
                    step = chain(dv, dve)
                    for s in range(2):
                        ang = sinT[:, s * half_t:(s + 1) * half_t]
                        oth = cosT[:, s * half_t:(s + 1) * half_t]
                        dv.wait_ge(loaded, 32 + 16 * s)
                        step(nc.vector.tensor_copy(ang, pos_i[:]))
                        step(nc.vector.tensor_scalar(ang, ang, inv[:, 0:1], None, ALU.mult))
                        for period, pieces in ((TWO_PI * COARSE, coarse), (TWO_PI, fine)):
                            step(nc.vector.tensor_scalar(turns[:], ang, 1.0 / period, None, ALU.mult))
                            step(nc.vector.tensor_copy(turns_i[:], turns[:]))
                            step(nc.vector.tensor_copy(turns[:], turns_i[:]))
                            for piece in pieces:
                                step(nc.vector.scalar_tensor_tensor(ang, turns[:], -piece, ang, ALU.mult, ALU.add))
                        for op, bound, turn in ((ALU.is_gt, TWO_PI / 2, -TWO_PI), (ALU.is_lt, -TWO_PI / 2, TWO_PI)):
                            step(nc.vector.tensor_scalar(turns[:], ang, bound, turn, op, ALU.mult))
                            step(nc.vector.tensor_tensor(ang, ang, turns[:], ALU.add))
                        step(nc.vector.tensor_scalar(ang, ang, 3.1415925, -3.1415925, ALU.min, ALU.max))
                        step(nc.vector.tensor_scalar(oth, ang, -1.0, None, ALU.mult))
                        step(nc.vector.tensor_tensor(oth, oth, ang, ALU.max))
                        step(nc.vector.tensor_scalar(oth, oth, -1.0, TWO_PI / 4, ALU.mult, ALU.add))
                        nc.vector.tensor_scalar(ang[64:P, :], ang[64:P, :], -1.0, None, ALU.mult).then_inc(angle, 1)

                @block.scalar
                def _(act):
                    for s in range(2):
                        act.wait_ge(angle, s + 1)
                        for tab in (sinT, cosT):
                            part = tab[:, s * half_t:(s + 1) * half_t]
                            nc.scalar.activation(part, part, ACT.Sin).then_inc(sined, 1)

        w_raw = b.sb("w_raw", [P, 2, KT, P])
        w_hi = b.sb("w_hi", [P, 2, KT, P], F32R)
        w_lo = b.sb("w_lo", [P, 2, KT, P], F32R)
        o_hi = b.sb("o_hi", [P, 2, CH], F32R)
        o_lo = b.sb("o_lo", [P, 2, CH], F32R)
        o_act = b.sb("o_act", [P, 2, CH])
        direct = b.sb("direct", [P, CH])
        crossed = b.sb("crossed", [P, CH])
        out_ps = b.ps("out_ps", [P, 2, NC, CH])
        passed = b.sem("passed")
        w_loaded = [b.sem(f"w_loaded{i}") for i in range(2)]
        w_hi_ready = b.sem("w_hi_ready")
        w_ready = b.sem("w_ready")
        chunk_done = b.sem("chunk_done")
        bank_free = b.sem("bank_free")
        rotated = b.sem("rotated")
        hi_ready = b.sem("hi_ready")
        lo_ready = b.sem("lo_ready")
        act_ready = b.sem("act_ready")
        stored = [b.sem(f"stored{i}") for i in range(2)]

        ROPES = 5
        SPLITS = 13
        DMAS = {ROPE: 4, RAW: 2, SILU: 1, SIGMOID: 1}

        def stored_before(kind, n, c):
            since = {ROPE: 0, RAW: ROPES, SILU: SPLITS, SIGMOID: SPLITS}[kind]
            base = {ROPE: 0, RAW: 2 * 4 * ROPES}.get(kind, 2 * 4 * ROPES + 2 * 2 * (SPLITS - ROPES))
            return (n - since) * (2 * 16 * DMAS[kind]) + 16 * (base + DMAS[kind] * (c // 2))

        with nc.Block() as block:
            @block.sync
            def _(sp):
                def emit(kind, n, par, col, factor, name, tile, row):
                    if not (isinstance(n, int) and n == 0):
                        sp.wait_ge(w_ready, n - 1)
                    sp.dma_start(w_raw[:, par, :, :],
                                 I["w_in"][0, :, bass.ds(col, P)].rearrange("(k p) c -> p k c", p=P)).then_inc(w_loaded[par], 16)
                each_tile(sp, emit)

            @block.gpsimd
            def _(gp):
                def emit(kind, n, par, col, factor, name, tile, row):
                    gp.wait_ge(w_loaded[par], (n - par) * 8 + 16)
                    if not (isinstance(n, int) and n == 0):
                        gp.wait_ge(chunk_done, (n - 1) * NC)
                        gp.sem_inc(passed, 1)
                    if kind == ROPE:
                        src = w_raw[:, par, :, :].rearrange("p k (h s c) -> p s k h c", h=2, s=2)
                        hi = w_hi[:, par, :, :].rearrange("p k (s h c) -> p s k h c", h=2, s=2)
                        lo = w_lo[:, par, :, :].rearrange("p k (s h c) -> p s k h c", h=2, s=2)
                        trios = [(src[:, s], hi[:, s], lo[:, s]) for s in range(2)]
                    else:
                        trios = [(w_raw[:, par, :, :], w_hi[:, par, :, :], w_lo[:, par, :, :])]
                    for s, h, _ in trios:
                        last = gp.tensor_copy(h, s)
                    last.then_inc(w_hi_ready, 1)
                    gp.wait_ge(w_hi_ready, n + 1)
                    for s, h, l in trios:
                        last = gp.tensor_tensor(l, s, f32(h), ALU.subtract)
                    last.then_inc(w_ready, 1)
                each_tile(gp, emit)

            @block.tensor
            def _(pe):
                def emit(kind, n, par, col, factor, name, tile, row):
                    pe.wait_ge(w_ready, n + 1)
                    if kind not in (ROPE, RAW):
                        pe.wait_ge(bank_free, (SPLITS + 2) * NC)
                    for c in range(NC):
                        if kind in (ROPE, RAW):
                            pe.wait_ge(bank_free, n * NC + (c + 1))
                        else:
                            pe.wait_ge(act_ready, (n - SPLITS) * NC + (c + 1))
                        tok = slice(c * CH, (c + 1) * CH)
                        out = out_ps[:, par, c, :]
                        for k in range(KT):
                            nc.tensor.matmul(out, w_hi[:, par, k, :], hT_hi[:, k, tok], start=(k == 0), stop=False)
                            nc.tensor.matmul(out, w_hi[:, par, k, :], hT_lo[:, k, tok], start=False, stop=False)
                            last = nc.tensor.matmul(out, w_lo[:, par, k, :], hT_hi[:, k, tok], start=False, stop=(k == KT - 1))
                        last.then_inc(chunk_done, 1)
                each_tile(pe, emit)

            @block.scalar
            def _(act):
                def emit(kind, n, par, col, factor, name, tile, row):
                    for c in range(NC):
                        q = n * NC + (c + 1)
                        out = out_ps[:, par, c, :]
                        tok = slice(c * CH, (c + 1) * CH)
                        act.wait_ge(stored[c % 2], stored_before(kind, n, c))
                        if kind in (ROPE, RAW):
                            act.wait_ge(rotated if kind == ROPE else chunk_done, q)
                            src = direct[:] if kind == ROPE else out
                            nc.scalar.activation(o_hi[:, c % 2, :], src, ACT.Copy, scale=factor).then_inc(hi_ready, 1)
                            act.wait_ge(lo_ready, q)
                            for part, stage in enumerate((o_hi, o_lo)):
                                if kind == RAW:
                                    dst = S[name][part, bass.ds(tile * 2 + row, 2), :, tok].rearrange("h d t -> (h d) t")
                                    act.dma_start(dst, f32(stage[:, c % 2, :])).then_inc(stored[c % 2], 16)
                                else:
                                    for s in range(2):
                                        dst = S[name][part, bass.ds(tile * 2 + row, 2), s * 32:(s + 1) * 32, tok]
                                        act.dma_start(dst, f32(stage[64 * s:64 * s + 64, c % 2, :])).then_inc(stored[c % 2], 16)
                        else:
                            act.wait_ge(chunk_done, q)
                            f = ACT.Silu if kind == SILU else ACT.Sigmoid
                            nc.scalar.activation(o_act[:, c % 2, :], out, f).then_inc(act_ready, 1)
                            act.wait_ge(act_ready, (n - SPLITS + 2) * NC + (c + 1))
                            act.dma_start(S[name][bass.ds(tile * P + row, P), tok], o_act[:, c % 2, :]).then_inc(stored[c % 2], 16)
                act.sem_inc(act_ready, 2 * NC)
                each_tile(act, emit)
                for par in range(2):
                    act.wait_ge(stored[par], 16 * 2 * (4 * ROPES + 2 * (SPLITS - ROPES) + 24))

            @block.vector
            def _(dv):
                dv.sem_inc(bank_free, 2 * NC)

                def emit(kind, n, par, col, factor, name, tile, row):
                    if kind not in (ROPE, RAW):
                        return
                    for c in range(NC):
                        q = n * NC + (c + 1)
                        out = out_ps[:, par, c, :]
                        tok = slice(c * CH, (c + 1) * CH)
                        src = out
                        if kind == ROPE:
                            dv.wait_ge(chunk_done, q)
                            nc.vector.tensor_tensor(direct[:], out, cosT[:, tok], ALU.mult)
                            nc.vector.tensor_tensor(crossed[0:64, :], out[64:P, :], sinT[64:P, tok], ALU.mult)
                            nc.vector.tensor_tensor(crossed[64:P, :], out[0:64, :], sinT[0:64, tok], ALU.mult).then_inc(bank_free, 1)
                            dv.wait_ge(bank_free, q + 2 * NC)
                            nc.vector.tensor_tensor(direct[:], direct[:], crossed[:], ALU.add).then_inc(rotated, 1)
                            src = direct[:]
                        dv.wait_ge(stored[c % 2], stored_before(kind, n, c))
                        dv.wait_ge(hi_ready, q)
                        lo = nc.vector.scalar_tensor_tensor(o_lo[:, c % 2, :], src, factor, f32(o_hi[:, c % 2, :]), ALU.mult, ALU.subtract)
                        lo.then_inc(lo_ready, 1)
                        dv.wait_ge(lo_ready, q)
                        if kind == RAW:
                            dv.sem_inc(bank_free, 1)
                first = 0
                for kind, col, tiles, factor, (name, row) in segments:
                    if kind in (ROPE, RAW):
                        if tiles == 1:
                            emit(kind, 0, 0, col, factor, name, 0, row)
                        else:
                            with dv.Fori(0, tiles // 2) as i:
                                for k in range(2):
                                    emit(kind, 2 * i + (first + k), (first + k) % 2, 0, factor, name, 2 * i + k, row)
                    first += tiles


SLIDING, FORGETTING = 0, 1
KINDS = (SLIDING, FORGETTING)
UNROLLED = 4
P_SLOTS = 4
Z_SLOTS = 4
MAX_FIRST = ((-0.5, -0.4), (-0.35, 0.1))
MAX_REST = ((0.1, 0.5), (0.5, 1.04))
BEHIND = 0.15
SLIDING_AT = (-0.1, 0.22, 0.18)
RECIP_PARTS = 4
RECIP_SPACING = (2, 4)
LAG = 3


def max_units(kind):
    units = []
    for i in range(NB):
        if kind == SLIDING:
            units.append((i, (i - 1) * P, 2 * P, 0, 2 * P, 2 * P) if i else (0, 0, 2 * P, 0, P, P))
        else:
            for kc in range(i // 4 + 1):
                used = min(CH, (i + 1) * P - kc * CH)
                units.append((i, kc * CH, max(used, 2 * P), kc, used, P if kc == i // 4 else 0))
    return units


def score_units(kind, c):
    units = []
    if kind == SLIDING:
        if c:
            units.append((4 * c - 1, 0, 2 * P, slice(2 * P, 4 * P)))
        units += [(4 * c + r, r * P, 2 * P, slice(P, 3 * P)) for r in range(3)]
    else:
        units += [(j, 0, CH, None) for j in range(4 * c)]
        units += [(4 * c + r, r * P, CH - r * P, slice(P, 2 * P)) for r in range(3)]
    units.append((4 * c + 3, 2 * P, 2 * P, slice(0, 2 * P)))
    return units


def attention_order():
    placed = []

    def spread(items, start, end):
        for n, item in enumerate(items):
            placed.append((start + (end - start) * (n + 0.5) / len(items), len(placed), item))

    for u in range(UNROLLED):
        for kind in KINDS:
            start, end = MAX_FIRST[kind] if u == 0 else (u - 1 + x for x in MAX_REST[kind])
            spread([("max", kind, u, n) for n in range(len(max_units(kind)))], start, end)
            spread([("turn", kind, u)], end + 0.02, end + 0.02)
        spread([("score", FORGETTING, u, c, n) for c in range(NC) for n in range(len(score_units(FORGETTING, c)))],
               u + BEHIND, u + 1 + BEHIND)
        for c in range(NC):
            spread([("score", SLIDING, u, c, n) for n in range(len(score_units(SLIDING, c)))],
                   u + SLIDING_AT[0] + SLIDING_AT[1] * c, u + SLIDING_AT[0] + SLIDING_AT[1] * c + SLIDING_AT[2])
    order, waiting = [], []
    for _, _, item in sorted(placed):
        order.append(item)
        if item[0] == "score":
            waiting.append(item)
            if len(waiting) > LAG:
                order.append(("value", *waiting.pop(0)[1:]))
    order += [("value", *item[1:]) for item in waiting]

    def behind(step, distance, item):
        at = next(i for i, x in enumerate(order) if x[:len(step)] == step)
        order.insert(min(at + 1 + distance, len(order)), item)

    for u in range(UNROLLED):
        for kind in KINDS:
            for c in range(NC):
                last, distance = ("value", kind, u, c, len(score_units(kind, c)) - 1), 1
                for part in range(RECIP_PARTS):
                    behind(last, distance, ("recip", kind, u, c, part))
                    last, distance = ("recip", kind, u, c, part), RECIP_SPACING[kind]
                behind(last, 1, ("fin", kind, u, c))
    for u in range(UNROLLED):
        for kind in KINDS:
            for c in range(NC):
                behind(("fin", kind, u, c), 7, ("gate", kind, u, c))
    for u in range(2, UNROLLED):
        for kind in KINDS:
            behind(("fin", kind, u - 2, NC - 1), 0, ("load", kind, u))
    order = [("load", kind, u) for u in range(2) for kind in KINDS] + order
    return order


def attend(nc, I, S):
    order = attention_order()
    UNITS = [max_units(kind) for kind in KINDS]
    KV_SETS = (1, 2)

    def numbered(*steps):
        return {item[1:]: n for n, item in enumerate(x for x in order if x[0] in steps)}

    max_no, score_no, fin_no, turn_no = (numbered(s) for s in ("max", "score", "fin", "turn"))
    bank_no = numbered("max", "turn")
    value_no, gate_no, recip_no = numbered("value"), numbered("gate"), numbered("recip")
    assert list(value_no) == list(score_no) and list(gate_no) == list(fin_no)
    MAXES, BANKS, SCORES, FINS, TURNS = len(max_no), len(bank_no), len(score_no), len(fin_no), len(turn_no)
    assert BANKS % 2 == 0 and SCORES % P_SLOTS == 0 and FINS % Z_SLOTS == 0

    def last_score(kind, u, c):
        return score_no[kind, u, c, len(score_units(kind, c)) - 1]

    with ExitStack() as ctx:
        b = Memory(nc, ctx, "att")
        qA = [b.sb(f"q_hi_lo{k}", [P, 2, T], F32R) for k in KINDS]
        qB = [b.sb(f"q_hi_rows{k}", [P, 2, T], F32R) for k in KINDS]
        kA = [b.sb(f"k_hi_hi{k}", [P, KV_SETS[k], T], F32R) for k in KINDS]
        kB = [b.sb(f"k_lo_rows{k}", [P, KV_SETS[k], T], F32R) for k in KINDS]
        v = [b.sb(f"v{k}", [P, KV_SETS[k], NB, 3 * HD], F32R) for k in KINDS]
        z = b.sb("z", [HD, Z_SLOTS, CH])
        p_raw = b.sb("p_raw", [P, P_SLOTS, CH])
        p_hi = b.sb("p_hi", [P, P_SLOTS, CH], F32R)
        p_lo = b.sb("p_lo", [P, P_SLOTS, CH], F32R)
        recip = b.sb("recip", [HD, 2, CH])
        head = b.sb("head", [HD, 2, CH])
        gated = b.sb("gated", [HD, 2, CH])
        part_max = [b.sb(f"part_max{k}", [P, NB, (1, NC)[k]]) for k in KINDS]
        neg_m = [b.sb(f"neg_m{k}", [P, NB]) for k in KINDS]
        m_hi = [b.sb(f"m_hi{k}", [NB, P], F32R) for k in KINDS]
        m_lo = [b.sb(f"m_lo{k}", [NB, P], F32R) for k in KINDS]
        e_raw = b.sb("e_raw", [NB, P])
        e_hi = b.sb("e_hi", [NB, P], F32R)
        e_lo = b.sb("e_lo", [NB, P], F32R)
        e_one = b.sb("e_one", [P, P], F32R)
        sink = b.sb("sink", [P, NH])
        ident = b.sb("ident", [P, P])
        ident_b = b.sb("ident_b", [P, P], BF16)
        mask_t = b.sb("mask_t", [P, 4 * P], BF16)
        mask_r = b.sb("mask_r", [P, 2 * P], BF16)
        s_ps = b.ps("s_ps", [P, 2, CH])
        max_ps = b.ps("max_ps", [P, 2, CH])
        value_ps = [b.ps(f"value_ps{k}", [P, 2, CH]) for k in KINDS]

        sink_loaded = b.sem("sink_loaded")
        consts = b.sem("constants")
        filled = b.sem("ones_rows_filled")
        q_loaded = [[b.sem(f"q_loaded{k}_{i}") for i in range(2)] for k in KINDS]
        kv_loaded = [[b.sem(f"kv_loaded{k}_{i}") for i in range(KV_SETS[k])] for k in KINDS]
        z_loaded = [b.sem(f"z_loaded{i}") for i in range(Z_SLOTS)]
        set_free = [b.sem(f"set_free{k}") for k in KINDS]
        max_done = b.sem("max_scores_done")
        maxed = b.sem("max_taken")
        m_ready = b.sem("neg_max_ready")
        turned = b.sem("max_turned")
        m_split = b.sem("max_split")
        e_ready = b.sem("sink_exp_ready")
        m_stored = b.sem("max_rows_stored")
        m_rows = [b.sem(f"max_rows_loaded{k}") for k in KINDS]
        s_done = b.sem("scores_done")
        p_raw_ready = b.sem("p_raw_ready")
        p_hi_ready = b.sem("p_hi_ready")
        p_lo_ready = b.sem("p_lo_ready")
        values_done = b.sem("values_done")
        recip_ready = b.sem("recip_ready")
        bank_free = [b.sem(f"value_bank_free{k}") for k in KINDS]
        head_ready = b.sem("head_ready")
        gated_ready = b.sem("gated_ready")
        stored = [b.sem(f"gated_stored{i}") for i in range(2)]
        passed = b.sem("passed")
        ROWS = (4, 2)
        rows_before = [sum(ROWS[k] for (k, _), n in turn_no.items() if n < t) for t in range(TURNS + 1)]
        ROWS_ALL = rows_before[TURNS]

        made_all = []
        with nc.Block() as block:
            @block.sync
            def _(sp):
                sp.dma_start(sink[:], I["sinks"].to_broadcast([P, NH])).then_inc(sink_loaded, 16)
                sp.wait_ge(filled, 2 + 2)

                def load(j, kind, u):
                    h = UNROLLED * j + u
                    s = u % KV_SETS[kind]
                    sp.wait_ge(set_free[kind], h + (2 if kind == SLIDING and u == 0 else 1))
                    sp.sem_inc(passed, 1)
                    if kind == FORGETTING or u == 0:
                        kh = j if kind == SLIDING else h + KV
                        vcol = W + HD * j if kind == SLIDING else HD * h
                        sem = kv_loaded[kind][s]
                        for part in range(2):
                            sp.dma_start(f32(kA[kind][part * HD:(part + 1) * HD, s, :]),
                                         S["k"][0, bass.ds(kh, 1), :, :].rearrange("h d t -> (h d) t")).then_inc(sem, 16)
                            sp.dma_start(f32(v[kind][:, s, :, part * 2 * HD:part * 2 * HD + HD]),
                                         S["v"][part, :, bass.ds(vcol, HD)].rearrange("(n p) d -> p n d", p=P)).then_inc(sem, 16)
                        sp.dma_start(f32(kB[kind][0:HD, s, :]), S["k"][1, bass.ds(kh, 1), :, :].rearrange("h d t -> (h d) t")).then_inc(sem, 16)
                        sp.dma_start(f32(kB[kind][HD:HD + 2, s, :]),
                                     S["negc"][:, bass.ds(h + NH * kind, 1), :].rearrange("s h t -> s (h t)")).then_inc(sem, 16)
                    for part, (dst, row) in enumerate(((qA, 0), (qA, HD), (qB, 0))):
                        src = S["q"][part % 2, bass.ds(h + NH * kind, 1), :, :].rearrange("h d t -> (h d) t")
                        sp.dma_start(f32(dst[kind][row:row + HD, u % 2, :]), src).then_inc(q_loaded[kind][u % 2], 16)

                def max_rows(j, kind, u):
                    h = UNROLLED * j + u
                    t = turn_no[kind, u]
                    sp.wait_ge(m_split, j * ROWS_ALL + rows_before[t + 1])
                    made = [(m_hi[kind], m_lo[kind])] + ([(e_hi, e_lo)] if kind == SLIDING else [])
                    for which, pair in enumerate(made):
                        for part, src in enumerate(pair):
                            sp.dma_start(S["m"][part, bass.ds(h + NH * (kind + 2 * which), 1), :].rearrange("h (n p) -> (h n) p", p=P),
                                         f32(src[:])).then_inc(m_stored, 16)
                    sp.wait_ge(m_stored, (j * ROWS_ALL + rows_before[t + 1]) * 16)
                    sp.dma_start(f32(qB[kind][HD + 2:HD + 4, u % 2, :]),
                                 S["m"][:, bass.ds(h + NH * kind, 1), :].rearrange("s h t -> s (h t)")).then_inc(m_rows[kind], 16)
                    if kind == SLIDING:
                        sp.dma_start(f32(qB[kind][HD + 4:HD + 6, u % 2, :]), S["m"][:, bass.ds(h + 2 * NH, 1), :].rearrange("s h t -> s (h t)")).then_inc(m_rows[kind], 16)

                def row_of(j, kind, u):
                    return HD * (UNROLLED * j + u) + W * kind

                gates = list(fin_no)

                def load_z(j, k):
                    kind, u, c = gates[k]
                    sp.wait_ge(gated_ready, j * FINS + (k + 1))
                    sp.dma_start(z[:, k % Z_SLOTS, :], S["z"][bass.ds(row_of(j, kind, u), HD), c * CH:(c + 1) * CH]).then_inc(z_loaded[k % Z_SLOTS], 16)

                with sp.Fori(0, NH // UNROLLED) as j:
                    for step, *what in order:
                        if step == "load":
                            load(j, *what)
                        elif step == "turn":
                            max_rows(j, *what)
                            if turn_no[tuple(what)] == 1:
                                for k in range(2):
                                    load_z(j, k)
                        elif step == "gate":
                            kind, u, c = what
                            k = fin_no[kind, u, c]
                            if k + 2 < FINS:
                                load_z(j, k + 2)
                            sp.wait_ge(gated_ready, j * FINS + (k + 1 + Z_SLOTS))
                            sp.dma_start(S["za"][bass.ds(row_of(j, kind, u), HD), c * CH:(c + 1) * CH], gated[:, k % 2, :]).then_inc(stored[k % 2], 16)
                for i in range(2):
                    sp.wait_ge(stored[i], NH * NC * 16)

            @block.gpsimd
            def _(gp):
                made = [0]

                def const(instruction):
                    made[0] += 1
                    instruction.then_inc(consts, 1)
                    gp.wait_ge(consts, made[0])

                for kind in KINDS:
                    const(gp.memset(f32(v[kind][:, :, :, HD:2 * HD]), 1.0))
                const(gp.memset(ident[:], 0.0))
                const(gp.memset(mask_t[:, 0:P], MASKED))
                const(gp.memset(mask_t[:, P:3 * P], 0.0))
                const(gp.memset(mask_t[:, 3 * P:4 * P], MASKED))
                const(gp.memset(mask_r[:], 0.0))
                const(gp.memset(f32(e_one[HD:HD + 6, :]), 0.0))
                const(gp.memset(f32(e_one[HD:HD + 6, HD:P]), 1.0))
                const(gp.memset(f32(e_one[HD:HD + 4, :]), 0.0))
                const(gp.affine_select(out=ident[:], in_=ident[:], compare_op=ALU.not_equal, fill=1.0,
                                       base=0, pattern=[[-1, P]], channel_multiplier=1))
                const(gp.affine_select(out=mask_t[:, P:2 * P], in_=mask_t[:, P:2 * P], compare_op=ALU.is_ge, fill=MASKED,
                                       base=0, pattern=[[1, P]], channel_multiplier=-1))
                const(gp.affine_select(out=mask_t[:, 2 * P:3 * P], in_=mask_t[:, 2 * P:3 * P], compare_op=ALU.is_gt, fill=MASKED,
                                       base=0, pattern=[[-1, P]], channel_multiplier=1))
                const(gp.affine_select(out=mask_r[:, 0:P], in_=mask_r[:, 0:P], compare_op=ALU.is_gt, fill=MASKED,
                                       base=0, pattern=[[1, P]], channel_multiplier=-1))
                const(gp.affine_select(out=mask_r[:, P:2 * P], in_=mask_r[:, P:2 * P], compare_op=ALU.is_ge, fill=MASKED,
                                       base=0, pattern=[[-1, P]], channel_multiplier=1))
                const(gp.tensor_copy(ident_b[:], ident[:]))
                made_all.append(made[0])
                gp.sem_inc(gated_ready, Z_SLOTS)
                with gp.Fori(0, NH // UNROLLED) as j:
                    for step, *what in order:
                        if step == "score":
                            kind, u, c, n = what
                            _, off, width, _ = score_units(kind, c)[n]
                            no = score_no[kind, u, c, n]
                            cols = slice(off, off + width)
                            gp.wait_ge(p_hi_ready, j * SCORES + (no + 1 + 2))
                            gp.tensor_tensor(p_lo[:, no % P_SLOTS, cols], p_raw[:, no % P_SLOTS, cols], f32(p_hi[:, no % P_SLOTS, cols]),
                                             ALU.subtract).then_inc(p_lo_ready, 1)
                        elif step == "gate":
                            k = fin_no[tuple(what)]
                            gp.wait_ge(z_loaded[k % Z_SLOTS], (j * (FINS // Z_SLOTS) + (k // Z_SLOTS + 1)) * 16)
                            gp.wait_ge(head_ready, j * FINS + (k + 1))
                            if k >= 2:
                                gp.wait_ge(stored[k % 2], (j * (FINS // 2) + k // 2) * 16)
                            gp.tensor_tensor(gated[:, k % 2, :], head[:, k % 2, :], z[:, k % Z_SLOTS, :], ALU.mult).then_inc(gated_ready, 1)

            @block.tensor
            def _(pe):
                pe.sem_inc(values_done, P_SLOTS)
                pe.sem_inc(turned, TURNS)
                pe.wait_ge(consts, made_all[0])
                with pe.Fori(0, NH // UNROLLED) as j:
                    for step, *what in order:
                        if step == "max":
                            kind, u, n = what
                            s, sq = u % KV_SETS[kind], u % 2
                            i, k0, width, _, used, mask = UNITS[kind][n]
                            no = bank_no[kind, u, n]
                            if n == 0:
                                pe.wait_ge(q_loaded[kind][sq], (j * (UNROLLED // 2) + (u // 2 + 1)) * 48)
                                pe.wait_ge(kv_loaded[kind][s], (j + 1) * 96 if kind == SLIDING else (j * 2 + (u // 2 + 1)) * 96)
                            pe.wait_ge(maxed, j * BANKS + (no + 1))
                            blk, keys = slice(i * P, (i + 1) * P), slice(k0, k0 + width)
                            out = max_ps[:, no % 2, 0:width]
                            nc.tensor.matmul(out, qA[kind][:, sq, blk], kA[kind][:, s, keys], start=True, stop=False)
                            last = nc.tensor.matmul(out, qB[kind][0:HD + 2, sq, blk], kB[kind][0:HD + 2, s, keys], start=False, stop=not mask)
                            if mask:
                                last = nc.tensor.matmul(max_ps[:, no % 2, used - mask:used], ident_b[:], mask_r[:, 2 * P - mask:2 * P],
                                                        start=False, stop=True)
                            last.then_inc(max_done, 1)
                        elif step == "turn":
                            kind, u = what
                            t, no = turn_no[kind, u], bank_no[kind, u]
                            pe.wait_ge(m_ready, j * TURNS + (t + 1))
                            pe.wait_ge(maxed, j * BANKS + (no + 1))
                            nc.tensor.transpose(max_ps[0:NB, no % 2, 0:P], neg_m[kind][:], ident[:]).then_inc(turned, 1)
                        elif step == "score":
                            kind, u, c, n = what
                            s, sq = u % KV_SETS[kind], u % 2
                            blk, off, width, mask = score_units(kind, c)[n]
                            no = score_no[kind, u, c, n]
                            if c == 0 and n == 0:
                                pe.wait_ge(m_rows[kind], (UNROLLED * j + (u + 1)) * (ROWS[kind] // 2 * 16))
                            pe.wait_ge(p_hi_ready, j * SCORES + (no + 1))
                            keys = slice(blk * P, (blk + 1) * P)
                            qry = slice(c * CH + off, c * CH + off + width)
                            out = s_ps[:, no % 2, off:off + width]
                            nc.tensor.matmul(out, kA[kind][:, s, keys], qA[kind][:, sq, qry], start=True, stop=False)
                            last = nc.tensor.matmul(out, kB[kind][0:HD + 4, s, keys], qB[kind][0:HD + 4, sq, qry], start=False, stop=mask is None)
                            if mask is not None:
                                last = nc.tensor.matmul(s_ps[:, no % 2, off:off + mask.stop - mask.start], ident_b[:], mask_t[:, mask],
                                                        start=False, stop=True)
                            last.then_inc(s_done, 1)
                        elif step == "value":
                            kind, u, c, n = what
                            s = u % KV_SETS[kind]
                            blk, off, width, _ = score_units(kind, c)[n]
                            no = score_no[kind, u, c, n]
                            bank = value_ps[kind][:, c % 2, :]
                            opens = n == 0
                            if opens:
                                pe.wait_ge(bank_free[kind], (UNROLLED * j + u) * NC + (c + 1))
                                if kind == SLIDING:
                                    nc.tensor.matmul(bank, e_one[HD:HD + 6, :], qB[kind][HD:HD + 6, u % 2, c * CH:(c + 1) * CH], start=True, stop=False)
                                    opens = False
                            pe.wait_ge(p_lo_ready, j * SCORES + (no + 1))
                            out = bank[:, off:off + width]
                            ones_v, lo_v = v[kind][:, s, blk, 0:2 * HD], v[kind][:, s, blk, 2 * HD:3 * HD]
                            hi, lo = p_hi[:, no % P_SLOTS, off:off + width], p_lo[:, no % P_SLOTS, off:off + width]
                            nc.tensor.matmul(out, ones_v, hi, start=opens, stop=False)
                            nc.tensor.matmul(out[0:HD, :], lo_v, hi, start=False, stop=False)
                            nc.tensor.matmul(out, ones_v, lo, start=False, stop=n == len(score_units(kind, c)) - 1).then_inc(values_done, 1)

            @block.scalar
            def _(act):
                act.sem_inc(p_hi_ready, 2)
                act.wait_ge(sink_loaded, 16)
                with act.Fori(0, NH // UNROLLED) as j:
                    for step, *what in order:
                        if step == "turn" and what[0] == SLIDING:
                            u = what[1]
                            act.wait_ge(turned, j * TURNS + (turn_no[SLIDING, u] + 1 + TURNS))
                            nc.scalar.activation(e_raw[:], max_ps[0:NB, bank_no[SLIDING, u] % 2, 0:P], ACT.Exp, bias=sink[0:NB, bass.ds(UNROLLED * j + u, 1)]).then_inc(e_ready, 1)
                        elif step == "score":
                            kind, u, c, n = what
                            _, off, width, _ = score_units(kind, c)[n]
                            no = score_no[kind, u, c, n]
                            cols = slice(off, off + width)
                            act.wait_ge(s_done, j * SCORES + (no + 1))
                            act.wait_ge(values_done, j * SCORES + (no + 1))
                            nc.scalar.activation(p_raw[:, no % P_SLOTS, cols], s_ps[:, no % 2, cols], ACT.Exp).then_inc(p_raw_ready, 1)
                            nc.scalar.activation(p_hi[:, no % P_SLOTS, cols], s_ps[:, no % 2, cols], ACT.Exp).then_inc(p_hi_ready, 1)

            @block.vector
            def _(dv):
                dv.sem_inc(maxed, 2)
                for kind in KINDS:
                    dv.sem_inc(set_free[kind], 2)
                    dv.sem_inc(bank_free[kind], 2)
                    nc.vector.memset(f32(kB[kind][HD:HD + 32, :, :]), 1.0).then_inc(filled, 1)
                    nc.vector.memset(f32(qB[kind][HD:HD + 32, :, :]), 1.0).then_inc(filled, 1)
                nc.vector.memset(part_max[FORGETTING][:], MASKED).then_inc(filled, 1)
                dv.wait_ge(filled, 5)
                dv.wait_ge(sink_loaded, 16)
                with dv.Fori(0, NH // UNROLLED) as j:
                    for step, *what in order:
                        if step == "max":
                            kind, u, n = what
                            i, _, _, col, used, _ = UNITS[kind][n]
                            no = bank_no[kind, u, n]
                            if n == 0:
                                before = turn_no[kind, u - 1] + TURNS if u else turn_no[kind, UNROLLED - 1]
                                dv.wait_ge(turned, j * TURNS + (before + 1))
                            dv.wait_ge(max_done, j * MAXES + (max_no[kind, u, n] + 1))
                            nc.vector.reduce_max(part_max[kind][:, i, col:col + 1], max_ps[:, no % 2, 0:used], AX.X).then_inc(maxed, 1)
                            if n == len(UNITS[kind]) - 1:
                                dv.wait_ge(maxed, j * BANKS + (no + 1 + 2))
                                if kind == SLIDING:
                                    nc.vector.tensor_scalar(neg_m[kind][:], part_max[kind][:, :, 0], sink[:, bass.ds(UNROLLED * j + u, 1)], -1.0,
                                                            ALU.max, ALU.mult).then_inc(m_ready, 1)
                                else:
                                    nc.vector.reduce_max(neg_m[kind][:], part_max[kind][:], AX.X, negate=True).then_inc(m_ready, 1)
                        elif step == "turn":
                            kind, u = what
                            t = turn_no[kind, u]
                            row = max_ps[0:NB, bank_no[kind, u] % 2, 0:P]
                            if kind == SLIDING:
                                dv.wait_ge(e_ready, UNROLLED * j + (u + 1))
                            else:
                                dv.wait_ge(turned, j * TURNS + (t + 1 + TURNS))
                            if t:
                                dv.wait_ge(m_stored, (j * ROWS_ALL + rows_before[t]) * 16)
                            nc.vector.tensor_copy(m_hi[kind][:], row).then_inc(m_split, 1)
                            dv.wait_ge(m_split, j * ROWS_ALL + (rows_before[t] + 1))
                            nc.vector.tensor_tensor(m_lo[kind][:], row, f32(m_hi[kind][:]), ALU.subtract).then_inc(m_split, 1)
                            if kind == SLIDING:
                                nc.vector.tensor_copy(e_hi[:], e_raw[:]).then_inc(m_split, 1)
                                dv.wait_ge(m_split, j * ROWS_ALL + (rows_before[t] + 3))
                                nc.vector.tensor_tensor(e_lo[:], e_raw[:], f32(e_hi[:]), ALU.subtract).then_inc(m_split, 1)
                            dv.wait_ge(m_split, j * ROWS_ALL + rows_before[t + 1])
                            dv.sem_inc(maxed, 1)
                        elif step == "recip":
                            kind, u, c, part = what
                            bank = value_ps[kind][:, c % 2, :]
                            if part == 0:
                                dv.wait_ge(values_done, j * SCORES + (last_score(kind, u, c) + 1 + P_SLOTS))
                            cols = slice(part * CH // RECIP_PARTS, (part + 1) * CH // RECIP_PARTS)
                            nc.vector.reciprocal(recip[:, fin_no[kind, u, c] % 2, cols], bank[HD:P, cols]).then_inc(recip_ready, 1)
                        elif step == "fin":
                            kind, u, c = what
                            k = fin_no[kind, u, c]
                            bank = value_ps[kind][:, c % 2, :]
                            dv.wait_ge(recip_ready, j * FINS * RECIP_PARTS + (recip_no[kind, u, c, RECIP_PARTS - 1] + 1))
                            dv.wait_ge(gated_ready, j * FINS + (k - 1 + Z_SLOTS))
                            nc.vector.tensor_tensor(head[:, k % 2, :], bank[0:HD, :], recip[:, k % 2, :], ALU.mult).then_inc(head_ready, 1)
                            dv.wait_ge(head_ready, j * FINS + (k + 1))
                            dv.sem_inc(bank_free[kind], 1)
                            if c == NC - 1:
                                dv.sem_inc(set_free[kind], 1)


def residual_gate(nc, I, gate_row):
    with ExitStack() as ctx:
        b = Memory(nc, ctx, "rg")
        cond = b.sb("cond", [P, KT])
        cond_bc = b.sb("cond_bc", [P, KT, P])
        w_gate = b.sb("w_gate", [P, KT, D])
        b_gate = b.sb("b_gate", [P, D])
        gate_ps = b.ps("gate_ps", [P, 2, CH])
        loaded = b.sem("loaded")
        w_loaded = b.sem("w_loaded")
        ready = b.sem("cond_ready")
        done = b.sem("gate_done")
        added = b.sem("gate_added")
        with nc.Block() as block:
            @block.sync
            def _(sp):
                sp.dma_start(cond[:], I["c"].rearrange("o (k p) -> p (o k)", p=P), allow_slow_non_contiguous=True).then_inc(loaded, 16)
                sp.dma_start(b_gate[:], I["b_ada"][:, 2 * D:3 * D].to_broadcast([P, D])).then_inc(loaded, 16)
                sp.dma_start(w_gate[:], I["w_ada"][0, :, 2 * D:3 * D].rearrange("(k p) n -> p k n", p=P)).then_inc(w_loaded, 16)

            @block.tensor
            def _(pe):
                pe.wait_ge(ready, 1)
                pe.wait_ge(w_loaded, 16)
                for half in range(2):
                    for k in range(KT):
                        last = nc.tensor.matmul(gate_ps[:, half, :], cond_bc[:, k, :], w_gate[:, k, half * CH:(half + 1) * CH],
                                                start=(k == 0), stop=(k == KT - 1))
                    last.then_inc(done, 1)

            @block.vector
            def _(dv):
                dv.wait_ge(loaded, 32)
                nc.vector.tensor_copy(cond_bc[:], cond[:].unsqueeze(2).to_broadcast([P, KT, P])).then_inc(ready, 1)
                for half in range(2):
                    dv.wait_ge(done, half + 1)
                    cols = slice(half * CH, (half + 1) * CH)
                    nc.vector.tensor_tensor(gate_row[:, cols], gate_ps[:, half, :], b_gate[:, cols], ALU.add).then_inc(added, 1)


def merge(nc, I, S):
    with ExitStack() as ctx:
        b = Memory(nc, ctx, "merge")
        a_raw = b.sb("a_raw", [P, KT, CH])
        a_hi = b.sb("a_hi", [P, KT, T], F32R)
        a_lo = b.sb("a_lo", [P, KT, T], F32R)
        w_raw = b.sb("w_raw", [P, 2, KT, P])
        w_hi = b.sb("w_hi", [P, 2, KT, P], F32R)
        w_lo = b.sb("w_lo", [P, 2, KT, P], F32R)
        gates = b.sb("gates", [P, 2, 2, CH])
        part = b.sb("part", [P, 2, CH])
        merged = b.sb("merged", [P, 2, CH])
        out_ps = b.ps("out_ps", [P, NC, 2, CH])
        passed = b.sem("passed")
        a_loaded = b.sem("a_loaded")
        a_hi_ready = b.sem("a_hi_ready")
        a_ready = b.sem("a_ready")
        w_loaded = [b.sem(f"w_loaded{i}") for i in range(2)]
        w_hi_ready = b.sem("w_hi_ready")
        w_ready = b.sem("w_ready")
        g_loaded = [b.sem(f"g_loaded{i}") for i in range(2)]
        chunk_done = b.sem("chunk_done")
        gated = b.sem("gated")
        merged_ready = b.sem("merged_ready")
        stored = [b.sem(f"stored{i}") for i in range(2)]
        TILES = D // P
        with nc.Block() as block:
            @block.sync
            def _(sp):
                def emit(n, par):
                    sp.wait_ge(w_ready, n + 1)
                    for half, w in enumerate(("w_o_swa", "w_o_fox")):
                        sp.dma_start(w_raw[:, par, 4 * half:4 * half + 4, :],
                                     I[w][0, :, bass.ds(n * P, P)].rearrange("(k p) c -> p k c", p=P)).then_inc(w_loaded[par], 16)
                    for c in range(NC):
                        sp.wait_ge(gated, n * NC + (c + 1))
                        for half in range(2):
                            sp.dma_start(gates[:, c % 2, half, :], S["g"][bass.ds(n * P + half * D, P), c * CH:(c + 1) * CH]).then_inc(g_loaded[c % 2], 16)
                for c in range(NC):
                    if c:
                        sp.wait_ge(a_ready, c)
                    sp.dma_start(a_raw[:], S["za"][:, c * CH:(c + 1) * CH].rearrange("(k p) t -> p k t", p=P)).then_inc(a_loaded, 16)
                with sp.Fori(0, TILES // 2) as i:
                    for par in range(2):
                        emit(2 * i + par, par)

            @block.gpsimd
            def _(gp):
                gp.sem_inc(w_ready, 2)
                with gp.Fori(0, TILES // 2) as i:
                    for par in range(2):
                        n = 2 * i + par
                        gp.wait_ge(w_loaded[par], (i + 1) * 32)
                        gp.wait_ge(chunk_done, n * NC)
                        gp.sem_inc(passed, 1)
                        gp.tensor_copy(w_hi[:, par], w_raw[:, par]).then_inc(w_hi_ready, 1)
                        gp.wait_ge(w_hi_ready, n + 1)
                        gp.tensor_tensor(w_lo[:, par], w_raw[:, par], f32(w_hi[:, par]), ALU.subtract).then_inc(w_ready, 1)

            @block.tensor
            def _(pe):
                pe.sem_inc(chunk_done, NC)
                with pe.Fori(0, TILES // 2) as i:
                    for par in range(2):
                        n = 2 * i + par
                        pe.wait_ge(w_ready, n + 3)
                        for c in range(NC):
                            tok = slice(c * CH, (c + 1) * CH)
                            pe.wait_ge(a_ready, c + 1)
                            pe.wait_ge(merged_ready, n * NC + (c + 1))
                            for k in range(KT):
                                out = out_ps[:, c, k // 4, :]
                                nc.tensor.matmul(out, w_hi[:, par, k, :], a_hi[:, k, tok], start=(k % 4 == 0), stop=False)
                                nc.tensor.matmul(out, w_hi[:, par, k, :], a_lo[:, k, tok], start=False, stop=False)
                                last = nc.tensor.matmul(out, w_lo[:, par, k, :], a_hi[:, k, tok], start=False, stop=(k % 4 == 3))
                            last.then_inc(chunk_done, 1)

            @block.scalar
            def _(act):
                for c in range(NC):
                    act.wait_ge(a_loaded, 16 * (c + 1))
                    nc.scalar.activation(a_hi[:, :, c * CH:(c + 1) * CH], a_raw[:], ACT.Copy).then_inc(a_hi_ready, 1)
                with act.Fori(0, TILES // 2) as i:
                    for par in range(2):
                        n = 2 * i + par
                        for c in range(NC):
                            act.wait_ge(merged_ready, n * NC + (c + 1 + NC))
                            act.dma_start(S["mg"][bass.ds(n * P, P), c * CH:(c + 1) * CH], merged[:, c % 2, :]).then_inc(stored[c % 2], 16)
                for c in range(2):
                    act.wait_ge(stored[c], TILES * NC // 2 * 16)

            @block.vector
            def _(dv):
                dv.sem_inc(gated, 2)
                dv.sem_inc(merged_ready, NC)
                for c in range(NC):
                    dv.wait_ge(a_hi_ready, c + 1)
                    nc.vector.tensor_tensor(a_lo[:, :, c * CH:(c + 1) * CH], a_raw[:], f32(a_hi[:, :, c * CH:(c + 1) * CH]),
                                            ALU.subtract).then_inc(a_ready, 1)
                with dv.Fori(0, TILES // 2) as i:
                    for par in range(2):
                        n = 2 * i + par
                        for c in range(NC):
                            dv.wait_ge(chunk_done, n * NC + (c + 1 + NC))
                            dv.wait_ge(g_loaded[c % 2], (n * 2 + (c // 2 + 1)) * 32)
                            for half in range(2):
                                last = nc.vector.tensor_tensor(part[:, half, :], out_ps[:, c, half, :], gates[:, c % 2, half, :], ALU.mult)
                            last.then_inc(gated, 1)
                            dv.wait_ge(gated, n * NC + (c + 3))
                            dv.wait_ge(stored[c % 2], (n * 2 + c // 2) * 16)
                            nc.vector.tensor_tensor(merged[:, c % 2, :], part[:, 0, :], part[:, 1, :], ALU.add).then_inc(merged_ready, 1)
                            dv.wait_ge(merged_ready, n * NC + (c + 1 + NC))


def finish(nc, I, S, gate_row, out):
    with ExitStack() as ctx:
        b = Memory(nc, ctx, "fin")
        w_raw = b.sb("w_raw", [P, 2, D])
        w_hi = b.sb("w_hi", [P, KT, D], F32R)
        w_lo = b.sb("w_lo", [P, KT, D], F32R)
        m_raw = b.sb("m_raw", [P, 2, KT, P])
        m_hi = b.sb("m_hi", [P, 2, KT, P], F32R)
        m_lo = b.sb("m_lo", [P, 2, KT, P], F32R)
        x_t = b.sb("x_t", [P, 2, D])
        res = b.sb("res", [P, 2, D])
        square = b.sb("square", [P, D])
        out_t = b.sb("out_t", [P, 2, D])
        g_row = b.sb("g_row", [P, D])
        ss = b.sb("ss", [P, 2])
        var = b.sb("var", [P, 2])
        inv = b.sb("inv", [P, 2])
        root = b.sb("root", [P, 2])
        fix = b.sb("fix", [P, 1])
        rstd = b.sb("rstd", [P, 1])
        out_ps = b.ps("out_ps", [P, 2, 2, CH])
        w_loaded = [b.sem(f"w_loaded{i}") for i in range(2)]
        w_hi_ready = b.sem("w_hi_ready")
        w_ready = b.sem("w_ready")
        small = b.sem("small_loaded")
        m_loaded = [b.sem(f"m_loaded{i}") for i in range(2)]
        x_loaded = [b.sem(f"x_loaded{i}") for i in range(2)]
        m_hi_ready = b.sem("m_hi_ready")
        m_ready = b.sem("m_ready")
        done = b.sem("products_done")
        scaled = b.sem("scaled")
        res_ready = b.sem("res_ready")
        summed = b.sem("summed")
        inverted = b.sem("inverted")
        rooted = b.sem("rooted")
        steps = b.sem("newton_steps")
        out_ready = b.sem("out_ready")
        stored = [b.sem(f"stored{i}") for i in range(2)]
        NEWTON = 5
        with nc.Block() as block:
            @block.sync
            def _(sp):
                sp.dma_start(g_row[:], I["g_final"].rearrange("(a n) -> a n", a=1).to_broadcast([P, D])).then_inc(small, 16)
                for k in range(KT):
                    if k >= 2:
                        sp.wait_ge(w_ready, k - 1)
                    sp.dma_start(w_raw[:, k % 2, :], I["w_out"][0, k * P:(k + 1) * P, :]).then_inc(w_loaded[k % 2], 16)
                with sp.Fori(0, NB // 2) as i:
                    for par in range(2):
                        n = 2 * i + par
                        sp.wait_ge(m_ready, n + 1)
                        sp.dma_start(m_raw[:, par], S["mg"][:, bass.ds(n * P, P)].rearrange("(k p) t -> p k t", p=P)).then_inc(m_loaded[par], 16)
                        sp.wait_ge(res_ready, n + 1)
                        sp.dma_start(x_t[:, par, :], I["x"][0, bass.ds(n * P, P), :]).then_inc(x_loaded[par], 16)

            @block.gpsimd
            def _(gp):
                for k in range(KT):
                    gp.wait_ge(w_loaded[k % 2], 16 * (k // 2 + 1))
                    gp.tensor_copy(w_hi[:, k, :], w_raw[:, k % 2, :]).then_inc(w_hi_ready, 1)
                    gp.wait_ge(w_hi_ready, k + 1)
                    gp.tensor_tensor(w_lo[:, k, :], w_raw[:, k % 2, :], f32(w_hi[:, k, :]), ALU.subtract).then_inc(w_ready, 1)

            @block.tensor
            def _(pe):
                pe.sem_inc(done, 2)
                pe.wait_ge(w_ready, KT)
                with pe.Fori(0, NB // 2) as i:
                    for par in range(2):
                        n = 2 * i + par
                        pe.wait_ge(m_ready, n + 3)
                        pe.wait_ge(scaled, n + 1)
                        for half in range(2):
                            cols = slice(half * CH, (half + 1) * CH)
                            o = out_ps[:, par, half, :]
                            for k in range(KT):
                                nc.tensor.matmul(o, m_hi[:, par, k, :], w_hi[:, k, cols], start=(k == 0), stop=False)
                                nc.tensor.matmul(o, m_hi[:, par, k, :], w_lo[:, k, cols], start=False, stop=False)
                                last = nc.tensor.matmul(o, m_lo[:, par, k, :], w_hi[:, k, cols], start=False, stop=(k == KT - 1))
                        last.then_inc(done, 1)

            @block.scalar
            def _(act):
                def split(n, par):
                    act.wait_ge(m_loaded[par], (n - par) * 8 + 16)
                    act.wait_ge(done, n + 1)
                    nc.scalar.activation(m_hi[:, par], m_raw[:, par], ACT.Copy).then_inc(m_hi_ready, 1)

                def norm(n, par):
                    act.wait_ge(res_ready, n + 3)
                    nc.scalar.activation(square[:], res[:, par, :], ACT.Square, accum_out=ss[:, par:par + 1]).then_inc(summed, 1)
                    act.wait_ge(inverted, n + 1)
                    nc.scalar.activation(root[:, par:par + 1], inv[:, par:par + 1], ACT.Sqrt).then_inc(rooted, 1)
                    act.wait_ge(out_ready, n + 1)
                    act.dma_start(out[0, bass.ds(n * P, P), :], out_t[:, par, :]).then_inc(stored[par], 16)

                split(0, 0)
                with act.Fori(0, NB // 2 - 1) as i:
                    for par in range(2):
                        split(2 * i + (par + 1), 1 - par)
                        norm(2 * i + par, par)
                split(NB - 1, 1)
                norm(NB - 2, 0)
                norm(NB - 1, 1)
                for par in range(2):
                    act.wait_ge(stored[par], NB // 2 * 16)

            @block.vector
            def _(dv):
                dv.sem_inc(m_ready, 2)
                dv.sem_inc(res_ready, 2)
                dv.sem_inc(scaled, 2)

                def split(n, par):
                    dv.wait_ge(m_hi_ready, n + 1)
                    nc.vector.tensor_tensor(m_lo[:, par], m_raw[:, par], f32(m_hi[:, par]), ALU.subtract).then_inc(m_ready, 1)

                def norm(n, par):
                    r = res[:, par, :]
                    dv.wait_ge(done, n + 3)
                    dv.wait_ge(out_ready, n)
                    nc.vector.tensor_tensor(r, out_ps[:, par, :, :].rearrange("p a b -> p (a b)"), gate_row[:], ALU.mult).then_inc(scaled, 1)
                    dv.wait_ge(scaled, n + 3)
                    dv.wait_ge(x_loaded[par], (n - par) * 8 + 16)
                    nc.vector.tensor_tensor(r, r, x_t[:, par, :], ALU.add).then_inc(res_ready, 1)
                    dv.wait_ge(summed, n + 1)
                    v, y = var[:, par:par + 1], root[:, par:par + 1]
                    nc.vector.tensor_scalar(v, ss[:, par:par + 1], 1.0 / D, EPS, ALU.mult, ALU.add).then_inc(steps, 1)
                    dv.wait_ge(steps, n * NEWTON + 1)
                    nc.vector.reciprocal(inv[:, par:par + 1], v).then_inc(inverted, 1)
                    dv.wait_ge(rooted, n + 1)
                    nc.vector.tensor_tensor(fix[:], y, y, ALU.mult).then_inc(steps, 1)
                    dv.wait_ge(steps, n * NEWTON + 2)
                    nc.vector.tensor_tensor(fix[:], fix[:], v, ALU.mult).then_inc(steps, 1)
                    dv.wait_ge(steps, n * NEWTON + 3)
                    nc.vector.tensor_scalar(fix[:], fix[:], -0.5, 1.5, ALU.mult, ALU.add).then_inc(steps, 1)
                    dv.wait_ge(steps, n * NEWTON + 4)
                    nc.vector.tensor_tensor(rstd[:], y, fix[:], ALU.mult).then_inc(steps, 1)
                    dv.wait_ge(steps, n * NEWTON + 5)
                    dv.wait_ge(stored[par], (n - par) * 8)
                    nc.vector.scalar_tensor_tensor(out_t[:, par, :], r, rstd[:, 0:1], g_row[:], ALU.mult, ALU.mult).then_inc(out_ready, 1)
                    dv.wait_ge(out_ready, n + 1)

                dv.wait_ge(small, 16)
                split(0, 0)
                with dv.Fori(0, NB // 2 - 1) as i:
                    for par in range(2):
                        split(2 * i + (par + 1), 1 - par)
                        norm(2 * i + par, par)
                split(NB - 1, 1)
                norm(NB - 2, 0)
                norm(NB - 1, 1)


_INS = ["x", "c", "positions", "w_ada", "b_ada", "g_norm", "w_in", "b_f", "sinks", "w_o_swa", "w_o_fox", "w_out", "g_final"]


def build(nc, I, out, upto=9):
    S = {
        "q": nc.dram_tensor("q_parts", (2, 2 * NH, HD, T), F32).ap(),
        "k": nc.dram_tensor("k_parts", (2, KV + NH, HD, T), F32).ap(),
        "v": nc.dram_tensor("v_parts", (2, T, VW), F32).ap(),
        "negc": nc.dram_tensor("negc_parts", (2, 2 * NH, T), F32).ap(),
        "m": nc.dram_tensor("m_parts", (2, 3 * NH, T), F32).ap(),
        "z": nc.dram_tensor("z_silu", (2 * W, T), F32).ap(),
        "g": nc.dram_tensor("sigmoid_gates", (2 * D, T), F32).ap(),
        "za": nc.dram_tensor("gated_heads", (2 * W, T), F32).ap(),
        "mg": nc.dram_tensor("merged", (D, T), F32).ap(),
    }
    with ExitStack() as ctx:
        keep = Memory(nc, ctx, "h")
        hT_hi = keep.sb("hT_hi", [P, KT, T], F32R)
        hT_lo = keep.sb("hT_lo", [P, KT, T], F32R)
        prepare_and_values(nc, I, S, hT_hi, hT_lo)
        if upto >= 2:
            project(nc, I, S, hT_hi, hT_lo)
    if upto >= 3:
        with ExitStack() as ctx:
            attend(nc, I, S)
            if upto >= 4:
                gate_row = Memory(nc, ctx, "gate").sb("row", [P, D])
                residual_gate(nc, I, gate_row)
                merge(nc, I, S)
                finish(nc, I, S, gate_row, out)


def kernel(**inputs):
    import numpy as _np
    import concourse.bacc as _bacc
    from concourse import mybir as _mybir
    from concourse.bass_utils import run_bass_kernel_spmd as _run

    nc = _bacc.Bacc("TRN2", target_bir_lowering=False, num_devices=1)
    arrays = {name: _np.ascontiguousarray(inputs[name]) for name in _INS}
    freq = _np.float64(10000.0) ** (-_np.arange(0, HD, 2, dtype=_np.float64) / HD)
    arrays["inv_freq"] = _np.tile(freq.astype(_np.float32), 4).reshape(P, 1)
    I = {n: nc.dram_tensor(f"in_{n}", a.shape, _mybir.dt.from_np(a.dtype), kind="ExternalInput").ap() for n, a in arrays.items()}
    out = nc.dram_tensor("out_0", (1, T, D), _mybir.dt.float32, kind="ExternalOutput").ap()
    build(nc, I, out)
    r = _run(nc, [{f"in_{n}": a for n, a in arrays.items()}], core_ids=[0])
    return r.results[0]["out_0"]
```

```python
from contextlib import ExitStack

import concourse.bass as bass
from concourse import mybir

ALU = mybir.AluOpType
ACT = mybir.ActivationFunctionType
AX = mybir.AxisListType
F32 = mybir.dt.float32
F32R = mybir.dt.float32r
BF16 = mybir.dt.bfloat16
I32 = mybir.dt.int32

P = 128
T = 2048
D = 1024
KT = D // P
HD = 64
NH = 8
W = NH * HD
KV = 2
GROUP = NH // KV
NB = T // P
CH = 512
NC = T // CH
SCALE = HD ** -0.5
EPS = 1e-6
MASKED = -1e30

QA0 = 0
KA0 = QA0 + W
VA0 = KA0 + KV * HD
ZA0 = VA0 + KV * HD
QB0 = ZA0 + W
KB0 = QB0 + W
VB0 = KB0 + W
FB0 = VB0 + W
ZB0 = FB0 + NH
GA0 = ZB0 + W

VW = W + KV * HD
VF = VW + NH
VN = VF // 2

TWO_PI = 6.283185307179586
COARSE = 4096.0


def parts_of(value, bits, count):
    import math
    out = []
    for _ in range(count):
        e = math.floor(math.log2(value)) + 1 - bits if value > 0 else 0
        part = math.floor(value / 2.0 ** e) * 2.0 ** e
        out.append(part)
        value -= part
    return out


def f32(ap):
    return ap.bitcast(F32)


class Memory:

    def __init__(self, nc, ctx, stage):
        self.nc, self.ctx, self.stage = nc, ctx, stage

    def sb(self, name, shape, dt=F32):
        return self.ctx.enter_context(self.nc.sbuf_tensor(f"{self.stage}_{name}", shape, dt))

    def ps(self, name, shape, dt=F32):
        return self.ctx.enter_context(self.nc.psum_tensor(f"{self.stage}_{name}", shape, dt))

    def sem(self, name):
        return self.ctx.enter_context(self.nc.semaphore(f"{self.stage}_{name}"))


def chain(eng, sem):
    count = [0]

    def step(instruction):
        count[0] += 1
        instruction.then_inc(sem, 1)
        eng.wait_ge(sem, count[0])
    return step


def prepare_and_values(nc, I, S, hT_hi, hT_lo):
    RING = 4
    ring = [("w", u) for u in range(14)] + [("x", 0), ("w", 14), ("w", 15)] + [("x", n) for n in range(1, NB)]
    ring += [("g", k) for k in range(KT)]
    slot = {item: at % RING for at, item in enumerate(ring)}
    loads = {item: at // RING + 1 for at, item in enumerate(ring)}
    with ExitStack() as ctx:
        b = Memory(nc, ctx, "prep")
        cond = b.sb("cond", [P, KT])
        bias_cols = b.sb("bias_cols", [P, 2 * KT])
        g_col = b.sb("g_col", [P, KT])
        gain = b.sb("gain", [P, KT])
        shift = b.sb("shift", [P, KT])
        ada_cols = b.sb("ada_cols", [P, 2 * KT])
        ident = b.sb("ident", [P, P])
        sums = b.sb("sums", [P, NB])
        rstd = b.sb("rstd", [P, NB])
        vv = b.sb("vv", [P, NB])
        tmp = b.sb("tmp", [P, NB])
        forget = b.sb("forget", [P, NB, NH])
        ring_sb = b.sb("ring", [P, RING, D])
        h_raw = b.sb("h_raw", [P, KT, P])
        w_raw = b.sb("w_raw", [P, 2, VF])
        w_hi = b.sb("w_hi", [P, KT, VF], F32R)
        w_lo = b.sb("w_lo", [P, KT, VF], F32R)
        v_hi = b.sb("v_hi", [P, 2, VN], F32R)
        v_lo = b.sb("v_lo", [P, 2, VN], F32R)
        bf_row = b.sb("bf_row", [P, NH])
        upper = b.sb("upper", [P, P])
        ones = b.sb("ones", [P, P])
        e_neg = b.sb("e_neg", [P, NB, NH])
        one_e = b.sb("one_e", [P, NB, NH])
        ln_e = b.sb("ln_e", [P, NB, NH])
        flat = b.sb("flat", [P, NB, NH])
        cum = b.sb("cum", [P, NH, NB])
        c_hi = b.sb("c_hi", [P, P], F32R)
        c_lo = b.sb("c_lo", [P, P], F32R)
        gate = h_raw[0:1].rearrange("p k c -> p (k c)")
        inv = b.sb("inv", [P, 1])
        pos_i = b.sb("pos_i", [P, CH], I32)
        table = h_raw[:].rearrange("p (a k) c -> p a (k c)", a=2)
        turns = f32(v_hi[:].rearrange("p h c -> p (h c)")[:, 0:CH])
        turns_i = v_lo[:].rearrange("p h c -> p (h c)")[:, 0:CH].bitcast(I32)
        square = b.ps("square", [P, D])
        turned = b.ps("turned", [P, 2, 4, P])
        out_ps = b.ps("out_ps", [P, 2, CH])
        ada_ps = b.ps("ada_ps", [P, CH])
        row_ps = b.ps("row_ps", [P, CH])

        ada_rows = (turned[0:1].rearrange("p h j c -> p h (j c)"), out_ps[0:1])
        ada_row = h_raw[0:1].rearrange("p k c -> p (k c)")

        small = b.sem("small_loaded")
        row_copied = b.sem("ada_row_copied")
        row_turned = b.sem("ada_row_turned")
        pos_loaded = b.sem("positions_loaded")
        ring_loaded = [b.sem(f"ring_loaded{i}") for i in range(RING)]
        wv_loaded = [b.sem(f"wv_loaded{i}") for i in range(2)]
        w_used = b.sem("w_ada_used")
        wg_used = b.sem("w_gate_used")
        gate_loaded = b.sem("gate_bias_loaded")
        gate_ready = b.sem("gate_ready")
        gate_stored = b.sem("gate_stored")
        summed = b.sem("squares_summed")
        dve = b.sem("dve_steps")
        inverted = b.sem("inverted")
        rooted = b.sem("rooted")
        xn_ready = b.sem("xn_ready")
        half_turned = b.sem("half_turned")
        raw_half = b.sem("raw_half_ready")
        h_hi_ready = b.sem("h_hi_ready")
        h_lo_ready = b.sem("h_lo_ready")
        wv_hi_ready = b.sem("wv_hi_ready")
        wv_split = b.sem("wv_split")
        done = b.sem("products_done")
        v_hi_ready = b.sem("v_hi_ready")
        v_lo_ready = b.sem("v_lo_ready")
        v_stored = [b.sem(f"v_stored{i}") for i in range(2)]
        consts = b.sem("constants")
        angle_ready = b.sem("angle_ready")
        sined = b.sem("sines_done")
        tab_stored = b.sem("tables_stored")
        logit_ready = b.sem("logit_ready")
        e_ready = b.sem("e_ready")
        one_ready = b.sem("one_ready")
        ln_ready = b.sem("ln_ready")
        logf_ready = b.sem("logf_ready")
        sums_ready = b.sem("sums_ready")
        cum_ready = b.sem("cum_ready")
        rows_ready = b.sem("rows_ready")
        rows_split = b.sem("rows_split")
        rows_stored = b.sem("rows_stored")
        zeros_stored = b.sem("zeros_stored")
        coarse = parts_of(TWO_PI * COARSE, 7, 8)
        fine = parts_of(TWO_PI, 10, 5)

        with nc.Block() as block:
            @block.sync
            def _(sp):
                sp.dma_start(inv[:], I["inv_freq"]).then_inc(pos_loaded, 16)
                for q in range(NC):
                    sp.dma_start(pos_i[32 * q:32 * q + 32, :], I["positions"][:, q * CH:(q + 1) * CH].to_broadcast([32, CH])).then_inc(pos_loaded, 16)
                sp.dma_start(cond[:], I["c"].rearrange("o (k p) -> p (o k)", p=P), allow_slow_non_contiguous=True).then_inc(small, 16)
                sp.dma_start(bias_cols[:], I["b_ada"][0, 0:2 * D].rearrange("(k p) -> p k", p=P), allow_slow_non_contiguous=True).then_inc(small, 16)
                sp.dma_start(g_col[:], I["g_norm"][0, :].rearrange("(k p) -> p k", p=P), allow_slow_non_contiguous=True).then_inc(small, 16)
                sp.dma_start(bf_row[:], I["b_f"].to_broadcast([P, NH])).then_inc(small, 16)

                def load_ring(at):
                    name, i = ring[at]
                    if at >= RING:
                        before, last = ring[at - RING]
                        if before == "w":
                            sp.wait_ge(w_used, last + 1)
                        elif before == "g":
                            sp.wait_ge(wg_used, last + 1)
                        else:
                            sp.wait_ge(half_turned, 2 * (last + 1))
                    src = {"w": I["w_ada"][0, i // 2 * P:(i // 2 + 1) * P, i % 2 * D:(i % 2 + 1) * D] if name == "w" else None,
                           "x": I["x"][0, i * P:(i + 1) * P, :],
                           "g": I["w_ada"][0, i % KT * P:(i % KT + 1) * P, 2 * D:3 * D]}
                    sp.dma_start(ring_sb[:, at % RING, :], src[name]).then_inc(ring_loaded[at % RING], 16)

                def load_wv(k):
                    if k >= 2:
                        sp.wait_ge(wv_split, k - 1)
                    rows = I["w_in"][0, k * P:(k + 1) * P, :]
                    sp.dma_start(w_raw[:, k % 2, 0:W], rows[:, VB0:VB0 + W]).then_inc(wv_loaded[k % 2], 16)
                    sp.dma_start(w_raw[:, k % 2, W:VW], rows[:, VA0:VA0 + KV * HD]).then_inc(wv_loaded[k % 2], 16)
                    sp.dma_start(w_raw[:, k % 2, VW:VF], rows[:, FB0:FB0 + NH]).then_inc(wv_loaded[k % 2], 16)

                AHEAD = 20
                for at in range(AHEAD):
                    load_ring(at)
                    if at % 2 and at // 2 < KT:
                        load_wv(at // 2)
                for n in range(NB):
                    if AHEAD + n < len(ring):
                        load_ring(AHEAD + n)
                    for half in range(2):
                        cols = slice(half * VN, min((half + 1) * VN, VW))
                        sp.wait_ge(v_lo_ready, 2 * n + half + 1)
                        for part, src in enumerate((v_hi, v_lo)):
                            sp.dma_start(S["v"][part, n * P:(n + 1) * P, cols], f32(src[:, half, 0:cols.stop - cols.start])).then_inc(v_stored[half], 16)
                for at in range(AHEAD + NB, len(ring)):
                    load_ring(at)
                sp.wait_ge(h_lo_ready, NB)
                sp.dma_start(gate, I["b_ada"][:, 2 * D:3 * D]).then_inc(gate_loaded, 16)
                sp.wait_ge(gate_ready, 1)
                sp.dma_start(S["gate"], gate).then_inc(gate_stored, 16)
                sp.wait_ge(rows_split, 2)
                for part, src in enumerate((c_hi, c_lo)):
                    sp.dma_start(S["negc"][part, NH:2 * NH, :].rearrange("h (n p) -> (h n) p", p=P), f32(src[:])).then_inc(rows_stored, 16)
                for half in range(2):
                    sp.wait_ge(v_stored[half], 32 * NB)
                sp.wait_ge(rows_stored, 32)
                sp.wait_ge(gate_stored, 16)

            @block.gpsimd
            def _(gp):
                gp.memset(f32(c_lo[:]), 0.0).then_inc(consts, 1)
                gp.memset(ident[:], 0.0).then_inc(consts, 1)
                gp.memset(upper[:], 1.0).then_inc(consts, 1)
                gp.memset(ones[:], 1.0).then_inc(consts, 1)
                gp.wait_ge(consts, 4)
                gp.affine_select(out=ident[:], in_=ident[:], compare_op=ALU.not_equal, fill=1.0,
                                 base=0, pattern=[[-1, P]], channel_multiplier=1).then_inc(consts, 1)
                gp.affine_select(out=upper[:], in_=upper[:], compare_op=ALU.is_ge, fill=0.0,
                                 base=0, pattern=[[1, P]], channel_multiplier=-1).then_inc(consts, 1)
                for k in range(KT):
                    gp.wait_ge(wv_loaded[k % 2], 48 * (k // 2 + 1))
                    gp.tensor_scalar(w_hi[:, k, :], w_raw[:, k % 2, :], 1.0, 0.0, ALU.mult, ALU.add).then_inc(wv_hi_ready, 1)
                    gp.wait_ge(wv_hi_ready, k + 1)
                    gp.tensor_tensor(w_lo[:, k, :], w_raw[:, k % 2, :], f32(w_hi[:, k, :]), ALU.subtract).then_inc(wv_split, 1)
                for n in range(NB):
                    tok = slice(n * P, (n + 1) * P)
                    gp.wait_ge(h_hi_ready, n + 1)
                    gp.tensor_tensor(hT_lo[:, :, tok], h_raw[:], f32(hT_hi[:, :, tok]), ALU.subtract).then_inc(h_lo_ready, 1)

            @block.tensor
            def _(pe):
                def turn(n):
                    pe.wait_ge(xn_ready, n + 1)
                    for half in range(2):
                        if n:
                            pe.wait_ge(raw_half, 2 * (n - 1) + half + 1)
                        for j in range(4):
                            k = 4 * half + j
                            last = nc.tensor.transpose(turned[:, half, j, :], ring_sb[:, slot["x", n], k * P:(k + 1) * P], ident[:])
                        last.then_inc(half_turned, 1)

                pe.wait_ge(small, 64)
                for u in range(2 * KT):
                    k, half = divmod(u, 2)
                    at = slot["w", u]
                    pe.wait_ge(ring_loaded[at], 16 * loads["w", u])
                    for q in range(2):
                        last = nc.tensor.matmul(ada_rows[half][:, q, :], cond[:, k:k + 1], ring_sb[:, at, q * CH:(q + 1) * CH],
                                                start=(k == 0), stop=(k == KT - 1))
                    last.then_inc(w_used, 1)
                pe.wait_ge(consts, 6)
                for half in range(2):
                    pe.wait_ge(row_copied, half + 1)
                    for j in range(KT):
                        col = half * KT + j
                        last = nc.tensor.matmul(ada_ps[:, col:col + 1], ada_row[:, j * P:(j + 1) * P], ones[0:1, 0:1],
                                                start=(col == 0), stop=True, skip_group_check=True)
                    last.then_inc(row_turned, 1)
                turn(0)
                for n in range(NB):
                    if n + 1 < NB:
                        turn(n + 1)
                    tok = slice(n * P, (n + 1) * P)
                    pe.wait_ge(h_lo_ready, n + 1)
                    for half in range(2):
                        unit = 2 * n + half
                        cols = slice(half * VN, (half + 1) * VN)
                        out = out_ps[:, half, 0:VN]
                        if n:
                            pe.wait_ge(v_lo_ready, unit - 1)
                        for k in range(KT):
                            if unit == 0:
                                pe.wait_ge(wv_split, k + 1)
                            nc.tensor.matmul(out, hT_hi[:, k, tok], w_hi[:, k, cols], start=(k == 0), stop=False)
                            nc.tensor.matmul(out, hT_hi[:, k, tok], w_lo[:, k, cols], start=False, stop=False)
                            last = nc.tensor.matmul(out, hT_lo[:, k, tok], w_hi[:, k, cols], start=False, stop=(k == KT - 1))
                        last.then_inc(done, 1)
                for k in range(KT):
                    at = slot["g", k]
                    pe.wait_ge(ring_loaded[at], 16 * loads["g", k])
                    for half in range(2):
                        last = nc.tensor.matmul(square[0:1, half * CH:(half + 1) * CH], cond[:, k:k + 1], ring_sb[:, at, half * CH:(half + 1) * CH],
                                                start=(k == 0), stop=(k == KT - 1))
                    last.then_inc(wg_used, 1)
                pe.wait_ge(logf_ready, 1)
                nc.tensor.matmul(ada_ps[:, 0:NB * NH], upper[:], flat[:].rearrange("p n h -> p (n h)"), start=True, stop=True)
                nc.tensor.matmul(row_ps[:, 0:NB * NH], ones[:], flat[:].rearrange("p n h -> p (n h)"), start=True, stop=True).then_inc(sums_ready, 1)
                pe.wait_ge(cum_ready, 1)
                nc.tensor.transpose(row_ps[:, P:2 * P], cum[:].rearrange("p h n -> p (h n)"), ident[:]).then_inc(rows_ready, 1)

            @block.scalar
            def _(act):
                def statistics(n):
                    at = slot["x", n]
                    act.wait_ge(ring_loaded[at], 16 * loads["x", n])
                    if n:
                        act.wait_ge(summed, n)
                    nc.scalar.activation(square[:], ring_sb[:, at, :], ACT.Square, accum_out=sums[:, n:n + 1]).then_inc(summed, 1)
                    act.wait_ge(inverted, n + 1)
                    nc.scalar.activation(rstd[:, n:n + 1], tmp[:, n:n + 1], ACT.Sqrt).then_inc(rooted, 1)

                def split(n):
                    act.wait_ge(raw_half, 2 * n + 2)
                    nc.scalar.activation(hT_hi[:, :, n * P:(n + 1) * P], h_raw[:], ACT.Copy).then_inc(h_hi_ready, 1)

                act.wait_ge(consts, 1)
                for part in range(2):
                    act.dma_start(S["negc"][part, 0:NH, :].rearrange("h (n p) -> (h n) p", p=P), f32(c_lo[:])).then_inc(zeros_stored, 16)
                act.wait_ge(angle_ready, 1)
                for i in range(2):
                    nc.scalar.activation(table[:, i, :], table[:, i, :], ACT.Sin).then_inc(sined, 1)
                act.wait_ge(sined, 2)
                for q in range(NC):
                    act.dma_start(S["tab"][:, :, q * CH:(q + 1) * CH].rearrange("i f t -> f i t"), table[32 * q:32 * q + 32, :, :]).then_inc(tab_stored, 16)
                statistics(0)
                statistics(1)
                split(0)
                for n in range(NB):
                    if n + 1 < NB:
                        split(n + 1)
                    if n + 2 < NB:
                        statistics(n + 2)
                    for half in range(2):
                        unit = 2 * n + half
                        act.wait_ge(done, unit + 1)
                        if n:
                            act.wait_ge(v_stored[half], 32 * n)
                        nc.scalar.activation(v_hi[:, half, :], out_ps[:, half, 0:VN], ACT.Copy).then_inc(v_hi_ready, 1)
                act.wait_ge(logit_ready, 1)
                nc.scalar.activation(e_neg[:], flat[:], ACT.Exp, scale=-1.0).then_inc(e_ready, 1)
                act.wait_ge(one_ready, 1)
                nc.scalar.activation(ln_e[:], one_e[:], ACT.Ln).then_inc(ln_ready, 1)
                act.wait_ge(rows_ready, 1)
                nc.scalar.activation(c_hi[:], row_ps[:, P:2 * P], ACT.Copy, scale=-1.0).then_inc(rows_split, 1)
                act.wait_ge(tab_stored, 16 * NC)

            @block.vector
            def _(dv):
                step = chain(dv, dve)

                def normalise(n):
                    v, t, r = vv[:, n:n + 1], tmp[:, n:n + 1], rstd[:, n:n + 1]
                    row = ring_sb[:, slot["x", n], :]
                    dv.wait_ge(summed, n + 1)
                    step(nc.vector.tensor_scalar(v, sums[:, n:n + 1], 1.0 / D, EPS, ALU.mult, ALU.add))
                    nc.vector.reciprocal(t, v).then_inc(inverted, 1)
                    dv.wait_ge(rooted, n + 1)
                    step(nc.vector.tensor_tensor(t, r, r, ALU.mult))
                    step(nc.vector.tensor_tensor(t, t, v, ALU.mult))
                    step(nc.vector.tensor_scalar(t, t, -0.5, 1.5, ALU.mult, ALU.add))
                    step(nc.vector.tensor_tensor(r, r, t, ALU.mult))
                    nc.vector.tensor_scalar(row, row, r, None, ALU.mult).then_inc(xn_ready, 1)

                def condition(n):
                    if n:
                        dv.wait_ge(h_lo_ready, n)
                    for half in range(2):
                        dv.wait_ge(half_turned, 2 * n + half + 1)
                        for j in range(4):
                            k = 4 * half + j
                            last = nc.vector.tensor_scalar(h_raw[:, k, :], turned[:, half, j, :], gain[:, k:k + 1], shift[:, k:k + 1],
                                                           ALU.mult, ALU.add)
                        last.then_inc(raw_half, 1)

                ang, oth = table[:, 0, :], table[:, 1, :]
                dv.wait_ge(pos_loaded, 16 * (1 + NC))
                step(nc.vector.tensor_copy(ang, pos_i[:]))
                step(nc.vector.tensor_scalar(ang, ang, inv[:, 0:1], None, ALU.mult))
                for period, pieces in ((TWO_PI * COARSE, coarse), (TWO_PI, fine)):
                    step(nc.vector.tensor_scalar(turns, ang, 1.0 / period, None, ALU.mult))
                    step(nc.vector.tensor_copy(turns_i, turns))
                    step(nc.vector.tensor_copy(turns, turns_i))
                    for piece in pieces:
                        step(nc.vector.scalar_tensor_tensor(ang, turns, -piece, ang, ALU.mult, ALU.add))
                for op, bound, turn in ((ALU.is_gt, TWO_PI / 2, -TWO_PI), (ALU.is_lt, -TWO_PI / 2, TWO_PI)):
                    step(nc.vector.tensor_scalar(turns, ang, bound, turn, op, ALU.mult))
                    step(nc.vector.tensor_tensor(ang, ang, turns, ALU.add))
                step(nc.vector.tensor_scalar(ang, ang, 3.1415925, -3.1415925, ALU.min, ALU.max))
                step(nc.vector.tensor_scalar(oth, ang, -1.0, None, ALU.mult))
                step(nc.vector.tensor_tensor(oth, oth, ang, ALU.max))
                nc.vector.tensor_scalar(oth, oth, -1.0, TWO_PI / 4, ALU.mult, ALU.add).then_inc(angle_ready, 1)

                normalise(0)
                dv.wait_ge(tab_stored, 16 * NC)
                dv.wait_ge(w_used, 2 * KT)
                for half in range(2):
                    if half:
                        dv.wait_ge(row_turned, 1)
                    nc.vector.tensor_copy(ada_row.rearrange("p (q c) -> p q c", q=2), ada_rows[half]).then_inc(row_copied, 1)
                dv.wait_ge(row_turned, 2)
                dv.wait_ge(small, 64)
                step(nc.vector.tensor_tensor(ada_cols[:], ada_ps[:, 0:2 * KT], bias_cols[:], ALU.add))
                step(nc.vector.tensor_copy(shift[:], ada_cols[:, 0:KT]))
                step(nc.vector.scalar_tensor_tensor(gain[:], ada_cols[:, KT:2 * KT], 1.0, g_col[:], ALU.add, ALU.mult))
                condition(0)
                normalise(1)
                for n in range(NB):
                    if n + 1 < NB:
                        condition(n + 1)
                    if n + 2 < NB:
                        normalise(n + 2)
                    for half in range(2):
                        unit = 2 * n + half
                        dv.wait_ge(v_hi_ready, unit + 1)
                        if half:
                            step(nc.vector.tensor_copy(forget[:, n, :], out_ps[:, half, VN - NH:VN]))
                        if n:
                            dv.wait_ge(v_stored[half], 32 * n)
                        nc.vector.tensor_tensor(v_lo[:, half, :], out_ps[:, half, 0:VN], f32(v_hi[:, half, :]), ALU.subtract).then_inc(v_lo_ready, 1)
                step(nc.vector.tensor_tensor(forget[:], forget[:], bf_row[:].unsqueeze(1).to_broadcast([P, NB, NH]), ALU.add))
                step(nc.vector.tensor_scalar(flat[:], forget[:], -1.0, None, ALU.mult))
                nc.vector.tensor_tensor(flat[:], flat[:], forget[:], ALU.max).then_inc(logit_ready, 1)
                dv.wait_ge(e_ready, 1)
                nc.vector.tensor_scalar(one_e[:], e_neg[:], 1.0, None, ALU.add).then_inc(one_ready, 1)
                dv.wait_ge(ln_ready, 1)
                step(nc.vector.tensor_scalar(one_e[:], one_e[:], -1.0, None, ALU.add))
                step(nc.vector.tensor_scalar(flat[:], one_e[:], 0.0, None, ALU.is_equal))
                step(nc.vector.tensor_tensor(ln_e[:], ln_e[:], flat[:], ALU.add))
                step(nc.vector.tensor_tensor(one_e[:], one_e[:], flat[:], ALU.add))
                step(nc.vector.reciprocal(one_e[:], one_e[:]))
                step(nc.vector.tensor_tensor(ln_e[:], ln_e[:], one_e[:], ALU.mult))
                step(nc.vector.tensor_tensor(ln_e[:], ln_e[:], e_neg[:], ALU.mult))
                nc.vector.scalar_tensor_tensor(flat[:], forget[:], 0.0, ln_e[:], ALU.min, ALU.subtract).then_inc(logf_ready, 1)
                dv.wait_ge(wg_used, KT)
                dv.wait_ge(gate_loaded, 16)
                nc.vector.tensor_tensor(gate, square[0:1, :], gate, ALU.add).then_inc(gate_ready, 1)
                dv.wait_ge(sums_ready, 1)
                step(nc.vector.memset(e_neg[:, 0, :], 0.0))
                for n in range(1, NB):
                    step(nc.vector.tensor_tensor(e_neg[:, n, :], e_neg[:, n - 1, :], row_ps[:, (n - 1) * NH:n * NH], ALU.add))
                nc.vector.tensor_tensor(cum[:].rearrange("p h n -> p n h"), ada_ps[:, 0:NB * NH].rearrange("p (n h) -> p n h", h=NH), e_neg[:],
                                        ALU.add).then_inc(cum_ready, 1)
                dv.wait_ge(rows_split, 1)
                dv.wait_ge(zeros_stored, 32)
                nc.vector.scalar_tensor_tensor(c_lo[:], row_ps[:, P:2 * P], -1.0, f32(c_hi[:]), ALU.mult, ALU.subtract).then_inc(rows_split, 1)


ROPE, RAW, SILU, SIGMOID = "rope", "raw", "silu", "sigmoid"


def project(nc, I, S, hT_hi, hT_lo):
    segments = [
        (ROPE, KA0, 1, 1.0, ("k", 0)),
        (ROPE, QA0, 4, SCALE, ("q", 0)),
        (RAW, QB0, 4, SCALE, ("q", NH)),
        (RAW, KB0, 4, 1.0, ("k", KV)),
        (SILU, ZA0, 4, 1.0, ("z", 0)),
        (SILU, ZB0, 4, 1.0, ("z", W)),
        (SIGMOID, GA0, 16, 1.0, ("g", 0)),
    ]

    def each_tile(eng, emit):
        first = 0
        for kind, col, tiles, factor, (name, row) in segments:
            if tiles == 1:
                emit(kind, 0, 0, col, factor, name, 0, row)
            else:
                with eng.Fori(0, tiles // 2) as i:
                    for k in range(2):
                        emit(kind, 2 * i + (first + k), (first + k) % 2, col + 2 * P * i + k * P, factor, name, 2 * i + k, row)
            first += tiles

    with ExitStack() as ctx:
        b = Memory(nc, ctx, "proj")
        cosT = b.sb("cos", [P, T])
        sinT = b.sb("sin", [P, T])

        w_raw = b.sb("w_raw", [P, 2, KT, P])
        w_hi = b.sb("w_hi", [P, 2, KT, P], F32R)
        w_lo = b.sb("w_lo", [P, 2, KT, P], F32R)
        o_hi = b.sb("o_hi", [P, 2, CH], F32R)
        o_lo = b.sb("o_lo", [P, 2, CH], F32R)
        o_act = b.sb("o_act", [P, 2, CH])
        direct = b.sb("direct", [P, CH])
        crossed = b.sb("crossed", [P, CH])
        out_ps = b.ps("out_ps", [P, 2, NC, CH])
        passed = b.sem("passed")
        tab_loaded = b.sem("tables_loaded")
        negated = b.sem("sines_negated")
        w_loaded = [b.sem(f"w_loaded{i}") for i in range(2)]
        w_hi_ready = b.sem("w_hi_ready")
        w_ready = b.sem("w_ready")
        chunk_done = b.sem("chunk_done")
        bank_free = b.sem("bank_free")
        rotated = b.sem("rotated")
        hi_ready = b.sem("hi_ready")
        lo_ready = b.sem("lo_ready")
        act_ready = b.sem("act_ready")
        stored = [b.sem(f"stored{i}") for i in range(2)]

        ROPES = 5
        SPLITS = 13
        DMAS = {ROPE: 4, RAW: 2, SILU: 1, SIGMOID: 1}

        def stored_before(kind, n, c):
            since = {ROPE: 0, RAW: ROPES, SILU: SPLITS, SIGMOID: SPLITS}[kind]
            base = {ROPE: 0, RAW: 2 * 4 * ROPES}.get(kind, 2 * 4 * ROPES + 2 * 2 * (SPLITS - ROPES))
            return (n - since) * (2 * 16 * DMAS[kind]) + 16 * (base + DMAS[kind] * (c // 2))

        with nc.Block() as block:
            @block.sync
            def _(sp):
                def emit(kind, n, par, col, factor, name, tile, row):
                    if not (isinstance(n, int) and n == 0):
                        sp.wait_ge(w_ready, n)
                    sp.dma_start(w_raw[:, par, :, :],
                                 I["w_in"][0, :, bass.ds(col, P)].rearrange("(k p) c -> p k c", p=P)).then_inc(w_loaded[par], 16)
                    if isinstance(n, int) and n == 0:
                        for r in range(4):
                            rows = slice(32 * r, 32 * r + 32)
                            sp.dma_start(cosT[rows, :], S["tab"][1]).then_inc(tab_loaded, 16)
                            sp.dma_start(sinT[rows, :], S["tab"][0]).then_inc(tab_loaded, 16)
                each_tile(sp, emit)

            @block.gpsimd
            def _(gp):
                def emit(kind, n, par, col, factor, name, tile, row):
                    gp.wait_ge(w_loaded[par], (n - par) * 8 + 16)
                    if not (isinstance(n, int) and n == 0):
                        gp.wait_ge(chunk_done, n * NC)
                        gp.sem_inc(passed, 1)
                    if kind == ROPE:
                        src = w_raw[:, par, :, :].rearrange("p k (h s c) -> p s k h c", h=2, s=2)
                        hi = w_hi[:, par, :, :].rearrange("p k (s h c) -> p s k h c", h=2, s=2)
                        lo = w_lo[:, par, :, :].rearrange("p k (s h c) -> p s k h c", h=2, s=2)
                        trios = [(src[:, s], hi[:, s], lo[:, s]) for s in range(2)]
                    else:
                        trios = [(w_raw[:, par, :, :], w_hi[:, par, :, :], w_lo[:, par, :, :])]
                    for s, h, _ in trios:
                        last = gp.tensor_scalar(h, s, 1.0, 0.0, ALU.mult, ALU.add)
                    last.then_inc(w_hi_ready, 1)
                    gp.wait_ge(w_hi_ready, n + 1)
                    for s, h, l in trios:
                        last = gp.tensor_tensor(l, s, f32(h), ALU.subtract)
                    last.then_inc(w_ready, 1)
                gp.sem_inc(w_ready, 1)
                each_tile(gp, emit)

            @block.tensor
            def _(pe):
                def emit(kind, n, par, col, factor, name, tile, row):
                    pe.wait_ge(w_ready, n + 2)
                    if kind not in (ROPE, RAW):
                        pe.wait_ge(bank_free, (SPLITS + 2) * NC)
                    for c in range(NC):
                        if kind in (ROPE, RAW):
                            pe.wait_ge(bank_free, n * NC + (c + 1))
                        else:
                            pe.wait_ge(act_ready, (n - SPLITS) * NC + (c + 1))
                        tok = slice(c * CH, (c + 1) * CH)
                        out = out_ps[:, par, c, :]
                        for k in range(KT):
                            nc.tensor.matmul(out, w_hi[:, par, k, :], hT_hi[:, k, tok], start=(k == 0), stop=False)
                            nc.tensor.matmul(out, w_hi[:, par, k, :], hT_lo[:, k, tok], start=False, stop=False)
                            last = nc.tensor.matmul(out, w_lo[:, par, k, :], hT_hi[:, k, tok], start=False, stop=(k == KT - 1))
                        last.then_inc(chunk_done, 1)
                pe.sem_inc(chunk_done, NC)
                each_tile(pe, emit)

            @block.scalar
            def _(act):
                def emit(kind, n, par, col, factor, name, tile, row):
                    for c in range(NC):
                        q = n * NC + (c + 1)
                        out = out_ps[:, par, c, :]
                        tok = slice(c * CH, (c + 1) * CH)
                        act.wait_ge(stored[c % 2], stored_before(kind, n, c))
                        if kind in (ROPE, RAW):
                            if kind == ROPE:
                                act.wait_ge(rotated, q)
                            else:
                                act.wait_ge(chunk_done, q + NC)
                            src = direct[:] if kind == ROPE else out
                            nc.scalar.activation(o_hi[:, c % 2, :], src, ACT.Copy, scale=factor).then_inc(hi_ready, 1)
                            act.wait_ge(lo_ready, q)
                            for part, stage in enumerate((o_hi, o_lo)):
                                if kind == RAW:
                                    dst = S[name][part, bass.ds(tile * 2 + row, 2), :, tok].rearrange("h d t -> (h d) t")
                                    act.dma_start(dst, f32(stage[:, c % 2, :])).then_inc(stored[c % 2], 16)
                                else:
                                    for s in range(2):
                                        dst = S[name][part, bass.ds(tile * 2 + row, 2), s * 32:(s + 1) * 32, tok]
                                        act.dma_start(dst, f32(stage[64 * s:64 * s + 64, c % 2, :])).then_inc(stored[c % 2], 16)
                        else:
                            act.wait_ge(chunk_done, q + NC)
                            f = ACT.Silu if kind == SILU else ACT.Sigmoid
                            nc.scalar.activation(o_act[:, c % 2, :], out, f).then_inc(act_ready, 1)
                            act.wait_ge(act_ready, (n - SPLITS + 2) * NC + (c + 1))
                            act.dma_start(S[name][bass.ds(tile * P + row, P), tok], o_act[:, c % 2, :]).then_inc(stored[c % 2], 16)
                act.sem_inc(act_ready, 2 * NC)
                each_tile(act, emit)
                for par in range(2):
                    act.wait_ge(stored[par], 16 * 2 * (4 * ROPES + 2 * (SPLITS - ROPES) + 24))

            @block.vector
            def _(dv):
                dv.sem_inc(bank_free, 2 * NC)

                def emit(kind, n, par, col, factor, name, tile, row):
                    if kind not in (ROPE, RAW):
                        return
                    for c in range(NC):
                        q = n * NC + (c + 1)
                        out = out_ps[:, par, c, :]
                        tok = slice(c * CH, (c + 1) * CH)
                        src = out
                        if kind == ROPE:
                            if isinstance(n, int) and n == 0 and c == 0:
                                dv.wait_ge(tab_loaded, 8 * 16)
                                nc.vector.tensor_scalar(sinT[64:P, :], sinT[64:P, :], -1.0, None, ALU.mult).then_inc(negated, 1)
                                dv.wait_ge(negated, 1)
                            dv.wait_ge(chunk_done, q + NC)
                            nc.vector.tensor_tensor(direct[:], out, cosT[:, tok], ALU.mult)
                            nc.vector.tensor_tensor(crossed[0:64, :], out[64:P, :], sinT[64:P, tok], ALU.mult)
                            nc.vector.tensor_tensor(crossed[64:P, :], out[0:64, :], sinT[0:64, tok], ALU.mult).then_inc(bank_free, 1)
                            dv.wait_ge(bank_free, q + 2 * NC)
                            nc.vector.tensor_tensor(direct[:], direct[:], crossed[:], ALU.add).then_inc(rotated, 1)
                            src = direct[:]
                        dv.wait_ge(stored[c % 2], stored_before(kind, n, c))
                        dv.wait_ge(hi_ready, q)
                        lo = nc.vector.scalar_tensor_tensor(o_lo[:, c % 2, :], src, factor, f32(o_hi[:, c % 2, :]), ALU.mult, ALU.subtract)
                        lo.then_inc(lo_ready, 1)
                        dv.wait_ge(lo_ready, q)
                        if kind == RAW:
                            dv.sem_inc(bank_free, 1)
                first = 0
                for kind, col, tiles, factor, (name, row) in segments:
                    if kind in (ROPE, RAW):
                        if tiles == 1:
                            emit(kind, 0, 0, col, factor, name, 0, row)
                        else:
                            with dv.Fori(0, tiles // 2) as i:
                                for k in range(2):
                                    emit(kind, 2 * i + (first + k), (first + k) % 2, 0, factor, name, 2 * i + k, row)
                    first += tiles


SLIDING, FORGETTING = 0, 1
KINDS = (SLIDING, FORGETTING)
UNROLLED = 4
P_SLOTS = 4
Z_SLOTS = 4
MAX_FIRST = ((-0.5, -0.4), (-0.39, 0.1))
MAX_REST = ((0.16, 0.5), (0.5, 1.02))
BEHIND = 0.19
SLIDING_AT = (-0.12, 0.25, 0.18)
RECIP_PARTS = 4
RECIP_SPACING = (6, 4)
LOWER_AFTER = 4
LAG = 3


def max_units(kind):
    units = []
    for i in range(NB):
        if kind == SLIDING:
            units.append((i, (i - 1) * P, 2 * P, 0, 2 * P, 2 * P) if i else (0, 0, 2 * P, 0, P, P))
        else:
            for kc in range(i // 4 + 1):
                used = min(CH, (i + 1) * P - kc * CH)
                units.append((i, kc * CH, max(used, 2 * P), kc, used, P if kc == i // 4 else 0))
    return units


def score_units(kind, c):
    units = []
    if kind == SLIDING:
        if c:
            units.append((4 * c - 1, 0, 2 * P, slice(2 * P, 4 * P)))
        units += [(4 * c + r, r * P, 2 * P, slice(P, 3 * P)) for r in range(3)]
    else:
        units += [(j, 0, CH, None) for j in range(4 * c)]
        units += [(4 * c + r, r * P, CH - r * P, slice(P, 2 * P)) for r in range(3)]
    units.append((4 * c + 3, 2 * P, 2 * P, slice(0, 2 * P)))
    return units


def attention_order():
    placed = []

    def spread(items, start, end):
        for n, item in enumerate(items):
            placed.append((start + (end - start) * (n + 0.5) / len(items), len(placed), item))

    for u in range(UNROLLED):
        for kind in KINDS:
            start, end = MAX_FIRST[kind] if u == 0 else (u - 1 + x for x in MAX_REST[kind])
            spread([("max", kind, u, n) for n in range(len(max_units(kind)))], start, end)
            spread([("turn", kind, u)], end + 0.02, end + 0.02)
        spread([("score", FORGETTING, u, c, n) for c in range(NC) for n in range(len(score_units(FORGETTING, c)))],
               u + BEHIND, u + 1 + BEHIND)
        for c in range(NC):
            spread([("score", SLIDING, u, c, n) for n in range(len(score_units(SLIDING, c)))],
                   u + SLIDING_AT[0] + SLIDING_AT[1] * c, u + SLIDING_AT[0] + SLIDING_AT[1] * c + SLIDING_AT[2])
    order, waiting = [], []
    for _, _, item in sorted(placed):
        order.append(item)
        if item[0] == "score":
            waiting.append(item)
            if len(waiting) > LAG:
                order.append(("value", *waiting.pop(0)[1:]))
    order += [("value", *item[1:]) for item in waiting]

    def behind(step, distance, item):
        at = next(i for i, x in enumerate(order) if x[:len(step)] == step)
        order.insert(min(at + 1 + distance, len(order)), item)

    for u in range(UNROLLED):
        for kind in KINDS:
            for c in range(NC):
                last, distance = ("value", kind, u, c, len(score_units(kind, c)) - 1), 1
                for part in range(RECIP_PARTS):
                    behind(last, distance, ("recip", kind, u, c, part))
                    last, distance = ("recip", kind, u, c, part), RECIP_SPACING[kind]
                behind(last, 1, ("fin", kind, u, c))
    for u in range(UNROLLED):
        for kind in KINDS:
            for c in range(NC):
                behind(("fin", kind, u, c), 7, ("gate", kind, u, c))
    for item in [item for item in order if item[:2] == ("score", SLIDING)]:
        behind(item, LOWER_AFTER, ("lower", *item[1:]))
    for u in range(2, UNROLLED):
        for kind in KINDS:
            behind(("fin", kind, u - 2, NC - 1), 0, ("load", kind, u))
    order = [("load", kind, u) for u in range(2) for kind in KINDS] + order
    return order


def attend(nc, I, S):
    order = attention_order()
    UNITS = [max_units(kind) for kind in KINDS]
    KV_SETS = (1, 2)

    def numbered(*steps):
        return {item[1:]: n for n, item in enumerate(x for x in order if x[0] in steps)}

    max_no, score_no, fin_no, turn_no = (numbered(s) for s in ("max", "score", "fin", "turn"))
    bank_no = numbered("max", "turn")
    value_no, gate_no, recip_no = numbered("value"), numbered("gate"), numbered("recip")
    assert list(value_no) == list(score_no) and list(gate_no) == list(fin_no)
    lo_no = {what: n for kind in KINDS for n, what in enumerate(x for x in score_no if x[0] == kind)}
    LOWER = [sum(x[0] == kind for x in score_no) for kind in KINDS]
    MAXES, BANKS, SCORES, FINS, TURNS = len(max_no), len(bank_no), len(score_no), len(fin_no), len(turn_no)
    assert BANKS % 2 == 0 and SCORES % P_SLOTS == 0 and FINS % Z_SLOTS == 0

    def last_score(kind, u, c):
        return score_no[kind, u, c, len(score_units(kind, c)) - 1]

    with ExitStack() as ctx:
        b = Memory(nc, ctx, "att")
        qA = [b.sb(f"q_hi_lo{k}", [P, 2, T], F32R) for k in KINDS]
        qB = [b.sb(f"q_hi_rows{k}", [P, 2, T], F32R) for k in KINDS]
        kA = [b.sb(f"k_hi_hi{k}", [P, KV_SETS[k], T], F32R) for k in KINDS]
        kB = [b.sb(f"k_lo_rows{k}", [P, KV_SETS[k], T], F32R) for k in KINDS]
        v = [b.sb(f"v{k}", [P, KV_SETS[k], NB, 3 * HD], F32R) for k in KINDS]
        z = b.sb("z", [HD, Z_SLOTS, CH])
        p_raw = b.sb("p_raw", [P, P_SLOTS, CH])
        p_hi = b.sb("p_hi", [P, P_SLOTS, CH], F32R)
        p_lo = b.sb("p_lo", [P, P_SLOTS, CH], F32R)
        recip = b.sb("recip", [HD, 2, CH])
        head = b.sb("head", [HD, 2, CH])
        gated = b.sb("gated", [HD, 2, CH])
        part_max = [b.sb(f"part_max{k}", [P, NB, (1, NC)[k]]) for k in KINDS]
        neg_m = [b.sb(f"neg_m{k}", [P, NB]) for k in KINDS]
        m_hi = [b.sb(f"m_hi{k}", [NB, P], F32R) for k in KINDS]
        m_lo = [b.sb(f"m_lo{k}", [NB, P], F32R) for k in KINDS]
        e_raw = b.sb("e_raw", [NB, P])
        e_hi = b.sb("e_hi", [NB, P], F32R)
        e_lo = b.sb("e_lo", [NB, P], F32R)
        e_one = b.sb("e_one", [P, P], F32R)
        sink = b.sb("sink", [P, NH])
        ident = b.sb("ident", [P, P])
        ident_b = b.sb("ident_b", [P, P], BF16)
        mask_t = b.sb("mask_t", [P, 4 * P], BF16)
        mask_r = b.sb("mask_r", [P, 2 * P], BF16)
        s_ps = b.ps("s_ps", [P, 2, CH])
        max_ps = b.ps("max_ps", [P, 2, CH])
        value_ps = [b.ps(f"value_ps{k}", [P, 2, CH]) for k in KINDS]

        sink_loaded = b.sem("sink_loaded")
        consts = b.sem("constants")
        filled = b.sem("ones_rows_filled")
        q_loaded = [[b.sem(f"q_loaded{k}_{i}") for i in range(UNROLLED)] for k in KINDS]
        k_loaded = [[b.sem(f"k_loaded{k}_{i}") for i in range((1, UNROLLED)[k])] for k in KINDS]
        v_loaded = [[b.sem(f"v_loaded{k}_{i}") for i in range((1, UNROLLED)[k])] for k in KINDS]
        z_loaded = [b.sem(f"z_loaded{i}") for i in range(Z_SLOTS)]
        set_free = [b.sem(f"set_free{k}") for k in KINDS]
        max_done = b.sem("max_scores_done")
        maxed = b.sem("max_taken")
        m_ready = b.sem("neg_max_ready")
        turned = b.sem("max_turned")
        m_split = b.sem("max_split")
        e_ready = b.sem("sink_exp_ready")
        m_stored = b.sem("max_rows_stored")
        m_rows = [b.sem(f"max_rows_loaded{k}") for k in KINDS]
        s_done = b.sem("scores_done")
        p_raw_ready = b.sem("p_raw_ready")
        p_hi_ready = b.sem("p_hi_ready")
        p_lo_ready = [b.sem(f"p_lo_ready{k}") for k in KINDS]
        values_done = b.sem("values_done")
        recip_ready = b.sem("recip_ready")
        bank_free = [b.sem(f"value_bank_free{k}") for k in KINDS]
        head_ready = b.sem("head_ready")
        gated_ready = b.sem("gated_ready")
        stored = [b.sem(f"gated_stored{i}") for i in range(2)]
        passed = b.sem("passed")
        act_passed = b.sem("act_passed")
        ROWS = (4, 2)
        rows_before = [sum(ROWS[k] for (k, _), n in turn_no.items() if n < t) for t in range(TURNS + 1)]
        ROWS_ALL = rows_before[TURNS]

        made_all = []
        def load(eng, carry, j, kind, u):
            h = UNROLLED * j + u
            s = u % KV_SETS[kind]
            eng.wait_ge(set_free[kind], h + 1)
            eng.sem_inc(carry, 1)

            def load_q(dst, row, part):
                src = S["q"][part, bass.ds(h + NH * kind, 1), :, :].rearrange("h d t -> (h d) t")
                eng.dma_start(f32(dst[kind][row:row + HD, u % 2, :]), src).then_inc(q_loaded[kind][u], 16)

            load_q(qA, 0, 0)
            load_q(qA, HD, 1)
            load_q(qB, 0, 0)
            if kind == FORGETTING or u == 0:
                if kind == SLIDING:
                    eng.wait_ge(set_free[kind], h + 2)
                    eng.sem_inc(carry, 1)
                kh = j if kind == SLIDING else h + KV
                vcol = W + HD * j if kind == SLIDING else HD * h
                for part in range(2):
                    eng.dma_start(f32(kA[kind][part * HD:(part + 1) * HD, s, :]),
                                  S["k"][0, bass.ds(kh, 1), :, :].rearrange("h d t -> (h d) t")).then_inc(k_loaded[kind][u], 16)
                eng.dma_start(f32(kB[kind][0:HD, s, :]), S["k"][1, bass.ds(kh, 1), :, :].rearrange("h d t -> (h d) t")).then_inc(k_loaded[kind][u], 16)
                eng.wait_ge(filled, 2)
                eng.dma_start(f32(kB[kind][HD:HD + 2, s, :]),
                              S["negc"][:, bass.ds(h + NH * kind, 1), :].rearrange("s h t -> s (h t)")).then_inc(k_loaded[kind][u], 16)
                for part in range(2):
                    eng.dma_start(f32(v[kind][:, s, :, part * 2 * HD:part * 2 * HD + HD]),
                                  S["v"][part, :, bass.ds(vcol, HD)].rearrange("(n p) d -> p n d", p=P)).then_inc(v_loaded[kind][u], 16)

        with nc.Block() as block:
            @block.sync
            def _(sp):
                sp.dma_start(sink[:], I["sinks"].to_broadcast([P, NH])).then_inc(sink_loaded, 16)
                def max_rows(j, kind, u):
                    h = UNROLLED * j + u
                    t = turn_no[kind, u]
                    sp.wait_ge(m_split, j * ROWS_ALL + rows_before[t + 1])
                    made = [(m_hi[kind], m_lo[kind])] + ([(e_hi, e_lo)] if kind == SLIDING else [])
                    for which, pair in enumerate(made):
                        for part, src in enumerate(pair):
                            sp.dma_start(S["m"][part, bass.ds(h + NH * (kind + 2 * which), 1), :].rearrange("h (n p) -> (h n) p", p=P),
                                         f32(src[:])).then_inc(m_stored, 16)
                    sp.wait_ge(m_stored, (j * ROWS_ALL + rows_before[t + 1]) * 16)
                    sp.dma_start(f32(qB[kind][HD + 2:HD + 4, u % 2, :]),
                                 S["m"][:, bass.ds(h + NH * kind, 1), :].rearrange("s h t -> s (h t)")).then_inc(m_rows[kind], 16)
                    if kind == SLIDING:
                        sp.dma_start(f32(qB[kind][HD + 4:HD + 6, u % 2, :]), S["m"][:, bass.ds(h + 2 * NH, 1), :].rearrange("s h t -> s (h t)")).then_inc(m_rows[kind], 16)

                def row_of(j, kind, u):
                    return HD * (UNROLLED * j + u) + W * kind

                gates = list(fin_no)

                def load_z(j, k):
                    kind, u, c = gates[k]
                    sp.wait_ge(gated_ready, j * FINS + (k + 1))
                    sp.dma_start(z[:, k % Z_SLOTS, :], S["z"][bass.ds(row_of(j, kind, u), HD), c * CH:(c + 1) * CH]).then_inc(z_loaded[k % Z_SLOTS], 16)

                with sp.Fori(0, NH // UNROLLED) as j:
                    for step, *what in order:
                        if step == "load" and what[1] >= 2:
                            load(sp, passed, j, *what)
                        elif step == "turn":
                            max_rows(j, *what)
                            if turn_no[tuple(what)] == 1:
                                for k in range(2):
                                    load_z(j, k)
                        elif step == "gate":
                            kind, u, c = what
                            k = fin_no[kind, u, c]
                            if k + 2 < FINS:
                                load_z(j, k + 2)
                            sp.wait_ge(gated_ready, j * FINS + (k + 1 + Z_SLOTS))
                            sp.dma_start(S["za"][bass.ds(row_of(j, kind, u), HD), c * CH:(c + 1) * CH], gated[:, k % 2, :]).then_inc(stored[k % 2], 16)
                for i in range(2):
                    sp.wait_ge(stored[i], NH * NC * 16)

            @block.gpsimd
            def _(gp):
                made = [0]

                def const(instruction):
                    made[0] += 1
                    instruction.then_inc(consts, 1)
                    gp.wait_ge(consts, made[0])

                for kind in KINDS:
                    const(gp.memset(f32(v[kind][:, :, :, HD:2 * HD]), 1.0))
                const(gp.memset(ident[:], 0.0))
                const(gp.memset(mask_t[:, 0:P], MASKED))
                const(gp.memset(mask_t[:, P:3 * P], 0.0))
                const(gp.memset(mask_t[:, 3 * P:4 * P], MASKED))
                const(gp.memset(mask_r[:], 0.0))
                const(gp.memset(f32(e_one[HD:HD + 6, :]), 0.0))
                const(gp.memset(f32(e_one[HD:HD + 6, HD:P]), 1.0))
                const(gp.memset(f32(e_one[HD:HD + 4, :]), 0.0))
                const(gp.affine_select(out=ident[:], in_=ident[:], compare_op=ALU.not_equal, fill=1.0,
                                       base=0, pattern=[[-1, P]], channel_multiplier=1))
                const(gp.affine_select(out=mask_t[:, P:2 * P], in_=mask_t[:, P:2 * P], compare_op=ALU.is_ge, fill=MASKED,
                                       base=0, pattern=[[1, P]], channel_multiplier=-1))
                const(gp.affine_select(out=mask_t[:, 2 * P:3 * P], in_=mask_t[:, 2 * P:3 * P], compare_op=ALU.is_gt, fill=MASKED,
                                       base=0, pattern=[[-1, P]], channel_multiplier=1))
                const(gp.affine_select(out=mask_r[:, 0:P], in_=mask_r[:, 0:P], compare_op=ALU.is_gt, fill=MASKED,
                                       base=0, pattern=[[1, P]], channel_multiplier=-1))
                const(gp.affine_select(out=mask_r[:, P:2 * P], in_=mask_r[:, P:2 * P], compare_op=ALU.is_ge, fill=MASKED,
                                       base=0, pattern=[[-1, P]], channel_multiplier=1))
                const(gp.tensor_copy(ident_b[:], ident[:]))
                made_all.append(made[0])
                gp.sem_inc(gated_ready, Z_SLOTS)
                with gp.Fori(0, NH // UNROLLED) as j:
                    for step, *what in order:
                        if step == "score" and what[0] == FORGETTING:
                            kind, u, c, n = what
                            _, off, width, _ = score_units(kind, c)[n]
                            no = score_no[kind, u, c, n]
                            cols = slice(off, off + width)
                            gp.wait_ge(p_hi_ready, j * SCORES + (no + 1 + 2))
                            gp.tensor_tensor(p_lo[:, no % P_SLOTS, cols], p_raw[:, no % P_SLOTS, cols], f32(p_hi[:, no % P_SLOTS, cols]),
                                             ALU.subtract).then_inc(p_lo_ready[FORGETTING], 1)
                        elif step == "gate":
                            k = fin_no[tuple(what)]
                            gp.wait_ge(z_loaded[k % Z_SLOTS], (j * (FINS // Z_SLOTS) + (k // Z_SLOTS + 1)) * 16)
                            gp.wait_ge(head_ready, j * FINS + (k + 1))
                            if k >= 2:
                                gp.wait_ge(stored[k % 2], (j * (FINS // 2) + k // 2) * 16)
                            gp.tensor_tensor(gated[:, k % 2, :], head[:, k % 2, :], z[:, k % Z_SLOTS, :], ALU.mult).then_inc(gated_ready, 1)

            @block.tensor
            def _(pe):
                pe.sem_inc(values_done, P_SLOTS)
                pe.sem_inc(turned, TURNS)
                pe.wait_ge(consts, made_all[0])
                pe.wait_ge(filled, 3)
                with pe.Fori(0, NH // UNROLLED) as j:
                    for step, *what in order:
                        if step == "max":
                            kind, u, n = what
                            s, sq = u % KV_SETS[kind], u % 2
                            i, k0, width, _, used, mask = UNITS[kind][n]
                            no = bank_no[kind, u, n]
                            if n == 0:
                                if kind == FORGETTING:
                                    pe.wait_ge(filled, 4)
                                pe.wait_ge(q_loaded[kind][u], (j + 1) * 48)
                                pe.wait_ge(k_loaded[kind][0 if kind == SLIDING else u], (j + 1) * 64)
                            pe.wait_ge(maxed, j * BANKS + (no + 1))
                            blk, keys = slice(i * P, (i + 1) * P), slice(k0, k0 + width)
                            out = max_ps[:, no % 2, 0:width]
                            nc.tensor.matmul(out, qA[kind][:, sq, blk], kA[kind][:, s, keys], start=True, stop=False)
                            last = nc.tensor.matmul(out, qB[kind][0:HD + 2, sq, blk], kB[kind][0:HD + 2, s, keys], start=False, stop=not mask)
                            if mask:
                                last = nc.tensor.matmul(max_ps[:, no % 2, used - mask:used], ident_b[:], mask_r[:, 2 * P - mask:2 * P],
                                                        start=False, stop=True)
                            last.then_inc(max_done, 1)
                        elif step == "turn":
                            kind, u = what
                            t, no = turn_no[kind, u], bank_no[kind, u]
                            pe.wait_ge(m_ready, j * TURNS + (t + 1))
                            pe.wait_ge(maxed, j * BANKS + (no + 1))
                            nc.tensor.transpose(max_ps[0:NB, no % 2, 0:P], neg_m[kind][:], ident[:]).then_inc(turned, 1)
                        elif step == "score":
                            kind, u, c, n = what
                            s, sq = u % KV_SETS[kind], u % 2
                            blk, off, width, mask = score_units(kind, c)[n]
                            no = score_no[kind, u, c, n]
                            if c == 0 and n == 0:
                                pe.wait_ge(m_rows[kind], (UNROLLED * j + (u + 1)) * (ROWS[kind] // 2 * 16))
                            pe.wait_ge(p_hi_ready, j * SCORES + (no + 1))
                            keys = slice(blk * P, (blk + 1) * P)
                            qry = slice(c * CH + off, c * CH + off + width)
                            out = s_ps[:, no % 2, off:off + width]
                            nc.tensor.matmul(out, kA[kind][:, s, keys], qA[kind][:, sq, qry], start=True, stop=False)
                            last = nc.tensor.matmul(out, kB[kind][0:HD + 4, s, keys], qB[kind][0:HD + 4, sq, qry], start=False, stop=mask is None)
                            if mask is not None:
                                last = nc.tensor.matmul(s_ps[:, no % 2, off:off + mask.stop - mask.start], ident_b[:], mask_t[:, mask],
                                                        start=False, stop=True)
                            last.then_inc(s_done, 1)
                        elif step == "value":
                            kind, u, c, n = what
                            s = u % KV_SETS[kind]
                            blk, off, width, _ = score_units(kind, c)[n]
                            no = score_no[kind, u, c, n]
                            bank = value_ps[kind][:, c % 2, :]
                            opens = n == 0
                            if c == 0 and n == 0:
                                pe.wait_ge(v_loaded[kind][0 if kind == SLIDING else u], (j + 1) * 32)
                            if opens:
                                pe.wait_ge(bank_free[kind], (UNROLLED * j + u) * NC + (c + 1))
                                if kind == SLIDING:
                                    nc.tensor.matmul(bank, e_one[HD:HD + 6, :], qB[kind][HD:HD + 6, u % 2, c * CH:(c + 1) * CH], start=True, stop=False)
                                    opens = False
                            pe.wait_ge(p_lo_ready[kind], j * LOWER[kind] + (lo_no[kind, u, c, n] + 1))
                            out = bank[:, off:off + width]
                            ones_v, lo_v = v[kind][:, s, blk, 0:2 * HD], v[kind][:, s, blk, 2 * HD:3 * HD]
                            hi, lo = p_hi[:, no % P_SLOTS, off:off + width], p_lo[:, no % P_SLOTS, off:off + width]
                            nc.tensor.matmul(out, ones_v, hi, start=opens, stop=False)
                            nc.tensor.matmul(out[0:HD, :], lo_v, hi, start=False, stop=False)
                            nc.tensor.matmul(out, ones_v, lo, start=False, stop=n == len(score_units(kind, c)) - 1).then_inc(values_done, 1)

            @block.scalar
            def _(act):
                act.sem_inc(p_hi_ready, 2)
                act.wait_ge(sink_loaded, 16)

                with act.Fori(0, NH // UNROLLED) as j:
                    for step, *what in order:
                        if step == "load" and what[1] < 2:
                            load(act, act_passed, j, *what)
                        elif step == "turn" and what[0] == SLIDING:
                            u = what[1]
                            act.wait_ge(turned, j * TURNS + (turn_no[SLIDING, u] + 1 + TURNS))
                            nc.scalar.activation(e_raw[:], max_ps[0:NB, bank_no[SLIDING, u] % 2, 0:P], ACT.Exp, bias=sink[0:NB, bass.ds(UNROLLED * j + u, 1)]).then_inc(e_ready, 1)
                        elif step == "score":
                            kind, u, c, n = what
                            _, off, width, _ = score_units(kind, c)[n]
                            no = score_no[kind, u, c, n]
                            cols = slice(off, off + width)
                            act.wait_ge(s_done, j * SCORES + (no + 1))
                            act.wait_ge(values_done, j * SCORES + (no + 1))
                            nc.scalar.activation(p_raw[:, no % P_SLOTS, cols], s_ps[:, no % 2, cols], ACT.Exp).then_inc(p_raw_ready, 1)
                            nc.scalar.activation(p_hi[:, no % P_SLOTS, cols], s_ps[:, no % 2, cols], ACT.Exp).then_inc(p_hi_ready, 1)

            @block.vector
            def _(dv):
                dv.sem_inc(maxed, 2)
                for kind in KINDS:
                    dv.sem_inc(set_free[kind], 2)
                    dv.sem_inc(bank_free[kind], 2)
                for kind in KINDS:
                    nc.vector.memset(f32(kB[kind][HD:HD + 32, :, :]), 1.0).then_inc(filled, 1)
                for kind in KINDS:
                    nc.vector.memset(f32(qB[kind][HD:HD + 32, :, :]), 1.0).then_inc(filled, 1)
                nc.vector.memset(part_max[FORGETTING][:], MASKED).then_inc(filled, 1)
                dv.wait_ge(filled, 5)
                dv.wait_ge(sink_loaded, 16)
                with dv.Fori(0, NH // UNROLLED) as j:
                    for step, *what in order:
                        if step == "max":
                            kind, u, n = what
                            i, _, _, col, used, _ = UNITS[kind][n]
                            no = bank_no[kind, u, n]
                            if n == 0:
                                before = turn_no[kind, u - 1] + TURNS if u else turn_no[kind, UNROLLED - 1]
                                dv.wait_ge(turned, j * TURNS + (before + 1))
                            dv.wait_ge(max_done, j * MAXES + (max_no[kind, u, n] + 1))
                            nc.vector.reduce_max(part_max[kind][:, i, col:col + 1], max_ps[:, no % 2, 0:used], AX.X).then_inc(maxed, 1)
                            if n == len(UNITS[kind]) - 1:
                                dv.wait_ge(maxed, j * BANKS + (no + 1 + 2))
                                if kind == SLIDING:
                                    nc.vector.tensor_scalar(neg_m[kind][:], part_max[kind][:, :, 0], sink[:, bass.ds(UNROLLED * j + u, 1)], -1.0,
                                                            ALU.max, ALU.mult).then_inc(m_ready, 1)
                                else:
                                    nc.vector.reduce_max(neg_m[kind][:], part_max[kind][:], AX.X, negate=True).then_inc(m_ready, 1)
                        elif step == "turn":
                            kind, u = what
                            t = turn_no[kind, u]
                            row = max_ps[0:NB, bank_no[kind, u] % 2, 0:P]
                            if kind == SLIDING:
                                dv.wait_ge(e_ready, UNROLLED * j + (u + 1))
                            else:
                                dv.wait_ge(turned, j * TURNS + (t + 1 + TURNS))
                            if t:
                                dv.wait_ge(m_stored, (j * ROWS_ALL + rows_before[t]) * 16)
                            nc.vector.tensor_copy(m_hi[kind][:], row).then_inc(m_split, 1)
                            dv.wait_ge(m_split, j * ROWS_ALL + (rows_before[t] + 1))
                            nc.vector.tensor_tensor(m_lo[kind][:], row, f32(m_hi[kind][:]), ALU.subtract).then_inc(m_split, 1)
                            if kind == SLIDING:
                                nc.vector.tensor_copy(e_hi[:], e_raw[:]).then_inc(m_split, 1)
                                dv.wait_ge(m_split, j * ROWS_ALL + (rows_before[t] + 3))
                                nc.vector.tensor_tensor(e_lo[:], e_raw[:], f32(e_hi[:]), ALU.subtract).then_inc(m_split, 1)
                            dv.wait_ge(m_split, j * ROWS_ALL + rows_before[t + 1])
                            dv.sem_inc(maxed, 1)
                        elif step == "lower":
                            kind, u, c, n = what
                            _, off, width, _ = score_units(kind, c)[n]
                            no = score_no[kind, u, c, n]
                            cols = slice(off, off + width)
                            dv.wait_ge(p_hi_ready, j * SCORES + (no + 1 + 2))
                            nc.vector.tensor_tensor(p_lo[:, no % P_SLOTS, cols], p_raw[:, no % P_SLOTS, cols], f32(p_hi[:, no % P_SLOTS, cols]),
                                                    ALU.subtract).then_inc(p_lo_ready[SLIDING], 1)
                        elif step == "recip":
                            kind, u, c, part = what
                            bank = value_ps[kind][:, c % 2, :]
                            if part == 0:
                                dv.wait_ge(values_done, j * SCORES + (last_score(kind, u, c) + 1 + P_SLOTS))
                            cols = slice(part * CH // RECIP_PARTS, (part + 1) * CH // RECIP_PARTS)
                            nc.vector.reciprocal(recip[:, fin_no[kind, u, c] % 2, cols], bank[HD:P, cols]).then_inc(recip_ready, 1)
                        elif step == "fin":
                            kind, u, c = what
                            k = fin_no[kind, u, c]
                            bank = value_ps[kind][:, c % 2, :]
                            dv.wait_ge(recip_ready, j * FINS * RECIP_PARTS + (recip_no[kind, u, c, RECIP_PARTS - 1] + 1))
                            dv.wait_ge(gated_ready, j * FINS + (k - 1 + Z_SLOTS))
                            nc.vector.tensor_tensor(head[:, k % 2, :], bank[0:HD, :], recip[:, k % 2, :], ALU.mult).then_inc(head_ready, 1)
                            dv.wait_ge(head_ready, j * FINS + (k + 1))
                            dv.sem_inc(bank_free[kind], 1)
                            if c == NC - 1:
                                dv.sem_inc(set_free[kind], 1)


def merge_and_finish(nc, I, S, out):
    TC = 256
    CHUNKS = T // TC
    TILES = D // P
    BLOCKS = TC // P
    MB = 4
    WU = TILES + KT
    NEWTON = 5
    with ExitStack() as ctx:
        b = Memory(nc, ctx, "fin")
        wo_hi = b.sb("wo_hi", [P, TILES, KT, P], F32R)
        wo_lo = b.sb("wo_lo", [P, TILES, KT, P], F32R)
        wt_hi = b.sb("wt_hi", [P, KT, D], F32R)
        wt_lo = b.sb("wt_lo", [P, KT, D], F32R)
        out_t = b.sb("out_t", [P, 2, D])
        a_raw = b.sb("a_raw", [P, KT, TC])
        a_hi = b.sb("a_hi", [P, KT, TC], F32R)
        a_lo = b.sb("a_lo", [P, KT, TC], F32R)
        gates = b.sb("gates", [P, 2, 2, TC])
        m_raw = b.sb("m_raw", [P, 2, TC])
        m_hi = b.sb("m_hi", [P, 2, KT, TC], F32R)
        m_lo = b.sb("m_lo", [P, 2, KT, TC], F32R)
        x_t = b.sb("x_t", [P, D])
        g_row = b.sb("g_row", [P, D])
        ss = b.sb("ss", [P, 2])
        var = b.sb("var", [P, 2])
        inv = b.sb("inv", [P, 2])
        root = b.sb("root", [P, 2])
        fix = b.sb("fix", [P, 1])
        rstd = b.sb("rstd", [P, 1])
        merge_ps = b.ps("merge_ps", [P, MB, 2, TC])
        out_ps = b.ps("out_ps", [P, BLOCKS, D])

        rows_loaded = b.sem("rows_loaded")
        w_loaded = [b.sem(f"w_loaded{i}") for i in range(2)]
        w_hi_ready = b.sem("w_hi_ready")
        wo_ready = b.sem("wo_ready")
        wt_ready = b.sem("wt_ready")
        a_loaded = b.sem("a_loaded")
        a_hi_ready = b.sem("a_hi_ready")
        a_ready = b.sem("a_ready")
        g_loaded = [b.sem(f"g_loaded{i}") for i in range(2)]
        x_loaded = b.sem("x_loaded")
        w_gated = b.sem("w_gated")
        merge_done = b.sem("merge_products_done")
        gated = b.sem("gated")
        merged = b.sem("merged")
        m_hi_ready = b.sem("m_hi_ready")
        m_ready = b.sem("m_ready")
        out_done = b.sem("out_products_done")
        res_ready = b.sem("res_ready")
        summed = b.sem("summed")
        inverted = b.sem("inverted")
        rooted = b.sem("rooted")
        steps = b.sem("newton_steps")
        out_ready = b.sem("out_ready")
        stored = [b.sem(f"stored{i}") for i in range(BLOCKS)]
        def each_section(eng, section):
            section(0, 0, True)
            with eng.Fori(0, (CHUNKS - 4) // 2) as i:
                section(2 * i + 1, 1, True)
                section(2 * i + 2, 0, True)
            section(CHUNKS - 3, 1, True)
            section(CHUNKS - 2, 0, False)
            section(CHUNKS - 1, 1, False)

        def last(c):
            return isinstance(c, int) and c == CHUNKS - 1

        def first(c):
            return isinstance(c, int) and c == 0

        def loads_of(u):
            return sum(2 if v < TILES else 1 for v in range(u % 2, u + 1, 2))

        with nc.Block() as block:
            @block.sync
            def _(sp):
                def load_a(c):
                    if not first(c):
                        sp.wait_ge(a_ready, c)
                    sp.dma_start(a_raw[:], S["za"][:, bass.ds(c * TC, TC)].rearrange("(k p) t -> p k t", p=P)).then_inc(a_loaded, 16)

                def load_gates(c, t):
                    if not first(c) or t >= 2:
                        sp.wait_ge(merged, c * TILES + (t - 1))
                    for half in range(2):
                        sp.dma_start(gates[:, t % 2, half, :],
                                     S["g"][half * D + t * P:half * D + (t + 1) * P, bass.ds(c * TC, TC)]).then_inc(g_loaded[t % 2], 16)

                def load_x(c, k):
                    if first(c) and k == 0:
                        sp.wait_ge(w_gated, KT)
                    else:
                        sp.wait_ge(out_ready, c * BLOCKS + k)
                    sp.dma_start(x_t[:], I["x"][0, bass.ds(c * TC + k * P, P), :]).then_inc(x_loaded, 16)

                load_a(0)
                sp.dma_start(x_t[:], S["gate"].to_broadcast([P, D])).then_inc(rows_loaded, 16)
                for t in range(TILES):
                    load_gates(0, t)
                    if t == 2:
                        load_a(1)
                sp.dma_start(g_row[:], I["g_final"].rearrange("(a n) -> a n", a=1).to_broadcast([P, D])).then_inc(rows_loaded, 16)

                def section(c, par, more):
                    for t in range(TILES):
                        if not last(c):
                            load_gates(c + 1, t)
                        if t == 1 and more:
                            load_a(c + 2)
                        if t == 3 and not first(c):
                            load_x(c, 0)
                    if first(c):
                        load_x(c, 0)
                    load_x(c, 1)
                each_section(sp, section)

            @block.tensor
            def _(pe):
                def merge(c):
                    pe.wait_ge(a_ready, c + 1)
                    for t in range(TILES):
                        if first(c):
                            pe.wait_ge(wo_ready, t + 1)
                        if not first(c) or t >= MB:
                            pe.wait_ge(merged, c * TILES + (t + 1 - MB))
                        for k in range(KT):
                            o = merge_ps[:, t % MB, k // 4, :]
                            nc.tensor.matmul(o, wo_hi[:, t, k, :], a_hi[:, k, :], start=(k % 4 == 0), stop=False)
                            nc.tensor.matmul(o, wo_hi[:, t, k, :], a_lo[:, k, :], start=False, stop=False)
                            end = nc.tensor.matmul(o, wo_lo[:, t, k, :], a_hi[:, k, :], start=False, stop=(k % 4 == 3))
                        end.then_inc(merge_done, 1)

                def finish(c, par):
                    pe.wait_ge(m_ready, (c + 1) * TILES)
                    for block_no in range(BLOCKS):
                        if not first(c):
                            pe.wait_ge(res_ready, c * BLOCKS + (block_no - 1))
                        tok = slice(block_no * P, (block_no + 1) * P)
                        for half in range(2):
                            cols = slice(half * CH, (half + 1) * CH)
                            o = out_ps[:, block_no, cols]
                            for k in range(KT):
                                if first(c):
                                    pe.wait_ge(wt_ready, k + 1)
                                nc.tensor.matmul(o, m_hi[:, par, k, tok], wt_hi[:, k, cols], start=(k == 0), stop=False)
                                nc.tensor.matmul(o, m_hi[:, par, k, tok], wt_lo[:, k, cols], start=False, stop=False)
                                end = nc.tensor.matmul(o, m_lo[:, par, k, tok], wt_hi[:, k, cols], start=False, stop=(k == KT - 1))
                        end.then_inc(out_done, 1)

                def section(c, par, more):
                    if not last(c):
                        merge(c + 1)
                    finish(c, par)
                merge(0)
                each_section(pe, section)

            @block.gpsimd
            def _(gp):
                def split_merged(c, par, t):
                    gp.wait_ge(m_hi_ready, c * TILES + (t + 1))
                    gp.tensor_tensor(m_lo[:, par, t, :], m_raw[:, t % 2, :], f32(m_hi[:, par, t, :]), ALU.subtract).then_inc(m_ready, 1)

                for t in range(TILES):
                    split_merged(0, 0, t)

                def section(c, par, more):
                    for t in range(TILES):
                        if first(c):
                            u = TILES + t
                            gp.wait_ge(w_hi_ready, u + 1)
                            gp.tensor_tensor(wt_lo[:, t, :], out_t[:, u % 2, :], f32(wt_hi[:, t, :]), ALU.subtract).then_inc(wt_ready, 1)
                        if not last(c):
                            split_merged(c + 1, 1 - par, t)
                each_section(gp, section)

            @block.scalar
            def _(act):
                def load_w(u):
                    if u < TILES:
                        raw = out_t[:, u % 2, :].rearrange("p (k c) -> p k c", k=KT)
                        for half, w in enumerate(("w_o_swa", "w_o_fox")):
                            act.dma_start(raw[:, 4 * half:4 * half + 4, :],
                                          I[w][0, :, u * P:(u + 1) * P].rearrange("(k p) c -> p k c", p=P)).then_inc(w_loaded[u % 2], 16)
                    else:
                        k = u - TILES
                        act.dma_start(out_t[:, u % 2, :], I["w_out"][0, k * P:(k + 1) * P, :]).then_inc(w_loaded[u % 2], 16)

                def split_w(u):
                    if u < TILES:
                        act.wait_ge(w_loaded[u % 2], 16 * loads_of(u))
                    else:
                        act.wait_ge(w_gated, u - TILES + 1)
                    raw = out_t[:, u % 2, :]
                    if u < TILES:
                        dst, src = wo_hi[:, u], raw.rearrange("p (k c) -> p k c", k=KT)
                    else:
                        dst, src = wt_hi[:, u - TILES, :], raw
                    nc.scalar.activation(dst, src, ACT.Copy).then_inc(w_hi_ready, 1)

                def reload_w(u):
                    if u + 2 < WU:
                        if u < TILES:
                            act.wait_ge(wo_ready, u + 1)
                        else:
                            act.wait_ge(wt_ready, u - TILES + 1)
                        load_w(u + 2)

                def split_a(c):
                    act.wait_ge(a_loaded, 16 * (c + 1))
                    if not first(c):
                        act.wait_ge(merge_done, c * TILES)
                    nc.scalar.activation(a_hi[:], a_raw[:], ACT.Copy).then_inc(a_hi_ready, 1)

                def split_merged(c, par, t):
                    act.wait_ge(merged, c * TILES + (t + 1))
                    nc.scalar.activation(m_hi[:, par, t, :], m_raw[:, t % 2, :], ACT.Copy).then_inc(m_hi_ready, 1)

                def norm(c, k):
                    n = c * BLOCKS + k
                    act.wait_ge(res_ready, n + 1)
                    if not first(c):
                        act.wait_ge(stored[k], c * 16)
                    nc.scalar.activation(out_t[:, k, :], x_t[:], ACT.Square, accum_out=ss[:, k:k + 1]).then_inc(summed, 1)
                    act.wait_ge(inverted, n + 1)
                    nc.scalar.activation(root[:, k:k + 1], inv[:, k:k + 1], ACT.Sqrt).then_inc(rooted, 1)
                    act.wait_ge(out_ready, n + 1)
                    act.dma_start(out[0, bass.ds(c * TC + k * P, P), :], out_t[:, k, :]).then_inc(stored[k], 16)

                def section(c, par, more):
                    for t in range(TILES):
                        if first(c):
                            split_w(TILES + t)
                        if not last(c):
                            split_merged(c + 1, 1 - par, t)
                        if first(c):
                            reload_w(TILES + t)
                    if more:
                        split_a(c + 2)
                    for k in range(BLOCKS):
                        norm(c, k)

                load_w(0)
                load_w(1)
                split_a(0)
                for u in range(TILES):
                    split_w(u)
                    if u >= 2:
                        split_merged(0, 0, u - 2)
                    reload_w(u)
                split_merged(0, 0, TILES - 2)
                split_merged(0, 0, TILES - 1)
                split_a(1)
                each_section(act, section)
                for k in range(BLOCKS):
                    act.wait_ge(stored[k], CHUNKS * 16)

            @block.vector
            def _(dv):
                def split_w(u):
                    dv.wait_ge(w_hi_ready, u + 1)
                    nc.vector.tensor_tensor(wo_lo[:, u], out_t[:, u % 2, :].rearrange("p (k c) -> p k c", k=KT), f32(wo_hi[:, u]),
                                            ALU.subtract).then_inc(wo_ready, 1)

                def split_a(c):
                    dv.wait_ge(a_hi_ready, c + 1)
                    nc.vector.tensor_tensor(a_lo[:], a_raw[:], f32(a_hi[:]), ALU.subtract).then_inc(a_ready, 1)

                def merge(c, t):
                    n = c * TILES
                    dv.wait_ge(g_loaded[t % 2], (c * (TILES // 2) + (t // 2 + 1)) * 32)
                    dv.wait_ge(merge_done, n + (t + 1))
                    for half in range(2):
                        end = nc.vector.tensor_tensor(gates[:, t % 2, half, :], merge_ps[:, t % MB, half, :], gates[:, t % 2, half, :], ALU.mult)
                    end.then_inc(gated, 1)
                    dv.wait_ge(gated, n + (t + 1))
                    if not first(c) or t >= 2:
                        dv.wait_ge(m_ready, n + (t - 1))
                    nc.vector.tensor_tensor(m_raw[:, t % 2, :], gates[:, t % 2, 0, :], gates[:, t % 2, 1, :], ALU.add).then_inc(merged, 1)

                def norm(c, k):
                    n = c * BLOCKS + k
                    dv.wait_ge(out_done, n + 1)
                    dv.wait_ge(x_loaded, n * 16 + 16)
                    nc.vector.tensor_tensor(x_t[:], x_t[:], out_ps[:, k, :], ALU.add).then_inc(res_ready, 1)
                    dv.wait_ge(summed, n + 1)
                    v, y = var[:, k:k + 1], root[:, k:k + 1]
                    nc.vector.tensor_scalar(v, ss[:, k:k + 1], 1.0 / D, EPS, ALU.mult, ALU.add).then_inc(steps, 1)
                    dv.wait_ge(steps, n * NEWTON + 1)
                    nc.vector.reciprocal(inv[:, k:k + 1], v).then_inc(inverted, 1)
                    dv.wait_ge(rooted, n + 1)
                    nc.vector.tensor_tensor(fix[:], y, y, ALU.mult).then_inc(steps, 1)
                    dv.wait_ge(steps, n * NEWTON + 2)
                    nc.vector.tensor_tensor(fix[:], fix[:], v, ALU.mult).then_inc(steps, 1)
                    dv.wait_ge(steps, n * NEWTON + 3)
                    nc.vector.tensor_scalar(fix[:], fix[:], -0.5, 1.5, ALU.mult, ALU.add).then_inc(steps, 1)
                    dv.wait_ge(steps, n * NEWTON + 4)
                    nc.vector.tensor_tensor(rstd[:], y, fix[:], ALU.mult).then_inc(steps, 1)
                    dv.wait_ge(steps, n * NEWTON + 5)
                    nc.vector.scalar_tensor_tensor(out_t[:, k, :], x_t[:], rstd[:, 0:1], g_row[:], ALU.mult, ALU.mult).then_inc(out_ready, 1)
                    dv.wait_ge(out_ready, n + 1)

                def section(c, par, more):
                    if not last(c):
                        for t in range(TILES):
                            if first(c):
                                u = TILES + t
                                dv.wait_ge(w_loaded[u % 2], 16 * loads_of(u))
                                nc.vector.tensor_tensor(out_t[:, u % 2, :], out_t[:, u % 2, :], x_t[:], ALU.mult).then_inc(w_gated, 1)
                            merge(c + 1, t)
                    if more:
                        split_a(c + 2)
                    for k in range(BLOCKS):
                        norm(c, k)

                split_a(0)
                for u in range(TILES):
                    split_w(u)
                    if u:
                        merge(0, u - 1)
                merge(0, TILES - 1)
                split_a(1)
                dv.wait_ge(rows_loaded, 32)
                each_section(dv, section)


_INS = ["x", "c", "positions", "w_ada", "b_ada", "g_norm", "w_in", "b_f", "sinks", "w_o_swa", "w_o_fox", "w_out", "g_final"]


def build(nc, I, out, upto=4):
    S = {
        "q": nc.dram_tensor("q_parts", (2, 2 * NH, HD, T), F32).ap(),
        "k": nc.dram_tensor("k_parts", (2, KV + NH, HD, T), F32).ap(),
        "v": nc.dram_tensor("v_parts", (2, T, VW), F32).ap(),
        "negc": nc.dram_tensor("negc_parts", (2, 2 * NH, T), F32).ap(),
        "tab": nc.dram_tensor("rotary_tables", (2, HD // 2, T), F32).ap(),
        "gate": nc.dram_tensor("residual_gate", (1, D), F32).ap(),
        "m": nc.dram_tensor("m_parts", (2, 3 * NH, T), F32).ap(),
        "z": nc.dram_tensor("z_silu", (2 * W, T), F32).ap(),
        "g": nc.dram_tensor("sigmoid_gates", (2 * D, T), F32).ap(),
        "za": nc.dram_tensor("gated_heads", (2 * W, T), F32).ap(),
    }
    with ExitStack() as ctx:
        keep = Memory(nc, ctx, "h")
        hT_hi = keep.sb("hT_hi", [P, KT, T], F32R)
        hT_lo = keep.sb("hT_lo", [P, KT, T], F32R)
        prepare_and_values(nc, I, S, hT_hi, hT_lo)
        if upto >= 2:
            project(nc, I, S, hT_hi, hT_lo)
    if upto >= 3:
        attend(nc, I, S)
    if upto >= 4:
        merge_and_finish(nc, I, S, out)


def kernel(**inputs):
    import numpy as _np
    import concourse.bacc as _bacc
    from concourse import mybir as _mybir
    from concourse.bass_utils import run_bass_kernel_spmd as _run

    nc = _bacc.Bacc("TRN2", target_bir_lowering=False, num_devices=1)
    arrays = {name: _np.ascontiguousarray(inputs[name]) for name in _INS}
    freq = _np.float64(10000.0) ** (-_np.arange(0, HD, 2, dtype=_np.float64) / HD)
    arrays["inv_freq"] = _np.tile(freq.astype(_np.float32), 4).reshape(P, 1)
    I = {n: nc.dram_tensor(f"in_{n}", a.shape, _mybir.dt.from_np(a.dtype), kind="ExternalInput").ap() for n, a in arrays.items()}
    out = nc.dram_tensor("out_0", (1, T, D), _mybir.dt.float32, kind="ExternalOutput").ap()
    build(nc, I, out)
    r = _run(nc, [{f"in_{n}": a for n, a in arrays.items()}], core_ids=[0])
    return r.results[0]["out_0"]
```
